# Optimizing a Trainium2 kernel written in Bass

```python
import math
import jax, jax.numpy as jnp
from jax import lax
import numpy as np

D_MODEL = 1024
BATCH = 1
SEQ = 2048
DEPTH = 1

CTX_LEN = 256
GRID_W = 64
EPS = 1e-6
SHORT_CONV = 3

D_HYENA = D_MODEL // 2
HYENA_ORDER = 2
HYENA_BANDS = 8
HYENA_EMB = 1 + 2 * HYENA_BANDS
HYENA_FILTER_HID = 64
HYENA_FAST_DECAY = 0.3
HYENA_SLOW_DECAY = 1.5
HYENA_TARGET = 1e-2

D_SSD = D_MODEL // 2
SSD_HEAD_DIM = 64
SSD_HEADS = D_SSD // SSD_HEAD_DIM
SSD_GROUPS = 2
SSD_HPG = SSD_HEADS // SSD_GROUPS
SSD_STATE = 128
SSD_CHUNK = 128

D_MIX = D_HYENA + D_SSD
D_XBC = D_SSD + 2 * SSD_GROUPS * SSD_STATE
HY_COLS = (HYENA_ORDER + 1) * D_HYENA
D_IN = HY_COLS + D_SSD + D_XBC + 2 * SSD_HEADS

MOE_GROUPS = 8
EXPERTS_PER_GROUP = 8
N_EXPERTS = MOE_GROUPS * EXPERTS_PER_GROUP
TOP_K = 2
D_EXPERT = 512
MOE_BLOCK = 128

kernel_name = 'hymba_hyena_ssd_hmoe_dit_block'

def rmsnorm(x, g):
    xf = x.astype(jnp.float32)
    y = xf * lax.rsqrt(jnp.mean(xf * xf, axis=-1, keepdims=True) + EPS)
    return y.astype(x.dtype) * g

def modulate(h, shift, scale):
    return h * (1 + scale) + shift

def short_conv_rows(u, w, b, n_rows):
    bsz, L, C = u.shape
    row_len = L // n_rows
    pad = SHORT_CONV // 2
    ur = jnp.pad(u.reshape(bsz, n_rows, row_len, C), ((0, 0), (0, 0), (pad, pad), (0, 0)))
    y = b + sum(ur[:, :, k:k + row_len] * w[k] for k in range(SHORT_CONV))
    return y.reshape(bsz, L, C)

def hyena_filters(L, f_w1, f_b1, f_freq, f_w2, f_b2, f_w3):
    f32 = jnp.float32
    pos = jnp.arange(L, dtype=f32)
    t = pos / max(L - 1, 1)
    bands = jnp.linspace(1e-4, HYENA_BANDS - 1, HYENA_BANDS, dtype=f32)
    ang = (2 * math.pi / L) * pos[:, None] * bands[None, :]
    feats = jnp.concatenate([t[:, None], jnp.cos(ang), -jnp.sin(ang)], axis=-1)
    freq = f_freq.astype(f32)
    h = jnp.sin(freq * (feats @ f_w1.astype(f32) + f_b1.astype(f32)))
    h = jnp.sin(freq * (h @ f_w2.astype(f32) + f_b2.astype(f32)))
    k = (h @ f_w3.astype(f32)).reshape(L, HYENA_ORDER, 2, D_HYENA)
    deltas = jnp.abs(jnp.linspace(math.log(HYENA_TARGET) / HYENA_SLOW_DECAY,
                                  math.log(HYENA_TARGET) / HYENA_FAST_DECAY, D_HYENA, dtype=f32))
    window = jnp.exp(-t[:, None] * deltas[None, :])
    return k * window[:, None, None, :]

def long_conv_bidir(z, k_f, k_b, bias):
    L = z.shape[1]
    k_full = jnp.concatenate([k_f, jnp.zeros_like(k_f[:1]), jnp.flip(k_b[1:], axis=0)], axis=0)
    zf = jnp.fft.rfft(z, n=2 * L, axis=1)
    kf = jnp.fft.rfft(k_full, axis=0)
    y = jnp.fft.irfft(zf * kf[None], n=2 * L, axis=1)[:, :L]
    return y + z * bias

def hyena_branch(p, conv_w, conv_b, f_w1, f_b1, f_freq, f_w2, f_b2, f_w3, h_bias, n_rows):
    L = p.shape[1]
    u = short_conv_rows(p, conv_w, conv_b, n_rows).astype(jnp.float32)
    parts = jnp.split(u, HYENA_ORDER + 1, axis=-1)
    k = hyena_filters(L, f_w1, f_b1, f_freq, f_w2, f_b2, f_w3)
    hb = h_bias.astype(jnp.float32)
    z = parts[0]
    for o in range(HYENA_ORDER):
        z = parts[o + 1] * long_conv_bidir(z, k[:, o, 0], k[:, o, 1], hb[o])
    return z.astype(p.dtype)

def ssd_prep(p, conv_w, conv_b, a_log, dt_bias, n_rows):
    bsz, L, _ = p.shape
    G, R, P, N = SSD_GROUPS, SSD_HPG, SSD_HEAD_DIM, SSD_STATE
    z = p[..., :D_SSD]
    xbc = jax.nn.silu(short_conv_rows(p[..., D_SSD:D_SSD + D_XBC], conv_w, conv_b, n_rows))
    xs = xbc[..., :D_SSD].reshape(bsz, L, G, R, P)
    bm = xbc[..., D_SSD:D_SSD + G * N].reshape(bsz, L, G, N)
    cm = xbc[..., D_SSD + G * N:].reshape(bsz, L, G, N)
    dt_raw = p[..., D_SSD + D_XBC:].astype(jnp.float32).reshape(bsz, L, 2, G, R)
    dt = jax.nn.softplus(dt_raw + dt_bias.astype(jnp.float32).reshape(2, G, R))
    a = -jnp.exp(a_log.astype(jnp.float32)).reshape(2, G, R) * dt
    return z, xs, bm, cm, dt, a

def ssd_scan(xs, a, bm, cm, h0):
    bsz, L, G, R, P = xs.shape
    N = bm.shape[-1]
    nc = L // SSD_CHUNK
    xs = xs.reshape(bsz, nc, SSD_CHUNK, G, R, P)
    a = a.reshape(bsz, nc, SSD_CHUNK, G, R)
    bm = bm.reshape(bsz, nc, SSD_CHUNK, G, N)
    cm = cm.reshape(bsz, nc, SSD_CHUNK, G, N)
    a_cum = jnp.cumsum(a, axis=2)
    lower = jnp.tril(jnp.ones((SSD_CHUNK, SSD_CHUNK), bool))[:, :, None, None]
    seg = a_cum[:, :, :, None] - a_cum[:, :, None, :]
    decay = jnp.exp(jnp.where(lower, seg, -jnp.inf))
    cb = jnp.einsum('bclgn,bcsgn->bclsg', cm, bm)
    y_diag = jnp.einsum('bclsg,bclsgr,bcsgrp->bclgrp', cb, decay, xs)
    to_end = jnp.exp(a_cum[:, :, -1:] - a_cum)
    chunk_states = jnp.einsum('bclgn,bclgr,bclgrp->bcgrpn', bm, to_end, xs)
    chunk_decay = jnp.exp(a_cum[:, :, -1])

    def step(h, inp):
        s_c, d_c = inp
        return h * d_c[..., None, None] + s_c, h

    h_final, h_in = lax.scan(step, h0, (jnp.moveaxis(chunk_states, 1, 0), jnp.moveaxis(chunk_decay, 1, 0)))
    h_in = jnp.moveaxis(h_in, 0, 1)
    y_off = jnp.einsum('bclgn,bcgrpn,bclgr->bclgrp', cm, h_in, jnp.exp(a_cum))
    return (y_diag + y_off).reshape(bsz, L, G, R, P), h_final

def ssd_final_state(xs, a, bm):
    a_cum = jnp.cumsum(a, axis=1)
    w = jnp.exp(a_cum[:, -1:] - a_cum)
    return jnp.einsum('blgn,blgr,blgrp->bgrpn', bm, w, xs)

def _rev(t):
    return jnp.flip(t, axis=1)

def ssd_context_states(prep):
    _, xs, bm, _, dt, a = prep
    xf = xs.astype(jnp.float32)
    bf = bm.astype(jnp.float32)
    h_f = ssd_final_state(xf * dt[:, :, 0, :, :, None], a[:, :, 0], bf)
    h_b = ssd_final_state(_rev(xf * dt[:, :, 1, :, :, None]), _rev(a[:, :, 1]), _rev(bf))
    return h_f, h_b

def ssd_branch(prep, d_skip, norm_g, h0_f, h0_b):
    z, xs, bm, cm, dt, a = prep
    bsz, L = z.shape[:2]
    xf = xs.astype(jnp.float32)
    bf = bm.astype(jnp.float32)
    cf = cm.astype(jnp.float32)
    y_f, h_f = ssd_scan(xf * dt[:, :, 0, :, :, None], a[:, :, 0], bf, cf, h0_f)
    y_b, h_b = ssd_scan(_rev(xf * dt[:, :, 1, :, :, None]), _rev(a[:, :, 1]), _rev(bf), _rev(cf), h0_b)
    y = y_f + _rev(y_b) + d_skip.astype(jnp.float32).reshape(SSD_GROUPS, SSD_HPG)[..., None] * xf
    y = y.reshape(bsz, L, D_SSD) * jax.nn.silu(z.astype(jnp.float32))
    y = y.reshape(bsz, L, SSD_GROUPS, D_SSD // SSD_GROUPS)
    y = y * lax.rsqrt(jnp.mean(y * y, axis=-1, keepdims=True) + EPS)
    y = y.reshape(bsz, L, D_SSD) * norm_g
    return y.astype(z.dtype), h_f, h_b

def moe_ffn(h, w_group, b_group, w_expert, b_expert, w1, w3, w2):
    T, D = h.shape
    group_prob = jax.nn.softmax((h @ w_group + b_group).astype(jnp.float32), axis=-1)
    p_group, g_sel = lax.top_k(group_prob, 1)
    exp_logits = (h @ w_expert + b_expert).astype(jnp.float32).reshape(T, MOE_GROUPS, EXPERTS_PER_GROUP)
    in_group = exp_logits[jnp.arange(T), g_sel[:, 0]]
    top_logit, top_idx = lax.top_k(in_group, TOP_K)
    gate = jax.nn.softmax(top_logit, axis=-1) * p_group
    expert_id = g_sel * EXPERTS_PER_GROUP + top_idx
    M = T * TOP_K
    eid = expert_id.reshape(M)
    tok = jnp.repeat(jnp.arange(T), TOP_K)
    order = jnp.argsort(eid)
    eid_s, tok_s, gate_s = eid[order], tok[order], gate.reshape(M)[order]
    counts = jnp.bincount(eid, length=N_EXPERTS)
    padded = (counts + MOE_BLOCK - 1) // MOE_BLOCK * MOE_BLOCK
    ends = jnp.cumsum(padded)
    dest = (ends - padded)[eid_s] + jnp.arange(M) - (jnp.cumsum(counts) - counts)[eid_s]
    n_blocks = -(-M // MOE_BLOCK) + N_EXPERTS
    buf = jnp.zeros((n_blocks * MOE_BLOCK, D), h.dtype).at[dest].set(h[tok_s])
    block_eid = jnp.minimum(jnp.searchsorted(ends, jnp.arange(n_blocks) * MOE_BLOCK, side='right'), N_EXPERTS - 1)

    def expert_block(args):
        xb, e = args
        return (jax.nn.silu(xb @ w1[e]) * (xb @ w3[e])) @ w2[e]

    yb = lax.map(expert_block, (buf.reshape(n_blocks, MOE_BLOCK, D), block_eid))
    contrib = yb.reshape(-1, D)[dest] * gate_s[:, None].astype(h.dtype)
    return jnp.zeros_like(h).at[tok_s].add(contrib)

def setup_inputs(seed: int = 0) -> dict:
    key = jax.random.key(seed)
    ks = jax.random.split(key, 40)

    def nrm(i, shape, s):
        return jax.random.normal(ks[i], shape, jnp.float32) * s

    NL = DEPTH
    FH = HYENA_FILTER_HID
    dt0 = jnp.exp(jax.random.uniform(ks[30], (NL, 2, SSD_HEADS)) * (math.log(0.1) - math.log(1e-3)) + math.log(1e-3))
    return {
        'x': nrm(0, (BATCH, SEQ, D_MODEL), 1.0),
        'c': nrm(1, (BATCH, D_MODEL), 1.0),
        'ctx': nrm(2, (BATCH, CTX_LEN, D_MODEL), 1.0),
        'c_ctx': nrm(3, (D_MODEL,), 1.0),
        'w_ada': nrm(4, (NL, D_MODEL, 6 * D_MODEL), D_MODEL ** -0.5),
        'b_ada': nrm(5, (NL, 6 * D_MODEL), 0.02),
        'g_norm1': 1.0 + nrm(6, (NL, D_MODEL), 0.05),
        'g_norm2': 1.0 + nrm(7, (NL, D_MODEL), 0.05),
        'w_in': nrm(8, (NL, D_MODEL, D_IN), D_MODEL ** -0.5),
        'hy_conv_w': nrm(9, (NL, SHORT_CONV, HY_COLS), SHORT_CONV ** -0.5),
        'hy_conv_b': nrm(10, (NL, HY_COLS), 0.02),
        'hy_f_w1': nrm(11, (NL, HYENA_EMB, FH), HYENA_EMB ** -0.5),
        'hy_f_b1': nrm(12, (NL, FH), 0.02),
        'hy_f_freq': 1.0 + nrm(13, (NL, FH), 0.05),
        'hy_f_w2': nrm(14, (NL, FH, FH), FH ** -0.5),
        'hy_f_b2': nrm(15, (NL, FH), 0.02),
        'hy_f_w3': nrm(16, (NL, FH, HYENA_ORDER * 2 * D_HYENA), 0.05 * FH ** -0.5),
        'hy_bias': nrm(17, (NL, HYENA_ORDER, D_HYENA), 0.5),
        'ssd_conv_w': nrm(18, (NL, SHORT_CONV, D_XBC), SHORT_CONV ** -0.5),
        'ssd_conv_b': nrm(19, (NL, D_XBC), 0.02),
        'ssd_a_log': jnp.log(jax.random.uniform(ks[31], (NL, 2, SSD_HEADS), minval=1.0, maxval=16.0)),
        'ssd_dt_bias': dt0 + jnp.log(-jnp.expm1(-dt0)),
        'ssd_d': 1.0 + nrm(20, (NL, SSD_HEADS), 0.1),
        'ssd_norm_g': 1.0 + nrm(21, (NL, D_SSD), 0.05),
        'w_out': nrm(22, (NL, D_MIX, D_MODEL), D_MIX ** -0.5),
        'w_group': nrm(23, (NL, D_MODEL, MOE_GROUPS), D_MODEL ** -0.5),
        'b_group': nrm(24, (NL, MOE_GROUPS), 0.01),
        'w_expert': nrm(25, (NL, D_MODEL, N_EXPERTS), D_MODEL ** -0.5),
        'b_expert': nrm(26, (NL, N_EXPERTS), 0.01),
        'w1': nrm(27, (NL, N_EXPERTS, D_MODEL, D_EXPERT), D_MODEL ** -0.5),
        'w3': nrm(28, (NL, N_EXPERTS, D_MODEL, D_EXPERT), D_MODEL ** -0.5),
        'w2': nrm(29, (NL, N_EXPERTS, D_EXPERT, D_MODEL), D_EXPERT ** -0.5),
        'g_final': 1.0 + nrm(32, (D_MODEL,), 0.05),
    }

def reference(x, c, ctx, c_ctx, w_ada, b_ada, g_norm1, g_norm2, w_in, hy_conv_w, hy_conv_b,
              hy_f_w1, hy_f_b1, hy_f_freq, hy_f_w2, hy_f_b2, hy_f_w3, hy_bias,
              ssd_conv_w, ssd_conv_b, ssd_a_log, ssd_dt_bias, ssd_d, ssd_norm_g, w_out,
              w_group, b_group, w_expert, b_expert, w1, w3, w2, g_final):
    bsz, seq_len, _ = x.shape
    rows = seq_len // GRID_W
    for l in range(DEPTH):
        last = l == DEPTH - 1
        hy_p = (hy_conv_w[l], hy_conv_b[l], hy_f_w1[l], hy_f_b1[l], hy_f_freq[l],
                hy_f_w2[l], hy_f_b2[l], hy_f_w3[l], hy_bias[l])
        ssd_p = (ssd_conv_w[l], ssd_conv_b[l], ssd_a_log[l], ssd_dt_bias[l])
        moe_p = (w_group[l], b_group[l], w_expert[l], b_expert[l], w1[l], w3[l], w2[l])
        sh1, sc1, ga1, sh2, sc2, ga2 = jnp.split((jax.nn.silu(c) @ w_ada[l] + b_ada[l])[:, None, :], 6, axis=-1)
        csh1, csc1, cga1, csh2, csc2, cga2 = jnp.split(jax.nn.silu(c_ctx) @ w_ada[l] + b_ada[l], 6, axis=-1)

        pc = modulate(rmsnorm(ctx, g_norm1[l]), csh1, csc1) @ w_in[l]
        prep_c = ssd_prep(pc[..., HY_COLS:], *ssd_p, 1)
        if last:
            h_f, h_b = ssd_context_states(prep_c)
        else:
            h_zero = jnp.zeros((bsz, SSD_GROUPS, SSD_HPG, SSD_HEAD_DIM, SSD_STATE), jnp.float32)
            yc_ssd, h_f, h_b = ssd_branch(prep_c, ssd_d[l], ssd_norm_g[l], h_zero, h_zero)
            yc_hy = hyena_branch(pc[..., :HY_COLS], *hy_p, 1)
            ctx = ctx + cga1 * (jnp.concatenate([yc_hy, yc_ssd], axis=-1) @ w_out[l])
            hcn = modulate(rmsnorm(ctx, g_norm2[l]), csh2, csc2)
            ctx = ctx + cga2 * moe_ffn(hcn.reshape(-1, D_MODEL), *moe_p).reshape(ctx.shape)

        px = modulate(rmsnorm(x, g_norm1[l]), sh1, sc1) @ w_in[l]
        y_hy = hyena_branch(px[..., :HY_COLS], *hy_p, rows)
        prep_x = ssd_prep(px[..., HY_COLS:], *ssd_p, rows)
        y_ssd, _, _ = ssd_branch(prep_x, ssd_d[l], ssd_norm_g[l], h_f, h_b)
        x = x + ga1 * (jnp.concatenate([y_hy, y_ssd], axis=-1) @ w_out[l])

        hxn = modulate(rmsnorm(x, g_norm2[l]), sh2, sc2)
        x = x + ga2 * moe_ffn(hxn.reshape(-1, D_MODEL), *moe_p).reshape(x.shape)
    return rmsnorm(x, g_final)


_drawn_inputs = setup_inputs


def setup_inputs(seed=0):
    import zlib

    import numpy as np

    out = dict(_drawn_inputs(seed))
    spreads = {}
    factors = {'ctx': 8.0,
     'c_ctx': 5.991,
     'g_norm2': 3.703,
     'ssd_conv_b': 8.0,
     'ssd_d': 8.0,
     'ssd_norm_g': 6.519,
     'b_group': 8.0,
     'b_expert': 8.0}
    for name, (base, spread) in spreads.items():
        noise = np.random.default_rng([zlib.crc32(name.encode()), seed]).standard_normal(out[name].shape)
        drawn = base * np.exp(spread * noise) if base else spread * noise
        out[name] = __import__('jax').numpy.asarray(drawn.astype(out[name].dtype))
    for name, factor in factors.items():
        out[name] = (out[name] * factor).astype(out[name].dtype)
    return out
```

```python
import math
from collections import namedtuple
from contextlib import ExitStack

import numpy as np

import concourse.bass as bass
from concourse import mybir

F32 = mybir.dt.float32
I32 = mybir.dt.int32
ALU = mybir.AluOpType
ACT = mybir.ActivationFunctionType
AX = mybir.AxisListType

P = 128
D = 1024
DT = D // P
L = 2048
LC = 256
TOK = LC + L
NTX = L // P
NTC = LC // P
NT = NTX + NTC
GRID = 64
EPS = 1e-6
BANK = 512
DH = 512
CT = DH // P
HYT = 12
ZT = 4
XBCT = 8
COLT = HYT + ZT + XBCT
HEADS = 8
MG, EPG = 8, 8
NE = MG * EPG
DE = 512
NOV = 2 * L // P
NBLK = NE + NOV
MAXB = L // P - 1
HD = 64
HPG = HEADS // 2
D_SSD = HEADS * HD
SSD_DT = HEADS
ORDER = 2
BANDS = 8
EMB = 1 + 2 * BANDS
HID = 64
FAST, SLOW, TARGET = 0.3, 1.5, 1e-2
N2 = 2 * L // P
NB1 = L // N2


def pools(nc, ctx):
    def sb(name, shape, dt=F32):
        return ctx.enter_context(nc.sbuf_tensor(name, shape, dt))

    def ps(name, shape, dt=F32):
        return ctx.enter_context(nc.psum_tensor(name, shape, dt))

    held = []

    def sem(name):
        held.append(nc.alloc_semaphore(name))
        return held[-1]

    def release():
        if held:
            nc.clear_and_free_semaphores(held)
            nc.all_engine_barrier()

    ctx.callback(release)
    return sb, ps, sem


class Steps:

    def __init__(self, eng, sem):
        self.eng, self.sem, self.n = eng, sem, 0

    def done(self, ins):
        ins.then_inc(self.sem, 1)
        self.n += 1
        return ins

    def join(self, base=0):
        self.eng.wait_ge(self.sem, base + self.n)

    def link(self, ins, base=0):
        self.done(ins)
        self.join(base)


def adaln(nc, d):
    NCH = 6 * D // BANK
    with ExitStack() as ctx:
        sb, ps, sem = pools(nc, ctx)
        cond = sb("cond", [P, 2, DT])
        act = sb("cond_silu", [P, DT, 2])
        w = sb("w_ada_sb", [P, 2, DT, BANK])
        bias = sb("b_ada_sb", [2, 6 * D])
        mod = sb("mod_sb", [2, 6 * D])
        acc = ps("mod_ps", [P, 2, BANK])
        cond_in, bias_in, silu_done, out_done = sem("cond_in"), sem("bias_in"), sem("silu_done"), sem("mod_out")
        w_in = [sem("w_ada_in0"), sem("w_ada_in1")]
        w_used, mm_done, mod_done = sem("w_ada_used"), sem("mod_mm"), sem("mod_done")
        wv = d.w_ada.rearrange("(p j) n -> p j n", p=P)
        block = ctx.enter_context(nc.Block())

        @block.sync
        def _(sp):
            sp.dma_start(cond[:, 0, :], d.c.rearrange("(p j) -> p j", p=P)).then_inc(cond_in, 16)
            sp.dma_start(cond[:, 1, :], d.c_ctx.rearrange("(p j) -> p j", p=P)).then_inc(cond_in, 16)
            for v in range(2):
                sp.dma_start(bias[v:v + 1, :], d.b_ada.rearrange("(a n) -> a n", a=1)).then_inc(bias_in, 16)
            for n in range(2):
                sp.dma_start(w[:, n], wv[:, :, n * BANK:(n + 1) * BANK]).then_inc(w_in[n], 16)
            with sp.Fori(1, NCH // 2) as i:
                for n in range(2):
                    sp.wait_ge(mm_done, i * 2 + (n - 1))
                    sp.dma_start(w[:, n], wv[:, :, bass.ds((i * 2 + n) * BANK, BANK)]).then_inc(w_in[n], 16)
            sp.wait_ge(mod_done, NCH)
            sp.dma_start(d.mod, mod[:, :]).then_inc(out_done, 16)
            sp.wait_ge(out_done, 16)

        @block.scalar
        def _(s):
            s.wait_ge(cond_in, 32)
            s.activation(act[:].rearrange("p j v -> p v j"), cond[:], ACT.Silu).then_inc(silu_done, 1)

        @block.tensor
        def _(pe):
            pe.wait_ge(silu_done, 1)
            for n in range(2):
                pe.wait_ge(w_in[n], 16)
                for j in range(DT):
                    last = pe.matmul(acc[0:2, n, :], act[:, j, :], w[:, n, j, :], start=(j == 0), stop=(j == DT - 1))
                last.then_inc(mm_done, 1)
            with pe.Fori(1, NCH // 2) as i:
                for n in range(2):
                    pe.wait_ge(w_in[n], i * 16 + 16)
                    pe.wait_ge(mod_done, i * 2 + (n - 1))
                    for j in range(DT):
                        last = pe.matmul(acc[0:2, n, :], act[:, j, :], w[:, n, j, :],
                                         start=(j == 0), stop=(j == DT - 1))
                    last.then_inc(mm_done, 1)

        @block.vector
        def _(v):
            v.wait_ge(bias_in, 32)
            with v.Fori(0, NCH // 2) as i:
                for n in range(2):
                    v.wait_ge(mm_done, i * 2 + (n + 1))
                    at = bass.ds((i * 2 + n) * BANK, BANK)
                    v.tensor_tensor(mod[:, at], acc[0:2, n, :], bias[:, at], ALU.add).then_inc(mod_done, 1)


def norm_in(nc, d, hT):
    with ExitStack() as ctx:
        sb, ps, sem = pools(nc, ctx)
        x = sb("x_tok", [P, NT, D])
        sq = sb("x_sq", [P, D])
        ms = sb("x_ms", [P, NT])
        rms = sb("x_rms", [P, NT])
        rstd = sb("x_rstd", [P, NT])
        xn = sb("x_n", [P, 2, D])
        ident = sb("ident", [P, P])
        m = sb("mod_cols", [P, 2, 2, DT])
        g = sb("g1_cols", [P, DT])
        gs = sb("g1_scale", [P, 2, DT])
        tp = ps("x_tp", [P, 2, 2, 4, P])
        x_in, small_in = sem("x_in"), sem("nin_small")
        ss_done, rs, scale_ready = sem("nin_ss"), sem("nin_rs"), sem("nin_scale")
        xn_done, tp_done, evac = sem("nin_xn"), sem("nin_tp"), sem("nin_evac")
        block = ctx.enter_context(nc.Block())

        @block.sync
        def _(sp):
            sp.dma_start(x[:, 0:NTC, :], d.ctx.rearrange("(t p) n -> p t n", p=P)).then_inc(x_in, 16)
            for q in range(4):
                a = q * 4
                sp.dma_start(x[:, NTC + a:NTC + a + 4, :], d.x.rearrange("(t p) n -> p t n", p=P)[:, a:a + 4, :])\
                    .then_inc(x_in, 16)

        @block.gpsimd
        def _(g_):
            g_.dma_start(ident[:], d.ident).then_inc(small_in, 16)
            with nc.allow_non_contiguous_dma(reason="modulation vectors as columns"):
                g_.dma_start(g[:], d.g_norm1.rearrange("(j p) -> p j", p=P)).then_inc(small_in, 16)
                for v in range(2):
                    for s in range(2):
                        g_.dma_start(m[:, v, s, :], d.mod[v, s * D:(s + 1) * D].rearrange("(j p) -> p j", p=P))\
                            .then_inc(small_in, 16)

        @block.scalar
        def _(s):
            s.wait_ge(x_in, 80)
            with s.Fori(0, NT) as t:
                s.activation(sq[:], x[:, bass.ds(t, 1), :], ACT.Square, accum_out=ms[:, bass.ds(t, 1)])\
                    .then_inc(ss_done, 1)
                s.wait_ge(ss_done, t + 1)
            s.wait_ge(rs, 1)
            s.activation(rms[:], ms[:], ACT.Sqrt).then_inc(rs, 1)
            s.wait_ge(scale_ready, 2)
            for v, t0, t1 in ((1, 0, NTC // 2), (0, NTC // 2, NT // 2)):
                with s.Fori(t0, t1) as i:
                    for n in range(2):
                        s.wait_ge(tp_done, (i * 2 + n) + 1)
                        s.wait_ge(scale_ready, 2)
                        for j in range(DT):
                            last = s.activation(hT[:, j, bass.ds((i * 2 + n) * P, P)], tp[:, n, j // 4, j % 4, :],
                                                ACT.Identity, bias=m[:, v, 0, j:j + 1], scale=gs[:, v, j:j + 1])
                        last.then_inc(evac, 1)

        @block.vector
        def _(v):
            st = Steps(v, scale_ready)
            v.wait_ge(small_in, 96)
            for k in range(2):
                v.scalar_tensor_tensor(out=gs[:, k, :], in0=m[:, k, 1, :], scalar=1.0, in1=g[:], op0=ALU.add,
                                       op1=ALU.mult).then_inc(scale_ready, 1)
            v.wait_ge(ss_done, NT)
            v.tensor_scalar(ms[:], ms[:], 1.0 / D, EPS, ALU.mult, ALU.add).then_inc(rs, 1)
            v.wait_ge(rs, 2)
            v.reciprocal(rstd[:], rms[:]).then_inc(rs, 1)
            v.wait_ge(rs, 3)
            for n in range(2):
                v.tensor_scalar(xn[:, n, :], x[:, n, :], rstd[:, n:n + 1], None, ALU.mult).then_inc(xn_done, 1)
            with v.Fori(1, NT // 2) as i:
                for n in range(2):
                    v.wait_ge(tp_done, i * 2 + (n - 1))
                    v.tensor_scalar(xn[:, n, :], x[:, bass.ds(i * 2 + n, 1), :], rstd[:, bass.ds(i * 2 + n, 1)], None,
                                    ALU.mult).then_inc(xn_done, 1)

        @block.tensor
        def _(pe):
            pe.wait_ge(small_in, 96)

            def tile(n):
                for j in range(DT):
                    last = pe.transpose(tp[:, n, j // 4, j % 4, :], xn[:, n, j * P:(j + 1) * P], ident[:])
                last.then_inc(tp_done, 1)

            for n in range(2):
                pe.wait_ge(xn_done, n + 1)
                tile(n)
            with pe.Fori(1, NT // 2) as i:
                for n in range(2):
                    pe.wait_ge(xn_done, i * 2 + (n + 1))
                    pe.wait_ge(evac, i * 2 + (n - 1))
                    tile(n)


def in_proj(nc, d, hT):
    NC4 = L // BANK
    ROWS = BANK // GRID
    NB = 2 * SSD_DT
    with ExitStack() as ctx:
        sb, ps, sem = pools(nc, ctx)
        w = sb("w_in_sb", [P, 2, DT, P])
        y = sb("proj_sb", [P, 2, NC4, BANK])
        cw = sb("conv_cols", [P, 4, COLT])
        mid = sb("conv_mid", [P, 2, 2])
        wdt = sb("w_dt", [P, DT, NB])
        dtb = sb("dt_bias_col", [NB, 1])
        alog = sb("a_log_row", [P, NB])
        arow = sb("a_row", [P, NB])
        dtT = sb("dt_T", [NB, TOK])
        ident = sb("ident2", [P, P])
        xr, ax, e, u, ln, dd, iz, r = [sb(f"sp_{n}", [P, NT * NB]) for n in ("x", "abs", "e", "u", "ln", "d", "z", "r")]
        dta = sb("dt_a", [P, 2, NT * NB])
        acc = ps("proj_ps", [P, 2, NC4, BANK])
        small_in, wdt_in = sem("ip_small"), sem("ip_wdt")
        w_in = [sem("ip_w0"), sem("ip_w1")]
        mm_done = sem("ip_mm")
        act_done, conv_step, bank_done, silu_done = sem("ip_act"), sem("ip_conv"), sem("ip_bank"), sem("ip_silu")
        z_done, mid_done = sem("ip_z"), sem("ip_mid")
        st_done = [sem("ip_st0"), sem("ip_st1")]
        dt_mm, dt_ev, dt_tp, sp_step, dt_out = sem("ip_dtmm"), sem("ip_dtev"), sem("ip_dttp"), sem("ip_sp"), sem("ip_dto")
        wv = d.w_in.rearrange("(j p) n -> p j n", p=P)
        XT = 6
        H2, Z2, S2, X2 = HYT // 2, (HYT + ZT) // 2, COLT // 2, (COLT + XT) // 2
        block = ctx.enter_context(nc.Block())

        @block.gpsimd
        def _(g):
            with nc.allow_non_contiguous_dma(reason="per-column convolution weights as columns"):
                for k in range(3):
                    g.dma_start(cw[:, k, 0:HYT], d.hy_conv_w[k].rearrange("(j p) -> p j", p=P)).then_inc(small_in, 16)
                    g.dma_start(cw[:, k, HYT + ZT:COLT], d.ssd_conv_w[k].rearrange("(j p) -> p j", p=P))\
                        .then_inc(small_in, 16)
                g.dma_start(cw[:, 3, 0:HYT], d.hy_conv_b.rearrange("(j p) -> p j", p=P)).then_inc(small_in, 16)
                g.dma_start(cw[:, 3, HYT + ZT:COLT], d.ssd_conv_b.rearrange("(j p) -> p j", p=P)).then_inc(small_in, 16)
            g.dma_start(ident[:], d.ident).then_inc(wdt_in, 16)
            g.dma_start(wdt[:], wv[:, :, COLT * P:COLT * P + NB]).then_inc(wdt_in, 16)
            g.dma_start(dtb[:], d.ssd_dt_bias.rearrange("a (h o) -> (a h) o", o=1)).then_inc(wdt_in, 16)
            g.dma_start(alog[:], d.ssd_a_log.rearrange("(o a) h -> o (a h)", o=1).broadcast_to([P, NB]))\
                .then_inc(wdt_in, 16)

        @block.sync
        def _(sp):
            for n in range(2):
                sp.dma_start(w[:, n], wv[:, :, n * P:(n + 1) * P]).then_inc(w_in[n], 16)

            def pair(i, store, load, done=lambda i, n: i * (2 * NC4) + (n + 1) * NC4):
                for n in range(2):
                    if load:
                        sp.wait_ge(mm_done, done(i, n))
                        sp.dma_start(w[:, n], wv[:, :, bass.ds(load(i, n) * P, P)]).then_inc(w_in[n], 16)
                    store(i, n)

            def store_h(i, n):
                sp.wait_ge(bank_done, i * (2 * NC4) + (n + 1) * NC4)
                sp.dma_start(d.uT[bass.ds(i * 2 + n, 1)].rearrange("a p t -> (a p) t"),
                             y[:, n].rearrange("p a b -> p (a b)")).then_inc(st_done[n], 16)

            def store_z(i, n):
                sp.wait_ge(z_done, (i - H2) * (2 * NC4) + (n + 1) * NC4)
                sp.dma_start(d.zT[bass.ds(i * 2 + (n - HYT), 1)].rearrange("a p t -> (a p) t"),
                             y[:, n].rearrange("p a b -> p (a b)")).then_inc(st_done[n], 16)

            def store_s(i, n):
                sp.wait_ge(silu_done, (i - Z2) * 2 + (n + 1))
                sp.dma_start(d.sT[bass.ds(i * 2 + (n - HYT - ZT), 1), :, LC:TOK].rearrange("a p t -> (a p) t"),
                             y[:, n].rearrange("p a b -> p (a b)")).then_inc(st_done[n], 16)

            def store_x(i, n):
                sp.wait_ge(silu_done, (i - Z2) * 2 + (n + 1))
                sp.dma_start(d.sT[bass.ds(i * 2 + (n - COLT), 1), :, 0:LC].rearrange("a p t -> (a p) t"),
                             y[:, n, 0, 0:LC]).then_inc(st_done[n], 16)

            nxt = lambda i, n: i * 2 + (n + 2)
            for a, b, store in ((0, H2, store_h), (H2, Z2, store_z), (Z2, S2 - 1, store_s)):
                with sp.Fori(a, b) as i:
                    pair(i, store, nxt)
            pair(S2 - 1, store_s, lambda i, n: HYT + ZT + n)
            with sp.Fori(S2, X2 - 1) as i:
                pair(i, store_x, lambda i, n: i * 2 + (n + 2 - COLT + HYT + ZT),
                     lambda i, n: COLT * NC4 + (i - S2) * 2 + (n + 1))
            pair(X2 - 1, store_x, None)
            sp.wait_ge(sp_step, 8)
            sp.dma_start(d.dt_a, dta[:].rearrange("p k (t h) -> p k t h", t=NT)).then_inc(dt_out, 16)
            sp.wait_ge(dt_out, 16)
            for n in range(2):
                sp.wait_ge(st_done[n], 16 * X2)

        @block.tensor
        def _(pe):
            def tile(i, n, read=None, off=0):
                pe.wait_ge(w_in[n], i * 16 + 16)
                for c in range(NC4):
                    if read is not None:
                        pe.wait_ge(read, (i - 1 - off) * (2 * NC4) + (n * NC4 + c + 1))
                    for j in range(DT):
                        last = pe.matmul(acc[:, n, c, :], w[:, n, j, :], hT[:, j, LC + c * BANK:LC + (c + 1) * BANK],
                                         start=(j == 0), stop=(j == DT - 1))
                    last.then_inc(mm_done, 1)

            for n in range(2):
                tile(0, n)
            for a, b, read, off in ((1, H2 + 1, bank_done, 0), (H2 + 1, Z2 + 1, z_done, H2),
                                    (Z2 + 1, S2, bank_done, Z2 - H2)):
                with pe.Fori(a, b) as i:
                    for n in range(2):
                        tile(i, n, read, off)
            with pe.Fori(S2, X2) as i:
                for n in range(2):
                    pe.wait_ge(w_in[n], i * 16 + 16)
                    pe.wait_ge(bank_done, (COLT - ZT) * NC4 + (i - S2) * 2 + (n - 1))
                    for j in range(DT):
                        last = pe.matmul(acc[:, n, 0, 0:LC], w[:, n, j, :], hT[:, j, 0:LC],
                                         start=(j == 0), stop=(j == DT - 1))
                    last.then_inc(mm_done, 1)
                pe.wait_ge(wdt_in, 64)
            pe.wait_ge(bank_done, (COLT - ZT) * NC4)
            for c in range(NC4 + 1):
                t0, t1 = c * BANK, min(TOK, (c + 1) * BANK)
                if c:
                    pe.wait_ge(dt_ev, c)
                for j in range(DT):
                    last = pe.matmul(acc[0:NB, 0, 1, 0:t1 - t0], wdt[:, j, :], hT[:, j, t0:t1],
                                     start=(j == 0), stop=(j == DT - 1))
                last.then_inc(dt_mm, 1)
            pe.wait_ge(dt_ev, NC4 + 1)
            for t in range(NT):
                last = pe.transpose(acc[:, 1, 1, t * NB:(t + 1) * NB], dtT[:, t * P:(t + 1) * P], ident[0:NB, 0:NB])
            last.then_inc(dt_tp, 1)

        @block.scalar
        def _(s):
            s.wait_ge(small_in, 128)

            def centre(i, n, first, skip=0):
                s.activation(mid[:, n, :], cw[:, 1:4:2, bass.ds(i * 2 + n, 1)], ACT.Copy).then_inc(mid_done, 1)
                s.wait_ge(mid_done, (i - skip) * 2 + (n + 1))
                if not first:
                    s.wait_ge(st_done[n], i * 16)
                for c in range(NC4):
                    s.wait_ge(mm_done, i * (2 * NC4) + (n * NC4 + c + 1))
                    s.activation(y[:, n, c, :], acc[:, n, c, :], ACT.Identity, bias=mid[:, n, 1:2],
                                 scale=mid[:, n, 0:1]).then_inc(act_done, 1)

            centre(0, 0, True)
            centre(0, 1, True)
            with s.Fori(1, H2) as i:
                for n in range(2):
                    centre(i, n, False)
            with s.Fori(H2, Z2) as i:
                for n in range(2):
                    s.wait_ge(st_done[n], i * 16)
                    for c in range(NC4):
                        s.wait_ge(mm_done, i * (2 * NC4) + (n * NC4 + c + 1))
                        s.activation(y[:, n, c, :], acc[:, n, c, :], ACT.Silu).then_inc(z_done, 1)
            with s.Fori(Z2, S2) as i:
                for n in range(2):
                    centre(i, n, False, Z2 - H2)
                    s.wait_ge(bank_done, (i - (Z2 - H2)) * (2 * NC4) + (n + 1) * NC4)
                    s.activation(y[:, n], y[:, n], ACT.Silu).then_inc(silu_done, 1)
            with s.Fori(S2, X2) as i:
                for n in range(2):
                    s.activation(mid[:, n, :], cw[:, 1:4:2, bass.ds(i * 2 + (n - COLT + HYT + ZT), 1)], ACT.Copy)\
                        .then_inc(mid_done, 1)
                    s.wait_ge(mid_done, (i - (Z2 - H2)) * 2 + (n + 1))
                    s.wait_ge(st_done[n], i * 16)
                    s.wait_ge(mm_done, COLT * NC4 + (i - S2) * 2 + (n + 1))
                    s.activation(y[:, n, 0, 0:LC], acc[:, n, 0, 0:LC], ACT.Identity, bias=mid[:, n, 1:2],
                                 scale=mid[:, n, 0:1]).then_inc(act_done, 1)
                    s.wait_ge(bank_done, (COLT - ZT) * NC4 + (i - S2) * 2 + (n + 1))
                    s.activation(y[:, n, 0, 0:LC], y[:, n, 0, 0:LC], ACT.Silu).then_inc(silu_done, 1)
            s.wait_ge(sp_step, 1)
            s.activation(arow[:], alog[:], ACT.Exp).then_inc(sp_step, 1)
            s.activation(ax[:], xr[:], ACT.Abs).then_inc(dt_ev, 1)
            s.wait_ge(dt_ev, NC4 + 2)
            s.activation(e[:], ax[:], ACT.Exp, scale=-1.0).then_inc(sp_step, 1)
            s.wait_ge(sp_step, 4)
            s.activation(ln[:], u[:], ACT.Ln).then_inc(sp_step, 1)

        @block.vector
        def _(v):
            v.wait_ge(small_in, 128)

            def taps(i, n, c, k, rows, width, act_at, conv_at):
                pv = acc[:, n, c, 0:rows * width].rearrange("p (r t) -> p r t", t=width)
                yv = y[:, n, c, 0:rows * width].rearrange("p (r t) -> p r t", t=width)
                v.wait_ge(act_done, act_at)
                v.scalar_tensor_tensor(out=yv[:, :, 1:], in0=pv[:, :, :-1], scalar=cw[:, 0, k], in1=yv[:, :, 1:],
                                       op0=ALU.mult, op1=ALU.add).then_inc(conv_step, 1)
                v.wait_ge(conv_step, conv_at)
                v.scalar_tensor_tensor(out=yv[:, :, :-1], in0=pv[:, :, 1:], scalar=cw[:, 2, k], in1=yv[:, :, :-1],
                                       op0=ALU.mult, op1=ALU.add).then_inc(bank_done, 1)

            for a, b, off in ((0, H2, 0), (Z2, S2, (Z2 - H2) * 2 * NC4)):
                with v.Fori(a, b) as i:
                    for n in range(2):
                        for c in range(NC4):
                            at = i * (2 * NC4) + (n * NC4 + c + 1 - off)
                            taps(i, n, c, bass.ds(i * 2 + n, 1), ROWS, GRID, at, at)
            base = (COLT - ZT) * NC4
            with v.Fori(S2, X2) as i:
                for n in range(2):
                    at = (i - S2) * 2 + (n + 1 + base)
                    taps(i, n, 0, bass.ds(i * 2 + (n - COLT + HYT + ZT), 1), 1, LC, at, at)
            v.wait_ge(wdt_in, 64)
            for c in range(NC4 + 1):
                t0, t1 = c * BANK, min(TOK, (c + 1) * BANK)
                v.wait_ge(dt_mm, c + 1)
                v.tensor_scalar(dtT[:, t0:t1], acc[0:NB, 0, 1, 0:t1 - t0], dtb[:, 0:1], None, ALU.add)\
                    .then_inc(dt_ev, 1)
            v.wait_ge(dt_tp, 1)
            v.tensor_copy(xr[:], acc[:, 1, 1, 0:NT * NB]).then_inc(sp_step, 1)
            v.wait_ge(sp_step, 3)
            v.tensor_scalar(u[:], e[:], 1.0, None, ALU.add).then_inc(sp_step, 1)
            v.wait_ge(sp_step, 5)
            st = Steps(v, conv_step)
            b0 = base + XT
            st.link(v.tensor_scalar(dd[:], u[:], -1.0, None, ALU.add), b0)
            st.link(v.tensor_scalar(iz[:], dd[:], 0.0, None, ALU.is_equal), b0)
            st.link(v.tensor_tensor(dd[:], dd[:], iz[:], ALU.add), b0)
            st.link(v.reciprocal(r[:], dd[:]), b0)
            st.link(v.tensor_tensor(ln[:], ln[:], r[:], ALU.mult), b0)
            st.link(v.tensor_tensor(ln[:], ln[:], iz[:], ALU.add), b0)
            st.link(v.tensor_tensor(ln[:], ln[:], e[:], ALU.mult), b0)
            v.scalar_tensor_tensor(out=dta[:, 0, :], in0=xr[:], scalar=0.0, in1=ln[:], op0=ALU.max, op1=ALU.add)\
                .then_inc(sp_step, 1)
            v.wait_ge(sp_step, 6)
            v.scalar_tensor_tensor(out=dta[:, 1, :].rearrange("p (t h) -> p t h", t=NT),
                                   in0=dta[:, 0, :].rearrange("p (t h) -> p t h", t=NT), scalar=-1.0,
                                   in1=arow[:].rearrange("p (o h) -> p o h", o=1).broadcast_to([P, NT, NB]),
                                   op0=ALU.mult, op1=ALU.mult).then_inc(sp_step, 2)


def hyena_filters(nc, d):
    NCH = L // BANK
    TWO_PI = 2 * math.pi
    C1 = 6.28125
    C2 = TWO_PI - C1
    MAGIC = 1.5 * 2.0 ** 23
    F2 = HID * 2
    with ExitStack() as ctx:
        sb, ps, sem = pools(nc, ctx)
        feats = sb("feats", [2 * EMB, L])
        w1 = sb("f_w1_diag", [2 * EMB, F2])
        w2 = sb("f_w2_diag", [F2, F2])
        w3 = sb("f_w3", [F2, ORDER, DH])
        cols = sb("f_cols", [F2, 3])
        fb = sb("f_fb", [F2, 2])
        h1 = sb("f_h1", [F2, L])
        h2 = sb("f_h2", [F2, L])
        x, k, r = sb("sin_x", [F2, 2, BANK]), sb("sin_k", [F2, BANK]), sb("sin_r", [F2, 2, BANK])
        tcol = sb("t_col", [P, N2])
        drow = sb("delta_row", [P, DH])
        win = sb("window", [P, 2, DH])
        stat = sb("h_stat", [F2, 2, P])
        blank = sb("blank", [P, D])
        f1 = sb("f1_sb", [P, 2, P])
        kf = sb("k_sb", [P, 2, ORDER, DH])
        tb = sb("tk_sb", [P, 2, ORDER, DH])
        kp = ps("k_ps", [P, 2, ORDER, DH])
        tp = ps("tk_ps", [P, 2, ORDER, DH])
        small_in, zeroed, pre = sem("hf_in"), sem("hf_zero"), sem("hf_pre")
        blanked, blank_out = sem("hf_blank"), sem("hf_blank_out")
        mm, sarg, sined = sem("hf_mm"), sem("hf_arg"), sem("hf_sin")
        f1_in = [sem("hf_f10"), sem("hf_f11")]
        st_out = [sem("hf_st0"), sem("hf_st1")]
        statd, kmm, wind, kfd, tmm, tev = (sem("hf_stat"), sem("hf_kmm"), sem("hf_win"), sem("hf_kf"), sem("hf_tmm"),
                                           sem("hf_tev"))
        step = sem("hf_step")
        block = ctx.enter_context(nc.Block())

        @block.gpsimd
        def _(g):
            g.memset(w1[:], 0.0).then_inc(zeroed, 1)
            g.memset(w2[:], 0.0).then_inc(zeroed, 1)
            g.memset(stat[:], 0.0).then_inc(zeroed, 1)
            g.memset(blank[:], 0.0).then_inc(blanked, 1)
            g.dma_start(feats[:], d.feats).then_inc(small_in, 16)
            g.wait_ge(zeroed, 3)
            for q in range(2):
                g.dma_start(w1[q * EMB:(q + 1) * EMB, q * HID:(q + 1) * HID], d.hy_f_w1).then_inc(small_in, 16)
                g.dma_start(w2[q * HID:(q + 1) * HID, q * HID:(q + 1) * HID], d.hy_f_w2).then_inc(small_in, 16)
                g.dma_start(w3[q * HID:(q + 1) * HID], d.hy_f_w3.rearrange("h (o q c) -> q h o c", o=ORDER, q=2)[q])\
                    .then_inc(small_in, 16)
                for n, a in enumerate((d.hy_f_b1, d.hy_f_b2, d.hy_f_freq)):
                    g.dma_start(cols[q * HID:(q + 1) * HID, n:n + 1], a.rearrange("(h o) -> h o", o=1))\
                        .then_inc(small_in, 16)
            g.dma_start(tcol[:], d.t_col).then_inc(small_in, 16)
            g.dma_start(drow[:], d.delta.rearrange("(o c) -> o c", o=1).broadcast_to([P, DH])).then_inc(small_in, 16)
            g.wait_ge(blanked, 1)
            g.dma_start(d.yb[NE * P:NBLK * P, :].rearrange("(p b) c -> p b c", p=P),
                        blank[:].unsqueeze(1).broadcast_to([P, NOV, D])).then_inc(blank_out, 16)
            g.wait_ge(blank_out, 16)

        @block.sync
        def _(sp):
            for n in range(2):
                sp.dma_start(f1[:, n], d.f1[n]).then_inc(f1_in[n], 16)
            with sp.Fori(0, N2 // 2 - 1) as i:
                for n in range(2):
                    sp.wait_ge(tmm, i * 2 + (n + 1))
                    sp.dma_start(f1[:, n], d.f1[bass.ds(i * 2 + (n + 2), 1)].rearrange("a p m -> (a p) m"))\
                        .then_inc(f1_in[n], 16)
                    sp.wait_ge(tev, i * 2 + (n + 1))
                    sp.dma_start(d.Tk[:, :, bass.ds(i * 2 + n, 1), :].rearrange("o p a c -> p o (a c)"), tb[:, n])\
                        .then_inc(st_out[n], 16)
            for n in range(2):
                sp.wait_ge(tev, N2 - 1 + n)
                sp.dma_start(d.Tk[:, :, N2 - 2 + n, :].rearrange("o p c -> p o c"), tb[:, n]).then_inc(st_out[n], 16)
            for n in range(2):
                sp.wait_ge(st_out[n], 16 * (N2 // 2))

        @block.tensor
        def _(pe):
            pe.wait_ge(small_in, 16 * 15)
            for c in range(NCH):
                if c >= 2:
                    pe.wait_ge(sarg, c - 1)
                pe.matmul(kp[:, c % 2, 0, :], w1[:], feats[:, c * BANK:(c + 1) * BANK], start=True, stop=True)\
                    .then_inc(mm, 1)
            for c in range(NCH):
                pe.wait_ge(sined, c + 1)
                pe.wait_ge(sarg, NCH + c - 1)
                pe.matmul(kp[:, c % 2, 0, :], w2[:], h1[:, c * BANK:(c + 1) * BANK], start=True, stop=True)\
                    .then_inc(mm, 1)
            with pe.Fori(0, N2 // 2) as i:
                for n in range(2):
                    pe.wait_ge(statd, i * 2 + (n + 1))
                    for o in range(ORDER):
                        last = pe.matmul(kp[:, n, o, :], stat[:, n], w3[:, o], start=True, stop=True)
                    last.then_inc(kmm, 1)
                for n in range(2):
                    pe.wait_ge(kfd, i * 2 + (n + 1))
                    pe.wait_ge(f1_in[n], i * 16 + 16)
                    for o in range(ORDER):
                        last = pe.matmul(tp[:, n, o, :], f1[:, n], kf[:, n, o], start=True, stop=True)
                    last.then_inc(tmm, 1)

        @block.vector
        def _(v):
            st = Steps(v, step)
            v.wait_ge(small_in, 16 * 15)
            for n in range(2):
                v.tensor_tensor(fb[:, n:n + 1], cols[:, n:n + 1], cols[:, 2:3], ALU.mult).then_inc(pre, 1)
            v.wait_ge(pre, 2)
            for q in range(2 * NCH):
                layer, c = q // NCH, q % NCH
                v.wait_ge(mm, q + 1)
                if q >= 2:
                    v.wait_ge(sined, q - 1)
                st.link(v.tensor_scalar(x[:, q % 2], kp[:, c % 2, 0, :], cols[:, 2:3], fb[:, layer:layer + 1],
                                        ALU.mult, ALU.add))
                st.link(v.tensor_scalar(k[:], x[:, q % 2], 1.0 / TWO_PI, MAGIC, ALU.mult, ALU.add))
                st.link(v.tensor_scalar(k[:], k[:], -MAGIC, None, ALU.add))
                st.link(v.scalar_tensor_tensor(out=r[:, q % 2], in0=k[:], scalar=-C1, in1=x[:, q % 2], op0=ALU.mult,
                                               op1=ALU.add))
                st.link(v.scalar_tensor_tensor(out=r[:, q % 2], in0=k[:], scalar=-C2, in1=r[:, q % 2], op0=ALU.mult,
                                               op1=ALU.add))
                v.tensor_scalar(r[:, q % 2], r[:, q % 2], 3.1415925, -3.1415925, ALU.min, ALU.max).then_inc(sarg, 1)
                v.wait_ge(sarg, q + 1)
            v.wait_ge(sined, 2 * NCH)
            v.memset(h2[HID:F2, 0:1], 0.0).then_inc(pre, 1)
            v.wait_ge(pre, 3)
            v.wait_ge(zeroed, 3)

            hv = h2[:].rearrange("p (a b) -> p a b", b=N2)

            def stationary(i, n, first):
                if not first:
                    v.wait_ge(kmm, i * 2 + (n - 1))
                v.tensor_copy(stat[0:HID, n, 0:HID], hv[0:HID, :, bass.ds(i * 2 + n, 1)]).then_inc(step, 1)
                v.tensor_copy(stat[HID:F2, n, HID:P], hv[HID:F2, :, bass.ds(i * 2 + n, 1)]).then_inc(statd, 1)

            def windowed(i, n, first):
                if not first:
                    v.wait_ge(tmm, i * 2 + (n - 1))
                v.wait_ge(kmm, i * 2 + (n + 1))
                v.wait_ge(wind, i * 2 + (n + 1))
                for o in range(ORDER):
                    last = v.tensor_tensor(kf[:, n, o], kp[:, n, o, :], win[:, n], ALU.mult)
                last.then_inc(kfd, 1)

            for n in range(2):
                stationary(0, n, True)
            for n in range(2):
                windowed(0, n, True)
            with v.Fori(1, N2 // 2) as i:
                for n in range(2):
                    stationary(i, n, False)
                for n in range(2):
                    windowed(i, n, False)

        @block.scalar
        def _(s):
            for q in range(2 * NCH):
                layer, c = q // NCH, q % NCH
                s.wait_ge(sarg, q + 1)
                s.activation((h1, h2)[layer][:, c * BANK:(c + 1) * BANK], r[:, q % 2], ACT.Sin).then_inc(sined, 1)

            def step_(i, n, first):
                if not first:
                    s.wait_ge(kfd, i * 2 + (n - 1))
                s.wait_ge(small_in, 16 * 15)
                s.activation(win[:, n], drow[:], ACT.Exp, scale=tcol[:, bass.ds(i * 2 + n, 1)]).then_inc(wind, 1)

            def evac(i, n, first):
                if not first:
                    s.wait_ge(st_out[n], i * 16)
                s.wait_ge(tmm, i * 2 + (n + 1))
                s.activation(tb[:, n], tp[:, n], ACT.Copy).then_inc(tev, 1)

            for n in range(2):
                step_(0, n, True)
            for n in range(2):
                evac(0, n, True)
            with s.Fori(1, N2 // 2) as i:
                for n in range(2):
                    step_(i, n, False)
                for n in range(2):
                    evac(i, n, False)


def hyena_forward(nc, d, z, tag):
    NPAIR = N2 // 2
    with ExitStack() as ctx:
        sb, ps, sem = pools(nc, ctx)
        ident = sb(f"ident_{tag}", [P, P])
        zc = sb(f"zc_{tag}", [P, 2, CT, 2, NB1])
        zs = sb(f"zs_{tag}", [P, 2, DH])
        f1 = sb(f"f1z_{tag}", [P, 2, P])
        tb = sb(f"tz_sb_{tag}", [P, 2, 2, DH])
        zt = ps(f"zt_ps_{tag}", [P, 2, DH])
        tp = ps(f"tz_ps_{tag}", [P, 2, 2, DH])
        small_in = sem(f"zf_in_{tag}")
        f1_in = [sem(f"zf_f10_{tag}"), sem(f"zf_f11_{tag}")]
        st_out = [sem(f"zf_st0_{tag}"), sem(f"zf_st1_{tag}")]
        picked, turned, zsd, tmm, tev = [sem(f"zf_{n}_{tag}") for n in ("pick", "turn", "zs", "mm", "ev")]
        block = ctx.enter_context(nc.Block())
        zv = z[:].rearrange("p c (a b) -> p c b a", b=N2)

        def pairs(eng, body):
            for n in range(2):
                body(n, n, 0, True)
            with eng.Fori(1, NPAIR // 2) as i:
                for n in range(2):
                    body(i * 2 + n, n, i, False)

        @block.sync
        def _(sp):
            sp.dma_start(ident[:], d.ident).then_inc(small_in, 16)

            def load(p, n):
                for k in range(2):
                    sp.dma_start(f1[k * NB1:(k + 1) * NB1, n],
                                 d.f1[bass.ds(p * 2 + k, 1), 0:NB1].rearrange("a p m -> (a p) m")).then_inc(f1_in[n], 16)

            def store(p, n):
                sp.wait_ge(tev, p + 1)
                sp.dma_start(d.Tz[:, bass.ds(p * 2, 2), :], tb[:, n]).then_inc(st_out[n], 16)

            for n in range(2):
                load(n, n)
            with sp.Fori(1, NPAIR // 2) as i:
                for n in range(2):
                    sp.wait_ge(tmm, i * 2 + (n - 1))
                    load(i * 2 + n, n)
                    store(i * 2 + (n - 2), n)
            for n in range(2):
                store(NPAIR - 2 + n, n)
            for n in range(2):
                sp.wait_ge(st_out[n], 16 * (NPAIR // 2))

        @block.scalar
        def _(s):
            def evac(p, n, h, first):
                s.wait_ge(tmm, p + 1)
                if not first:
                    s.wait_ge(st_out[n], h * 16)
                s.activation(tb[:, n], tp[:, n], ACT.Copy).then_inc(tev, 1)

            pairs(s, evac)

        @block.gpsimd
        def _(g):
            def pick(p, n, h, first):
                if not first:
                    g.wait_ge(turned, p - 1)
                for k in range(2):
                    last = g.tensor_copy(zc[:, n, :, k, :], zv[:, :, bass.ds(p * 2 + k, 1), :]
                                         .rearrange("p c o a -> p c (o a)"))
                last.then_inc(picked, 1)

            pairs(g, pick)

        @block.tensor
        def _(pe):
            pe.wait_ge(small_in, 16)

            def turn(p, n):
                pe.wait_ge(picked, p + 1)
                for c in range(CT):
                    last = pe.transpose(zt[:, n, c * P:(c + 1) * P], zc[:, n, c].rearrange("p a b -> p (a b)"), ident[:])
                last.then_inc(turned, 1)

            def stage(p, n, h, first):
                if first and n == 0:
                    turn(0, 0)
                turn(p + 1, 1 - n)
                pe.wait_ge(zsd, p + 1)
                pe.wait_ge(f1_in[n], h * 32 + 32)
                if not first:
                    pe.wait_ge(tev, p - 1)
                for k in range(2):
                    at = slice(k * NB1, (k + 1) * NB1)
                    last = pe.matmul(tp[:, n, k], f1[at, n], zs[at, n], start=True, stop=True)
                last.then_inc(tmm, 1)

            for n in range(2):
                stage(n, n, 0, True)
            with pe.Fori(1, NPAIR // 2 - 1) as i:
                for n in range(2):
                    stage(i * 2 + n, n, i, False)
            stage(NPAIR - 2, 0, NPAIR // 2 - 1, False)
            pe.wait_ge(zsd, NPAIR)
            pe.wait_ge(f1_in[1], 16 * NPAIR)
            pe.wait_ge(tev, NPAIR - 2)
            for k in range(2):
                at = slice(k * NB1, (k + 1) * NB1)
                last = pe.matmul(tp[:, 1, k], f1[at, 1], zs[at, 1], start=True, stop=True)
            last.then_inc(tmm, 1)

        @block.vector
        def _(v):
            def evac(p, n, h, first):
                v.wait_ge(turned, p + 1)
                if not first:
                    v.wait_ge(tmm, p - 1)
                v.tensor_copy(zs[:, n], zt[:, n]).then_inc(zsd, 1)

            pairs(v, evac)


def hyena_spectrum(nc, d, o, tag):
    NS = N2 + 1
    with ExitStack() as ctx:
        sb, ps, sem = pools(nc, ctx)
        m2 = sb(f"m2_{tag}", [P, 15, P])
        zi = sb(f"zi_{tag}", [P, 2, DH])
        ki = sb(f"ki_{tag}", [P, 2, DH])
        ks = sb(f"ks_{tag}", [P, 2, 2, DH])
        m = sb(f"prod_{tag}", [P, 2, 2, DH])
        pr = sb(f"spec_{tag}", [P, 2, DH])
        vb = sb(f"v_sb_{tag}", [P, 2, DH])
        za = ps(f"za_ps_{tag}", [P, 2, 2, DH])
        ka = ps(f"ka_ps_{tag}", [P, 2, DH])
        vp = ps(f"v_ps_{tag}", [P, 2, DH])
        m2_in = sem(f"sp_m2_{tag}")
        in_ = [sem(f"sp_in0_{tag}"), sem(f"sp_in1_{tag}")]
        st_out = [sem(f"sp_st0_{tag}"), sem(f"sp_st1_{tag}")]
        fwd, kmm, ksd, mul, prd, inv, vev = [sem(f"sp_{n}_{tag}") for n in
                                             ("fwd", "kmm", "ks", "mul", "pr", "inv", "vev")]
        zt = d.Tz.rearrange("(b j) n c -> b (j n) c", j=4)
        kt = d.Tk[o].rearrange("(b j) n c -> b (j n) c", j=4)
        vt = d.V.rearrange("(b j) n c -> b (j n) c", j=4)
        block = ctx.enter_context(nc.Block())
        FIRST = 3
        VAR = {0: (1, 0, P // 2), 1: (2, P // 2, P)}

        def loop(eng, body):
            with eng.Fori(1, NS // 2) as i:
                body(i * 2 + 1, 1, i, None)
                body(i * 2 + 2, 0, i + 1, None)

        def lead(body):
            for q in range(FIRST):
                body(q, q % 2, q // 2, q)

        @block.sync
        def _(sp):
            sp.dma_start(m2[:], d.m2).then_inc(m2_in, 16)

            def load(q, n, h, known):
                if known is None or known >= 2:
                    sp.wait_ge(kmm, q - 1)
                b = q - 1 if known is None else max(known - 1, 0)
                for t, src in ((zi, zt), (ki, kt)):
                    sp.dma_start(t[:, n], src[bass.ds(b, 1)].rearrange("a p c -> (a p) c")).then_inc(in_[n], 16)

            def store(q, n, known):
                sp.wait_ge(vev, q + 1)
                lo, hi = VAR[known][1:] if known in VAR else (0, P)
                b = q - 1 if known is None else max(known - 1, 0)
                sp.dma_start(vt[bass.ds(b, 1), lo:hi].rearrange("a p c -> (a p) c"), vb[lo:hi, n])\
                    .then_inc(st_out[n], 16)

            lead(load)
            store(0, 0, 0)
            store(1, 1, 1)

            def both(q, n, h, known):
                load(q, n, h, known)
                store(q - 1, 1 - n, None)

            loop(sp, both)
            store(NS - 1, 0, None)
            sp.wait_ge(st_out[0], 16 * (NS // 2 + 1))
            sp.wait_ge(st_out[1], 16 * (NS // 2))

        @block.tensor
        def _(pe):
            pe.wait_ge(m2_in, 16)

            def forward(q, n, h, known):
                v = VAR[known][0] if known in VAR else 0
                pe.wait_ge(in_[n], h * 32 + 32)
                if known is None or known >= 2:
                    pe.wait_ge(mul, q - 1)
                for k in range(2):
                    last = pe.matmul(za[:, n, k], m2[:, v * 5 + k], zi[:, n], start=True, stop=True)
                last.then_inc(fwd, 1)
                if known is None or known >= 1:
                    pe.wait_ge(ksd, q)
                for k in range(2):
                    last = pe.matmul(ka[:, k], m2[:, v * 5 + 2 + k], ki[:, n], start=True, stop=True)
                last.then_inc(kmm, 1)

            def inverse(q, n, known):
                v = VAR[known][0] if known in VAR else 0
                pe.wait_ge(prd, q + 1)
                if known is None or known >= 2:
                    pe.wait_ge(vev, q - 1)
                pe.matmul(vp[:, n], m2[:, v * 5 + 4], pr[:, n], start=True, stop=True).then_inc(inv, 1)

            def both(q, n, h, known):
                forward(q, n, h, known)
                if known != 0:
                    inverse(q - 1, 1 - n, None if known is None else known - 1)

            lead(both)
            loop(pe, both)
            inverse(NS - 1, 0, None)

        @block.scalar
        def _(s):
            def filters(q, n, h, known):
                s.wait_ge(kmm, q + 1)
                if known is None or known >= 2:
                    s.wait_ge(mul, q - 1)
                s.activation(ks[:, n], ka[:], ACT.Copy).then_inc(ksd, 1)

            def evac(q, n, h, known):
                s.wait_ge(inv, q + 1)
                if known is None or known >= 2:
                    s.wait_ge(st_out[n], h * 16)
                s.activation(vb[:, n], vp[:, n], ACT.Copy).then_inc(vev, 1)

            def both(q, n, h, known):
                filters(q, n, h, known)
                if known != 0:
                    evac(q - 1, 1 - n, h if n else h - 1, None if known is None else known - 1)

            lead(both)
            loop(s, both)
            evac(NS - 1, 0, NS // 2, None)

        @block.vector
        def _(v):
            def product(q, n, h, known):
                v.wait_ge(fwd, q + 1)
                v.wait_ge(ksd, q + 1)
                v.tensor_tensor(m[:, n], za[:, n], ks[:, n], ALU.mult).then_inc(mul, 1)
                v.wait_ge(mul, q + 1)
                if known is None or known >= 2:
                    v.wait_ge(inv, q - 1)
                v.tensor_tensor(pr[:, n], m[:, n, 0], m[:, n, 1], ALU.add).then_inc(prd, 1)

            lead(product)
            loop(v, product)


def hyena_inverse(nc, d, z, o, tag):
    with ExitStack() as ctx:
        sb, ps, sem = pools(nc, ctx)
        g1 = sb(f"g1_{tag}", [P, N2, NB1])
        gate = sb(f"gate_{tag}", [P, CT, L])
        zb = sb(f"zb_{tag}", [P, CT, L])
        hb = sb(f"hb_{tag}", [P, CT])
        vi = sb(f"vi_{tag}", [P, 2, 2, DH])
        tmp = sb(f"y_tmp_{tag}", [P, 2, 2, CT, NB1])
        yp = ps(f"y_ps_{tag}", [P, 2, 2, CT, NB1])
        g1_in, gate_in, hb_in = sem(f"hi_g1_{tag}"), sem(f"hi_gate_{tag}"), sem(f"hi_hb_{tag}")
        v_in = [sem(f"hi_v0_{tag}"), sem(f"hi_v1_{tag}")]
        zbd, mm, added, gated = [sem(f"hi_{n}_{tag}") for n in ("zb", "mm", "add", "gate_done")]
        ND = N2 // 2
        block = ctx.enter_context(nc.Block())

        @block.gpsimd
        def _(g):
            with nc.allow_non_contiguous_dma(reason="bias as columns"):
                g.dma_start(hb[:], d.hy_bias[o].rearrange("(j p) -> p j", p=P)).then_inc(hb_in, 16)

        @block.sync
        def _(sp):
            sp.dma_start(g1[:], d.g1).then_inc(g1_in, 16)
            for n in range(2):
                sp.dma_start(vi[:, n], d.V[:, 2 * n:2 * n + 2, :]).then_inc(v_in[n], 16)
            sp.dma_start(gate[:], d.uT[CT * (o + 1):CT * (o + 2)].rearrange("c p t -> p c t")).then_inc(gate_in, 16)
            with sp.Fori(1, ND // 2) as i:
                for n in range(2):
                    sp.wait_ge(mm, i * 2 + (n - 1))
                    sp.dma_start(vi[:, n], d.V[:, bass.ds(i * 4 + 2 * n, 2), :]).then_inc(v_in[n], 16)

        @block.scalar
        def _(s):
            s.wait_ge(hb_in, 16)
            for c in range(CT):
                s.activation(zb[:, c], z[:, c], ACT.Copy, scale=hb[:, c:c + 1]).then_inc(zbd, 1)

        @block.tensor
        def _(pe):
            pe.wait_ge(g1_in, 16)

            def pair(i, n, first):
                pe.wait_ge(v_in[n], i * 16 + 16)
                if not first:
                    pe.wait_ge(added, i * 2 + (n - 1))
                for k in range(2):
                    for c in range(CT):
                        last = pe.matmul(yp[:, n, k, c, :], vi[:, n, k, c * P:(c + 1) * P],
                                         g1[:, bass.ds(i * 4 + (2 * n + k), 1), :], start=True, stop=True)
                last.then_inc(mm, 1)

            for n in range(2):
                pair(0, n, True)
            with pe.Fori(1, ND // 2) as i:
                for n in range(2):
                    pair(i, n, False)

        @block.vector
        def _(v):
            zv, bv, gv = [t[:].rearrange("p c (a b) -> p c a b", b=N2) for t in (z, zb, gate)]
            v.wait_ge(zbd, CT)
            v.wait_ge(gate_in, 16)

            with v.Fori(0, ND // 2) as i:
                for n in range(2):
                    v.wait_ge(mm, i * 2 + (n + 1))
                    for k in range(2):
                        last = v.tensor_tensor(tmp[:, n, k], yp[:, n, k], bv[:, :, :, bass.ds(i * 4 + (2 * n + k), 1)],
                                               ALU.add)
                    last.then_inc(added, 1)
                    v.wait_ge(added, i * 2 + (n + 1))
                    for k in range(2):
                        at = bass.ds(i * 4 + (2 * n + k), 1)
                        last = v.tensor_tensor(zv[:, :, :, at], tmp[:, n, k], gv[:, :, :, at], ALU.mult)
                    last.then_inc(gated, 1)
            v.wait_ge(gated, ND)


def hyena(nc, d):
    hyena_filters(nc, d)
    with ExitStack() as ctx:
        z = ctx.enter_context(nc.sbuf_tensor("z_hy", [P, CT, L], F32))
        move(nc, z[:], d.uT[0:CT].rearrange("c p t -> p c t"), "zin")
        for o in range(ORDER):
            hyena_forward(nc, d, z, f"a{o}")
            hyena_spectrum(nc, d, o, f"b{o}")
            hyena_inverse(nc, d, z, o, f"c{o}")
        move(nc, d.yT[0:CT].rearrange("c p t -> p c t"), z[:], "zout")


def move(nc, dst, src, tag):
    with ExitStack() as ctx:
        done = ctx.enter_context(nc.semaphore(f"moved_{tag}"))
        block = ctx.enter_context(nc.Block())

        @block.sync
        def _(sp):
            sp.dma_start(dst, src).then_inc(done, 16)
            sp.wait_ge(done, 16)


def ssd_weights(nc, d, dta, cum, wend, dec):
    NB = 2 * HEADS
    with ExitStack() as ctx:
        sb, ps, sem = pools(nc, ctx)
        tri = sb("tri", [P, 5, P])
        ident = sb("ident_w", [P, P])
        cT = sb("cum_T", [P, 3, P])
        cp = ps("cum_ps", [P, BANK])
        ep = ps("end_ps", [P, BANK])
        tp = ps("tot_ps", [P, BANK])
        ct = ps("cumT_ps", [P, 3, P])
        ins, mm, cumd, turned, wstep, out_done, evd = (sem("sw_in"), sem("sw_mm"), sem("sw_cum"), sem("sw_turn"),
                                                       sem("sw_step"), sem("sw_out"), sem("sw_ev"))
        block = ctx.enter_context(nc.Block())
        W = NT * NB

        @block.sync
        def _(sp):
            sp.dma_start(tri[:], d.tri).then_inc(ins, 16)
            sp.dma_start(ident[:], d.ident).then_inc(ins, 16)
            sp.dma_start(dta[:], d.dt_a).then_inc(ins, 16)
            sp.wait_ge(evd, 1)
            for k in range(3):
                rows = min(P, W - k * P)
                sp.dma_start(d.cumT[k * P:k * P + rows, :], cT[0:rows, k, :]).then_inc(out_done, 16)
            sp.wait_ge(out_done, 48)

        @block.tensor
        def _(pe):
            pe.wait_ge(ins, 48)
            av = dta[:, 1]
            for k, (acc, lo) in enumerate(((cp, 0), (cp, HEADS), (ep, 0), (ep, HEADS))):
                v = acc[:, 0:W].rearrange("p (t h) -> p t h", h=NB)[:, :, lo:lo + HEADS]
                pe.matmul(v, tri[:, k, :], av[:, :, lo:lo + HEADS], start=True, stop=True)
            pe.matmul(tp[:, 0:W], tri[:, 4, :], av.rearrange("p t h -> p (t h)"), start=True, stop=True).then_inc(mm, 1)
            pe.wait_ge(cumd, 1)
            for k in range(3):
                rows = min(P, W - k * P)
                last = pe.transpose(ct[0:rows, k, :], cum[:].rearrange("p t h -> p (t h)")[:, k * P:k * P + rows],
                                    ident[:])
            last.then_inc(turned, 1)

        @block.vector
        def _(v):
            v.wait_ge(mm, 1)
            v.tensor_copy(cum[:].rearrange("p t h -> p (t h)"), cp[:, 0:W]).then_inc(cumd, 1)
            v.wait_ge(wstep, 1)
            v.tensor_tensor(wend[:], wend[:], dta[:, 0], ALU.mult).then_inc(wstep, 1)
            v.wait_ge(turned, 1)
            v.tensor_copy(cT[:, 0:2], ct[:, 0:2])
            v.tensor_copy(cT[0:W - 2 * P, 2], ct[0:W - 2 * P, 2]).then_inc(evd, 1)

        @block.scalar
        def _(s):
            s.wait_ge(mm, 1)
            s.activation(dec[:].rearrange("p t h -> p (t h)"), tp[:, 0:W], ACT.Exp)
            s.activation(wend[:].rearrange("p t h -> p (t h)"), ep[:, 0:W], ACT.Exp).then_inc(wstep, 1)


def ssd_states(nc, d, H, dirn, wend, dec, lead, many, tag):
    N = len(lead) + (NTX if many else 0)
    W = D_SSD
    with ExitStack() as ctx:
        sb, ps, sem = pools(nc, ctx)
        ident = sb(f"ident_{tag}", [P, P])
        ch = sb(f"ch_{tag}", [P, 2, 6, P])
        bn = sb(f"bn_{tag}", [P, 2, 2 * P])
        xw = sb(f"xw_{tag}", [P, 2, W])
        th = sb(f"th_{tag}", [P, W])
        xp = ps(f"xp_{tag}", [P, 2, W])
        bp = ps(f"bp_{tag}", [P, 2, W])
        sp_ = ps(f"s_{tag}", [P, 2, W])
        small_in = sem(f"st_small_{tag}")
        in_ = [sem(f"st_in0_{tag}"), sem(f"st_in1_{tag}")]
        tp, bnd, xwd, smm, thd, hd = [sem(f"st_{n}_{tag}") for n in ("tp", "bn", "xw", "smm", "th", "h")]
        h_out = [sem(f"st_h0_{tag}"), sem(f"st_h1_{tag}")]
        block = ctx.enter_context(nc.Block())
        h0 = dirn * HEADS

        def run(eng, body):
            for k, c in enumerate(lead):
                body(k, k % 2, 0, c, False)
            if many:
                with eng.Fori(1, N // 2) as i:
                    for n in range(2):
                        body(i * 2 + n, n, i, eng.snap(i * -2 + (NT + 1 - n)), True)

        @block.sync
        def _(sp):
            sp.dma_start(ident[:], d.ident).then_inc(small_in, 16)
            src = d.sT.rearrange("j p t -> p j t")

            def step(k, n, h, c, many_):
                if many_:
                    sp.wait_ge(tp, k - 1)
                at = bass.ds(c * P, P)
                sp.dma_start(ch[:, n], src[:, 0:6, at]).then_inc(in_[n], 16)
                if many:
                    sp.wait_ge(hd, k + 1)
                    sp.dma_start(d.Hb[bass.ds(c, 1)].rearrange("a p w -> (a p) w"), H[:, n]).then_inc(h_out[n], 16)

            run(sp, step)
            if many:
                for n in range(2):
                    sp.wait_ge(h_out[n], 16 * (NT // 2))

        @block.tensor
        def _(pe):
            def step(k, n, h, c, many_):
                pe.wait_ge(in_[n], h * 16 + 16)
                if many_:
                    pe.wait_ge(xwd, k - 1)
                    pe.wait_ge(bnd, k - 1)
                pe.wait_ge(small_in, 16)
                for j in range(4):
                    pe.transpose(xp[:, n, j * P:(j + 1) * P], ch[:, n, j, :], ident[:])
                for j in range(2):
                    last = pe.transpose(bp[:, n, j * P:(j + 1) * P], ch[:, n, 4 + j, :], ident[:])
                last.then_inc(tp, 1)
                pe.wait_ge(xwd, k + 1)
                pe.wait_ge(bnd, k + 1)
                if many_:
                    pe.wait_ge(hd, k)
                for g in range(2):
                    last = pe.matmul(sp_[:, n, g * (W // 2):(g + 1) * (W // 2)], bn[:, n, g * P:(g + 1) * P],
                                     xw[:, n, g * (W // 2):(g + 1) * (W // 2)], start=True, stop=True)
                last.then_inc(smm, 1)

            run(pe, step)

        @block.scalar
        def _(s):
            def step(k, n, h, c, many_):
                s.wait_ge(tp, k + 1)
                if many_:
                    s.wait_ge(smm, k - 1)
                s.activation(bn[:, n], bp[:, n, 0:2 * P], ACT.Copy).then_inc(bnd, 1)

            run(s, step)

        @block.vector
        def _(v):
            v.memset(H[:, 0], 0.0).then_inc(hd, 1)

            def step(k, n, h, c, many_):
                v.wait_ge(tp, k + 1)
                if many_:
                    v.wait_ge(smm, k - 1)
                hs = [t[:, bass.ds(c, 1), h0:h0 + HEADS].rearrange("p a h -> p (a h)").unsqueeze(2)
                      .broadcast_to([P, HEADS, HD]) for t in (wend, dec)]
                v.tensor_tensor(xw[:, n].rearrange("p (h q) -> p h q", q=HD),
                                xp[:, n].rearrange("p (h q) -> p h q", q=HD), hs[0], ALU.mult).then_inc(xwd, 1)
                v.wait_ge(hd, k + 1)
                v.tensor_tensor(th[:].rearrange("p (h q) -> p h q", q=HD),
                                H[:, n].rearrange("p (h q) -> p h q", q=HD), hs[1], ALU.mult).then_inc(thd, 1)
                v.wait_ge(thd, k + 1)
                v.wait_ge(smm, k + 1)
                if many and (many_ or k > 0):
                    v.wait_ge(h_out[1 - n], (h + n) * 16)
                v.tensor_tensor(H[:, 1 - n], th[:], sp_[:, n], ALU.add).then_inc(hd, 1)

            run(v, step)


def ssd_main(nc, d, H, y, cum, wend, dec):
    W = D_SSD
    NB = 2 * HEADS
    with ExitStack() as ctx:
        sb, ps, sem = pools(nc, ctx)
        ident = sb("ident_m", [P, P])
        mask = sb("mask_m", [P, 2, P])
        dta = sb("dta_m", [P, NT, NB])
        dsk = sb("dskip_m", [P, CT])
        ch = sb("ch_m", [P, 2, 8, P])
        zc = sb("z_m", [P, 2, CT, P])
        bc = sb("bc_m", [P, 2, NB, P])
        hb = sb("hb_m", [P, 2, W])
        xn, bn = sb("xn_m", [P, 2, W]), sb("bn_m", [P, 2, 2 * P])
        E = sb("E_m", [P, NB, P])
        Wt = sb("W_m", [P, 2, HEADS, P])
        eb = sb("eb_m", [P, NB, P])
        cs = sb("cs_m", [P, 2, NB, P])
        xw, th = sb("xw_m", [P, 2, W]), sb("th_m", [P, W])
        yt = sb("yt_m", [P, CT, P])
        xp = ps("xp_m", [P, 2, W])
        bp = ps("bp_m", [P, W])
        cbp = ps("cb_m", [P, 2, W])
        s_ps = ps("s_m", [P, W])
        yp = ps("yp_m", [P, 2, CT, P])
        small_in, dsk_in = sem("sm_small"), sem("sm_dsk")
        in_ = [sem("sm_in0"), sem("sm_in1")]
        tp, xnd, bnd, segd, expd, ebd, csd, xwd, smm, hd, wd, ymm, ytd, yd, vstep = [
            sem(f"sm_{n}") for n in ("tp", "xn", "bn", "seg", "exp", "eb", "cs", "xw", "smm", "h", "w", "ymm", "yt", "y",
                                     "step")]
        block = ctx.enter_context(nc.Block())

        def chunks(eng, body):
            for n in range(2):
                body(n, n, 0, True)
            with eng.Fori(1, NTX // 2) as i:
                for n in range(2):
                    body(i * 2 + n, n, i, False)

        @block.sync
        def _(sp):
            sp.dma_start(ident[:], d.ident).then_inc(small_in, 16)
            sp.dma_start(mask[:], d.mask).then_inc(small_in, 16)
            sp.dma_start(dta[:], d.dt_a[:, 0]).then_inc(small_in, 16)

            def step(k, n, h, first):
                if not first:
                    sp.wait_ge(yd, k - 1)
                    sp.wait_ge(csd, k - 1)
                    sp.wait_ge(segd, k - 1)
                sp.dma_start(ch[:, n], d.sT.rearrange("j p t -> p j t")[:, :, bass.ds(LC + k * P, P)])\
                    .then_inc(in_[n], 16)
                sp.dma_start(zc[:, n], d.zT.rearrange("j p t -> p j t")[:, :, bass.ds(k * P, P)]).then_inc(in_[n], 16)
                sp.dma_start(bc[:, n].rearrange("p a b -> p (a b)"),
                             d.cumT[bass.ds((k + NTC) * NB, NB), :].rearrange("(o a) b -> o (a b)", o=1)
                             .broadcast_to([P, NB * P])).then_inc(in_[n], 16)
                sp.dma_start(hb[:, n], d.Hb[bass.ds(k + NTC, 1)].rearrange("a p w -> (a p) w")).then_inc(in_[n], 16)

            chunks(sp, step)

        @block.gpsimd
        def _(g):
            for c in range(CT):
                for a in range(2):
                    g.dma_start(dsk[a * HD:(a + 1) * HD, c:c + 1],
                                d.ssd_d[2 * c + a:2 * c + a + 1].rearrange("(o a) -> o a", o=1).broadcast_to([HD, 1]))\
                        .then_inc(dsk_in, 16)

            def step(k, n, h, first):
                g.wait_ge(ebd, k + 1)
                if not first:
                    g.wait_ge(ymm, k - 1)
                cv = cs[:, n].rearrange("p (v h) t -> p v h t", v=2)
                ev = eb[:].rearrange("p (v h) t -> p v h t", v=2)
                for q in range(2):
                    hs = slice(q * HPG, (q + 1) * HPG)
                    c_ = ch[:, n, 6 + q, :].unsqueeze(1).unsqueeze(1).broadcast_to([P, 2, HPG, P])
                    last = g.tensor_tensor(cv[:, :, hs, :], ev[:, :, hs, :], c_, ALU.mult)
                last.then_inc(csd, 1)

            chunks(g, step)

        @block.tensor
        def _(pe):
            pe.wait_ge(small_in, 16 * 3)

            def turn(k, n, h, first):
                pe.wait_ge(in_[n], h * 64 + 64)
                if not first:
                    pe.wait_ge(xnd, k - 1)
                    pe.wait_ge(wd, k - 1)
                if not first or k > 0:
                    pe.wait_ge(bnd, k)
                pe.wait_ge(small_in, 16 * 3)
                for j in range(4):
                    pe.transpose(xp[:, n, j * P:(j + 1) * P], ch[:, n, j, :], ident[:])
                for j in range(2):
                    pe.transpose(bp[:, j * P:(j + 1) * P], ch[:, n, 4 + j, :], ident[:])
                for j in range(2):
                    last = pe.matmul(cbp[:, n, j * P:(j + 1) * P], ch[:, n, 4 + j, :], ch[:, n, 6 + j, :],
                                     start=True, stop=True)
                last.then_inc(tp, 1)

            def out(k, n, first):
                pe.wait_ge(wd, k + 1)
                pe.wait_ge(csd, k + 1)
                pe.wait_ge(xnd, k + 1)
                pe.wait_ge(hd, k + 1)
                if not first:
                    pe.wait_ge(ytd, k)
                for a in range(HEADS):
                    dst = yp[(a % 2) * HD:(a % 2 + 1) * HD, n, a // 2, :]
                    hs = slice(a * HD, (a + 1) * HD)
                    pe.matmul(dst, xn[:, n, hs], Wt[:, n, a, :], start=True, stop=False, skip_group_check=True)
                    pe.matmul(dst, H[:, n, hs], cs[:, n, a, :], start=False, stop=False, skip_group_check=True)
                    last = pe.matmul(dst, hb[:, n, hs], cs[:, n, HEADS + a, :], start=False, stop=True,
                                     skip_group_check=True)
                last.then_inc(ymm, 1)

            def states(k, n):
                pe.wait_ge(xwd, k + 1)
                pe.wait_ge(bnd, k + 1)
                pe.wait_ge(hd, k + 1)
                for g in range(2):
                    hs = slice(g * (W // 2), (g + 1) * (W // 2))
                    last = pe.matmul(s_ps[:, hs], bn[:, n, g * P:(g + 1) * P], xw[:, n, hs], start=True, stop=True)
                last.then_inc(smm, 1)

            for k in range(2):
                turn(k, k, 0, True)
                if k:
                    out(k - 1, 1 - k, True)
                states(k, k)
            with pe.Fori(1, NTX // 2) as i:
                for n in range(2):
                    k = i * 2 + n
                    turn(k, n, i, False)
                    out(i * 2 + (n - 1), 1 - n, False)
                    states(k, n)
            out(NTX - 1, 1, False)

        @block.scalar
        def _(s):
            def step(k, n, h, first):
                s.wait_ge(in_[n], h * 64 + 64)
                if not first:
                    s.wait_ge(csd, k)
                elif k > 0:
                    s.wait_ge(csd, k)
                s.activation(eb[:], bc[:, n], ACT.Exp).then_inc(ebd, 1)
                s.wait_ge(tp, k + 1)
                if not first:
                    s.wait_ge(ymm, k - 1)
                s.activation(xn[:, n], xp[:, n], ACT.Copy).then_inc(xnd, 1)
                if not first:
                    s.wait_ge(smm, k - 1)
                s.activation(bn[:, n], bp[:, 0:2 * P], ACT.Copy).then_inc(bnd, 1)
                s.wait_ge(segd, k + 1)
                s.activation(E[:], E[:], ACT.Exp).then_inc(expd, 1)

            chunks(s, step)

        @block.vector
        def _(v):
            v.wait_ge(small_in, 16 * 3)
            v.wait_ge(dsk_in, 16 * 2 * CT)

            def spread(t, k, lo, inner):
                return t[:, bass.ds(k + NTC, 1), lo:lo + HEADS].rearrange("p a h -> p (a h)").unsqueeze(2)\
                    .broadcast_to([P, HEADS, inner])

            def post(k, n, first):
                v.wait_ge(ymm, k + 1)
                if not first:
                    v.wait_ge(yd, k)
                for c in range(CT):
                    last = v.scalar_tensor_tensor(out=yt[:, c, :], in0=ch[:, n, c, :], scalar=dsk[:, c:c + 1],
                                                  in1=yp[:, n, c, :], op0=ALU.mult, op1=ALU.add)
                last.then_inc(ytd, 1)
                v.wait_ge(ytd, k + 1)
                v.tensor_tensor(y[:, :, bass.ds(k * P, P)], yt[:], zc[:, n], ALU.mult).then_inc(yd, 1)

            def step(k, n, h, first):
                v.wait_ge(in_[n], h * 64 + 64)
                if first is False or k:
                    v.wait_ge(wd, k)
                for a in range(NB):
                    last = v.scalar_tensor_tensor(out=E[:, a, :], in0=bc[:, n, a, :],
                                                  scalar=cum[:, bass.ds(k + NTC, 1), a], in1=mask[:, a // HEADS, :],
                                                  op0=ALU.subtract, op1=ALU.min)
                last.then_inc(segd, 1)
                v.wait_ge(xnd, k + 1)
                if not first:
                    v.wait_ge(smm, k - 1)
                v.tensor_tensor(xw[:, n].rearrange("p (h q) -> p h q", q=HD),
                                xn[:, n].rearrange("p (h q) -> p h q", q=HD), spread(wend, k, 0, HD), ALU.mult)\
                    .then_inc(xwd, 1)
                v.wait_ge(hd, k + 1)
                v.tensor_tensor(th[:].rearrange("p (h q) -> p h q", q=HD),
                                H[:, n].rearrange("p (h q) -> p h q", q=HD), spread(dec, k, 0, HD), ALU.mult)\
                    .then_inc(vstep, 1)
                v.wait_ge(expd, k + 1)
                for q in range(2):
                    last = v.tensor_tensor(E[:, q * HEADS:(q + 1) * HEADS, :], E[:, q * HEADS:(q + 1) * HEADS, :],
                                           spread(dta, k, q * HEADS, P), ALU.mult)
                last.then_inc(vstep, 1)
                v.wait_ge(vstep, k * 3 + 2)
                v.tensor_tensor(E[:, 0:HEADS, :], E[:, 0:HEADS, :], E[:, HEADS:NB, :], ALU.add).then_inc(vstep, 1)
                v.wait_ge(vstep, k * 3 + 3)
                if not first:
                    v.wait_ge(ymm, k - 1)
                for g in range(2):
                    hs = slice(g * HPG, (g + 1) * HPG)
                    cb = cbp[:, n, g * P:(g + 1) * P].unsqueeze(1).broadcast_to([P, HPG, P])
                    last = v.tensor_tensor(Wt[:, n, hs, :], E[:, hs, :], cb, ALU.mult)
                last.then_inc(wd, 1)

            def update(k, n):
                v.wait_ge(smm, k + 1)
                v.tensor_tensor(H[:, 1 - n], th[:], s_ps[:], ALU.add).then_inc(hd, 1)

            v.sem_inc(hd, 1)
            for n in range(2):
                step(n, n, 0, True)
                if n:
                    post(0, 0, True)
                update(n, n)
            with v.Fori(1, NTX // 2) as i:
                for n in range(2):
                    step(i * 2 + n, n, i, False)
                    post(i * 2 + n - 1, 1 - n, False)
                    update(i * 2 + n, n)
            post(NTX - 1, 1, False)
            v.wait_ge(yd, NTX)


def ssd_norm(nc, d, y):
    with ExitStack() as ctx:
        sb, ps, sem = pools(nc, ctx)
        ones = sb("ones_n", [P, P])
        gn = sb("gn_n", [P, CT])
        sq = sb("sq_n", [P, 2, CT, BANK])
        ms = sb("ms_n", [P, 2, 2, BANK])
        rs = sb("rs_n", [P, 2, 2, BANK])
        acc = ps("acc_n", [P, 2, 2, BANK])
        small_in, sqd, mm, msd, rtd, rcd, yd, out_done = [
            sem(f"sn_{n}") for n in ("in", "sq", "mm", "ms", "rt", "rc", "y", "out")]
        NC4 = L // BANK
        block = ctx.enter_context(nc.Block())

        @block.sync
        def _(sp):
            sp.dma_start(ones[:], d.tri[:, 4, :]).then_inc(small_in, 16)
            with nc.allow_non_contiguous_dma(reason="norm weight as columns"):
                sp.dma_start(gn[:], d.ssd_norm_g.rearrange("(j p) -> p j", p=P)).then_inc(small_in, 16)
            for c in range(NC4):
                sp.wait_ge(yd, c + 1)
                at = slice(c * BANK, (c + 1) * BANK)
                sp.dma_start(d.yT[CT:2 * CT, :, at].rearrange("j p t -> p j t"), y[:, :, at]).then_inc(out_done, 16)
            sp.wait_ge(out_done, 16 * NC4)

        @block.scalar
        def _(s):
            for c in range(NC4):
                if c >= 2:
                    s.wait_ge(mm, c - 1)
                s.activation(sq[:, c % 2], y[:, :, c * BANK:(c + 1) * BANK], ACT.Square).then_inc(sqd, 1)
            for c in range(NC4):
                s.wait_ge(msd, c + 1)
                s.activation(rs[:, c % 2], ms[:, c % 2], ACT.Sqrt).then_inc(rtd, 1)

        @block.tensor
        def _(pe):
            pe.wait_ge(small_in, 32)
            for c in range(NC4):
                pe.wait_ge(sqd, c + 1)
                if c >= 2:
                    pe.wait_ge(msd, c - 1)
                for g in range(2):
                    for j in range(2):
                        last = pe.matmul(acc[:, c % 2, g], ones[:], sq[:, c % 2, 2 * g + j], start=(j == 0), stop=(j == 1))
                last.then_inc(mm, 1)

        @block.vector
        def _(v):
            v.wait_ge(small_in, 32)
            for c in range(NC4):
                n = c % 2
                v.wait_ge(mm, c + 1)
                v.tensor_scalar(ms[:, n], acc[:, n], 2.0 / D_SSD, EPS, ALU.mult, ALU.add).then_inc(msd, 1)
                v.wait_ge(rtd, c + 1)
                v.reciprocal(rs[:, n], rs[:, n]).then_inc(rcd, 1)
                v.wait_ge(rcd, c + 1)
                for j in range(CT):
                    yv = y[:, j, c * BANK:(c + 1) * BANK]
                    last = v.scalar_tensor_tensor(out=yv, in0=yv, scalar=gn[:, j:j + 1], in1=rs[:, n, j // 2],
                                                  op0=ALU.mult, op1=ALU.mult)
                last.then_inc(yd, 1)


def ssd(nc, d):
    NB = 2 * HEADS
    with ExitStack() as ctx:
        sb, _, _ = pools(nc, ctx)
        cum, wend, dec = sb("cum", [P, NT, NB]), sb("wend", [P, NT, NB]), sb("dec", [P, NT, NB])
        H = sb("H_state", [P, 2, D_SSD])
        y = sb("y_ssd", [P, CT, L])
        with ExitStack() as inner:
            dta = inner.enter_context(nc.sbuf_tensor("dta_w", [P, 2, NT, NB], F32))
            ssd_weights(nc, d, dta, cum, wend, dec)
        ssd_states(nc, d, H, 1, wend, dec, [1, 0], True, "bwd")
        ssd_states(nc, d, H, 0, wend, dec, [0, 1], False, "fwd")
        ssd_main(nc, d, H, y, cum, wend, dec)
        ssd_norm(nc, d, y)


def out_proj(nc, d, logits):
    NR = MG + NE
    with ExitStack() as ctx:
        sb, ps, sem = pools(nc, ctx)
        wo = sb("w_out_sb", [P, DT, D])
        wr = sb("w_router", [P, DT, NR])
        br = sb("b_router", [P, NR])
        ga, gs, sh = sb("gate1_row", [P, D]), sb("gs2_row", [P, D]), sb("sh2_row", [P, D])
        g2 = sb("g2_row", [P, D])
        ident = sb("ident_o", [P, P])
        yk = sb("yk", [P, 2, DT, P])
        x = sb("x_o", [P, 2, D])
        t1, x1, h, sq = sb("t_o", [P, D]), sb("x1_o", [P, 2, D]), sb("h2_o", [P, 2, D]), sb("sq_o", [P, D])
        ms, rt, rs = sb("ms_o", [P, 2]), sb("rt_o", [P, 2]), sb("rs_o", [P, 2])
        hT = sb("hT_o", [P, 2, DT, P])
        op = ps("o_ps", [P, 2, 2, BANK])
        tp = ps("h_tp", [P, 2, BANK])
        rp = ps("r_ps", [P, BANK])
        wo_in, row_in, row_done = sem("op_wo"), sem("op_row"), sem("op_rowd")
        in_ = [sem("op_in0"), sem("op_in1")]
        x1_out = [sem("op_x10"), sem("op_x11")]
        h_out = [sem("op_h0"), sem("op_h1")]
        mm, gated, x1d, ssd_, msd, rtd, rsd, nd, hd, h2d, tpd, hTd, rmm, lgd = [
            sem(f"op_{n}") for n in ("mm", "gated", "x1", "ss", "ms", "rt", "rs", "n", "hm", "h", "tp", "hT", "rmm",
                                     "lg")]
        block = ctx.enter_context(nc.Block())

        def tiles(eng, body):
            for n in range(2):
                body(n, n, 0, True)
            with eng.Fori(1, NTX // 2) as i:
                for n in range(2):
                    body(i * 2 + n, n, i, False)

        @block.gpsimd
        def _(g):
            row = lambda a: a.rearrange("(o n) -> o n", o=1)
            for dst, src in ((ga, d.mod[0, 2 * D:3 * D]), (sh, d.mod[0, 3 * D:4 * D]), (gs, d.mod[0, 4 * D:5 * D]),
                             (g2, d.g_norm2)):
                g.dma_start(dst[:], row(src).broadcast_to([P, D])).then_inc(row_in, 16)
            g.dma_start(br[:, 0:MG], row(d.b_group).broadcast_to([P, MG])).then_inc(row_in, 16)
            g.dma_start(br[:, MG:NR], row(d.b_expert).broadcast_to([P, NE])).then_inc(row_in, 16)
            g.dma_start(ident[:], d.ident).then_inc(row_in, 16)
            g.dma_start(wr[:, :, 0:MG], d.w_group.rearrange("(j p) n -> p j n", p=P)).then_inc(row_in, 16)
            g.dma_start(wr[:, :, MG:NR], d.w_expert.rearrange("(j p) n -> p j n", p=P)).then_inc(row_in, 16)

        @block.sync
        def _(sp):
            yv = d.yT.rearrange("j p t -> p j t")

            def load(t, n, h_, first):
                if not first:
                    sp.wait_ge(mm, t - 1)
                    sp.wait_ge(x1d, t - 1)
                at = bass.ds(t * P, P)
                sp.dma_start(yk[:, n], yv[:, :, at]).then_inc(in_[n], 16)
                sp.dma_start(x[:, n], d.x[at, :]).then_inc(in_[n], 16)

            def store(t, n):
                at = bass.ds(t * P, P)
                sp.wait_ge(x1d, t + 1)
                sp.dma_start(d.x1[at, :], x1[:, n]).then_inc(x1_out[n], 16)
                sp.wait_ge(h2d, t + 1)
                sp.dma_start(d.h2[at, :], h[:, n]).then_inc(h_out[n], 16)

            load(0, 0, 0, True)
            sp.dma_start(wo[:, 0:DT // 2], d.w_out.rearrange("(j p) n -> p j n", p=P)[:, 0:DT // 2]).then_inc(wo_in, 16)
            sp.dma_start(wo[:, DT // 2:], d.w_out.rearrange("(j p) n -> p j n", p=P)[:, DT // 2:]).then_inc(wo_in, 16)
            load(1, 1, 0, True)
            with sp.Fori(1, NTX // 2) as i:
                for n in range(2):
                    load(i * 2 + n, n, i, False)
                    store(i * 2 + (n - 2), n)
            for n in range(2):
                store(NTX - 2 + n, n)
            for n in range(2):
                sp.wait_ge(x1_out[n], 16 * (NTX // 2))
                sp.wait_ge(h_out[n], 16 * (NTX // 2))

        @block.tensor
        def _(pe):
            pe.wait_ge(wo_in, 32)
            pe.wait_ge(row_in, 16 * 9)

            def project(t, n, h_, first):
                pe.wait_ge(in_[n], h_ * 32 + 32)
                if not first:
                    pe.wait_ge(gated, t - 1)
                for c in range(2):
                    for j in range(DT):
                        last = pe.matmul(op[:, n, c], yk[:, n, j], wo[:, j, c * BANK:(c + 1) * BANK], start=(j == 0),
                                         stop=(j == DT - 1))
                last.then_inc(mm, 1)

            def route(t, n, first):
                pe.wait_ge(h2d, t + 1)
                if not first:
                    pe.wait_ge(hTd, t)
                pe.wait_ge(wo_in, 32)
                for j in range(DT):
                    last = pe.transpose(tp[:, j // 4, (j % 4) * P:(j % 4 + 1) * P], h[:, n, j * P:(j + 1) * P], ident[:])
                last.then_inc(tpd, 1)
                pe.wait_ge(hTd, t + 1)
                if not first:
                    pe.wait_ge(lgd, t)
                for j in range(DT):
                    last = pe.matmul(rp[:, 0:NR], hT[:, n, j], wr[:, j], start=(j == 0), stop=(j == DT - 1))
                last.then_inc(rmm, 1)

            project(0, 0, 0, True)
            project(1, 1, 0, True)
            route(0, 0, True)
            with pe.Fori(1, NTX // 2) as i:
                for n in range(2):
                    project(i * 2 + n, n, i, False)
                    route(i * 2 + (n - 1), 1 - n, False)
            route(NTX - 1, 1, False)

        @block.scalar
        def _(s):
            def step(t, n, h_, first):
                s.wait_ge(x1d, t + 1)
                if not first or n:
                    s.wait_ge(ssd_, t)
                s.activation(sq[:], x1[:, n], ACT.Square, accum_out=ms[:, n:n + 1]).then_inc(ssd_, 1)
                s.wait_ge(msd, t + 1)
                s.activation(rt[:, n:n + 1], ms[:, n:n + 1], ACT.Sqrt).then_inc(rtd, 1)
                s.wait_ge(tpd, t + 1)
                s.activation(hT[:, n].rearrange("p j t -> p (j t)"), tp[:].rearrange("p a b -> p (a b)"), ACT.Copy)\
                    .then_inc(hTd, 1)

            tiles(s, step)

        @block.vector
        def _(v):
            v.wait_ge(row_in, 16 * 9)
            v.scalar_tensor_tensor(out=gs[:], in0=gs[:], scalar=1.0, in1=g2[:], op0=ALU.add, op1=ALU.mult)\
                .then_inc(row_done, 1)

            def step(t, n, h_, first):
                v.wait_ge(mm, t + 1)
                if not first or n:
                    v.wait_ge(x1d, t)
                v.tensor_tensor(t1[:], op[:, n].rearrange("p a b -> p (a b)"), ga[:], ALU.mult).then_inc(gated, 1)
                v.wait_ge(gated, t + 1)
                if not first:
                    v.wait_ge(x1_out[n], h_ * 16)
                    v.wait_ge(nd, t - 1)
                    v.wait_ge(ssd_, t - 1)
                v.tensor_tensor(x1[:, n], t1[:], x[:, n], ALU.add).then_inc(x1d, 1)
                v.wait_ge(ssd_, t + 1)
                v.tensor_scalar(ms[:, n:n + 1], ms[:, n:n + 1], 1.0 / D, EPS, ALU.mult, ALU.add).then_inc(msd, 1)
                v.wait_ge(rtd, t + 1)
                v.reciprocal(rs[:, n:n + 1], rt[:, n:n + 1]).then_inc(rsd, 1)
                v.wait_ge(rsd, t + 1)
                v.wait_ge(row_done, 1)
                if not first:
                    v.wait_ge(h_out[n], h_ * 16)
                    v.wait_ge(tpd, t - 1)
                v.scalar_tensor_tensor(out=h[:, n], in0=x1[:, n], scalar=rs[:, n:n + 1], in1=gs[:], op0=ALU.mult,
                                       op1=ALU.mult).then_inc(nd, 1)
                v.wait_ge(nd, t + 1)
                v.tensor_tensor(h[:, n], h[:, n], sh[:], ALU.add).then_inc(h2d, 1)
                v.wait_ge(rmm, t + 1)
                v.tensor_tensor(logits[:, bass.ds(t, 1), :].rearrange("p a e -> p (a e)"), rp[:, 0:NR], br[:], ALU.add)\
                    .then_inc(lgd, 1)

            tiles(v, step)
            v.wait_ge(lgd, NTX)


def dispatch(nc, d, logits, gates, slots, blocks):
    T = NTX
    with ExitStack() as ctx:
        sb, ps, sem = pools(nc, ctx)
        tri = sb("tri_d", [P, 5, P])
        iot = sb("iota_d", [P, NE])
        mul = sb("mult_d", [P, MAXB])
        desc = sb("desc_d", [P, EPG])
        tok = sb("tok_d", [P, T], I32)
        zero = sb("zero_d", [P, NBLK], I32)
        s1 = [sb(f"s1_{n}", [P, T, 1]) for n in range(8)]
        m1, den, pg, mv, a1, a2, w1, w2 = s1
        gd, v8, oh, ing, o1, o2, u8 = [sb(f"s8_{n}", [P, T, EPG]) for n in range(7)]
        big = sb("big_d", [P, T, MG, EPG])
        E1, E2, Es = [sb(f"E_{n}", [P, T, NE]) for n in range(3)]
        run = sb("run_d", [P, T + 1, NE])
        cnt, nov, incl, excl, one = [sb(f"c_{n}", [P, NE]) for n in range(5)]
        cb = sb("cmp_d", [P, NE, MAXB])
        r_, e_, o_, q_, b_, f_ = [sb(f"k_{n}", [P, 2, T]) for n in range(6)]
        cq = sb("cmpq_d", [P, T, MAXB])
        idx = sb("idx_d", [P, 2, T], I32)
        ob = sb("ob_d", [1, NOV, NE])
        ov = sb("ov_d", [1, NOV])
        rank = ps("rank_ps", [P, T, NE])
        cps = ps("cnt_ps", [P, NE])
        small_in, z_out, sc_out, tbl_in, tokd = sem("di_in"), sem("di_z"), sem("di_sc"), sem("di_tbl"), sem("di_tok")
        step, gexp, dexp, eready, rmm, idxd, zd, b_in = [sem(f"di_{n}") for n in
                                                         ("step", "gexp", "dexp", "E", "rmm", "idx", "zero", "bin")]
        subd = sem("di_sub")
        block = ctx.enter_context(nc.Block())

        @block.sync
        def _(sp):
            sp.dma_start(tri[:], d.tri).then_inc(small_in, 16)
            for dst, src in ((iot, d.iota), (mul, d.mult), (desc, d.desc)):
                sp.dma_start(dst[:], src.rearrange("(o n) -> o n", o=1).broadcast_to([P, src.shape[0]]))\
                    .then_inc(small_in, 16)
            sp.dma_start(blocks[0:1, 0:NE], d.i_own.rearrange("(o n) -> o n", o=1)).then_inc(b_in, 16)
            sp.wait_ge(b_in, 16)

        @block.gpsimd
        def _(g):
            g.memset(zero[:], 0).then_inc(zd, 1)
            g.iota(tok[:], pattern=[[P, T]], base=0, channel_multiplier=1).then_inc(tokd, 1)
            g.wait_ge(zd, 1)
            g.dma_start(d.i_slot.rearrange("(p b) o -> p (b o)", p=P), zero[:]).then_inc(z_out, 16)
            g.wait_ge(z_out, 16)
            g.wait_ge(tokd, 1)
            g.wait_ge(idxd, 2)
            for k in range(2):
                for t in range(T):
                    g.indirect_dma_start(out=d.i_slot, out_offset=bass.IndirectOffsetOnAxis(ap=idx[:, k, t:t + 1], axis=0),
                                         in_=tok[:, t:t + 1], in_offset=None).then_inc(sc_out, 16)
            g.wait_ge(sc_out, 16 * 2 * T)
            g.dma_start(slots[:, 2], d.i_slot.rearrange("(p b) o -> p (b o)", p=P)).then_inc(tbl_in, 16)
            g.wait_ge(tbl_in, 16)

        @block.scalar
        def _(s):
            s.wait_ge(subd, 1)
            s.activation(gd[:], gd[:], ACT.Exp).then_inc(gexp, 1)
            s.wait_ge(subd, 2)
            s.activation(a2[:], a1[:], ACT.Exp).then_inc(dexp, 1)

        @block.tensor
        def _(pe):
            pe.wait_ge(eready, 1)
            pe.wait_ge(small_in, 64)
            HT = T // 2
            for q in range(2):
                at = slice(q * HT, (q + 1) * HT)
                pe.matmul(rank[:, at], tri[:, 3], Es[:, at], start=True, stop=False)
                pe.matmul(rank[:, at], tri[:, 4], run[:, at], start=False, stop=True)
            pe.matmul(cps[:], tri[:, 4], run[:, T], start=True, stop=True).then_inc(rmm, 1)

        @block.vector
        def _(v):
            st = Steps(v, step)
            link = st.link
            v.wait_ge(small_in, 64)
            gl = logits[:, :, 0:MG]
            el = logits[:, :, MG:MG + NE].rearrange("p t (g e) -> p t g e", g=MG)
            wide = lambda a, n: a[:].broadcast_to([P, T, n])
            dsc = desc[:].unsqueeze(1).broadcast_to([P, T, EPG])

            def first_of(out, val, m):
                link(v.tensor_tensor(out[:], val, wide(m, EPG), ALU.is_equal))
                link(v.tensor_tensor(out[:], out[:], dsc, ALU.mult))
                link(v.tensor_reduce(mv[:], out[:], AX.X, ALU.max))
                link(v.tensor_tensor(out[:], out[:], wide(mv, EPG), ALU.is_equal))

            link(v.tensor_reduce(m1[:], gl, AX.X, ALU.max))
            v.tensor_tensor(gd[:], gl, wide(m1, MG), ALU.subtract).then_inc(subd, 1)
            first_of(oh, gl, m1)
            link(v.tensor_tensor(big[:], el, oh[:].unsqueeze(3).broadcast_to([P, T, MG, EPG]), ALU.mult))
            link(v.tensor_reduce(ing[:], big[:].rearrange("p t g e -> p t e g"), AX.X, ALU.add))
            link(v.tensor_reduce(m1[:], ing[:], AX.X, ALU.max))
            first_of(o1, ing[:], m1)
            link(v.scalar_tensor_tensor(out=u8[:], in0=o1[:], scalar=-1e30, in1=ing[:], op0=ALU.mult, op1=ALU.add))
            link(v.tensor_reduce(a1[:], u8[:], AX.X, ALU.max))
            first_of(o2, u8[:], a1)
            link(v.tensor_tensor(a1[:], a1[:], m1[:], ALU.subtract))
            v.tensor_scalar(a1[:], a1[:], 0.0, None, ALU.add).then_inc(subd, 1)
            v.wait_ge(gexp, 1)
            link(v.tensor_reduce(den[:], gd[:], AX.X, ALU.add))
            link(v.reciprocal(pg[:], den[:]))
            v.wait_ge(dexp, 1)
            link(v.tensor_scalar(w1[:], a2[:], 1.0, None, ALU.add))
            link(v.reciprocal(w1[:], w1[:]))
            link(v.tensor_tensor(w2[:], w1[:], a2[:], ALU.mult))
            for k, w in enumerate((w1, w2)):
                link(v.tensor_tensor(gates[:, k], w[:].rearrange("p t o -> p (t o)"), pg[:].rearrange("p t o -> p (t o)"),
                                     ALU.mult))
            for E, o in ((E1, o1), (E2, o2)):
                link(v.tensor_tensor(E[:].rearrange("p t (g e) -> p t g e", g=MG),
                                     oh[:].unsqueeze(3).broadcast_to([P, T, MG, EPG]),
                                     o[:].unsqueeze(2).broadcast_to([P, T, MG, EPG]), ALU.mult))
            link(v.tensor_tensor(Es[:], E1[:], E2[:], ALU.add))
            link(v.memset(run[:, 0], 0.0))
            for t in range(T):
                link(v.tensor_tensor(run[:, t + 1], run[:, t], Es[:, t], ALU.add))
            v.memset(one[:], 1.0).then_inc(eready, 1)
            v.wait_ge(eready, 1)
            v.wait_ge(rmm, 1)
            link(v.tensor_copy(cnt[:], cps[:]))
            link(v.tensor_tensor(cb[:], cnt[:].unsqueeze(2).broadcast_to([P, NE, MAXB]),
                                 mul[:].unsqueeze(1).broadcast_to([P, NE, MAXB]), ALU.is_gt))
            link(v.tensor_reduce(nov[:], cb[:], AX.X, ALU.add))
            link(v.tensor_tensor_scan(incl[:], one[:], nov[:], 0.0, ALU.mult, ALU.add))
            link(v.tensor_tensor(excl[:], incl[:], nov[:], ALU.subtract))
            row = lambda a: a[:].unsqueeze(1).broadcast_to([P, T, NE])
            bigf = big[:].rearrange("p t g e -> p t (g e)")
            for k, E in enumerate((E1, E2)):
                for dst, src in ((r_, rank[:]), (e_, row(iot)), (o_, row(excl))):
                    link(v.tensor_tensor(bigf, E[:], src, ALU.mult))
                    link(v.tensor_reduce(dst[:, k], bigf, AX.X, ALU.add))
                link(v.tensor_tensor(cq[:], r_[:, k].unsqueeze(2).broadcast_to([P, T, MAXB]),
                                     mul[:].unsqueeze(1).broadcast_to([P, T, MAXB]), ALU.is_ge))
                link(v.tensor_reduce(q_[:, k], cq[:], AX.X, ALU.add))
            link(v.tensor_tensor(o_[:], o_[:], q_[:], ALU.add))
            link(v.scalar_tensor_tensor(out=o_[:], in0=o_[:], scalar=float(NE - 1), in1=e_[:], op0=ALU.add,
                                        op1=ALU.subtract))
            link(v.tensor_scalar(f_[:], q_[:], 0.0, None, ALU.is_gt))
            link(v.tensor_tensor(o_[:], o_[:], f_[:], ALU.mult))
            link(v.tensor_tensor(b_[:], e_[:], o_[:], ALU.add))
            link(v.scalar_tensor_tensor(out=r_[:], in0=q_[:], scalar=-float(P), in1=r_[:], op0=ALU.mult, op1=ALU.add))
            link(v.scalar_tensor_tensor(out=f_[:], in0=r_[:], scalar=float(NBLK), in1=b_[:], op0=ALU.mult, op1=ALU.add))
            v.tensor_copy(idx[:], f_[:]).then_inc(idxd, 1)
            link(v.scalar_tensor_tensor(out=q_[:], in0=b_[:], scalar=float(P), in1=r_[:], op0=ALU.mult, op1=ALU.add))
            v.tensor_copy(slots[:, 0:2, 0:T], q_[:]).then_inc(idxd, 1)
            link(v.tensor_tensor(ob[:], incl[0:1, :].unsqueeze(1).broadcast_to([1, NOV, NE]),
                                 iot[0:1, 0:NOV].unsqueeze(2).broadcast_to([1, NOV, NE]), ALU.is_le))
            link(v.tensor_reduce(ov[:], ob[:], AX.X, ALU.add))
            link(v.tensor_scalar(ov[:], ov[:], float(NE - 1), None, ALU.min))
            link(v.tensor_copy(blocks[0:1, NE:NBLK], ov[:]))
            link(v.tensor_scalar(blocks[0:1, NBLK:NBLK + 1], incl[0:1, NE - 1:NE], float(NE), None, ALU.add))


def experts(nc, d, slots, blocks):
    FT = DE // P
    with ExitStack() as ctx:
        sb, ps, sem = pools(nc, ctx)
        ident = sb("ident_e", [P, P])
        wa, wb, wc = sb("w1_sb", [P, 2, DT, DE]), sb("w3_sb", [P, 2, DT, DE]), sb("w2_sb", [P, 2, FT, D])
        idx = sb("idx_e", [P, 2], I32)
        xb = sb("xb", [P, 2, D])
        xT = sb("xT_e", [P, 2, DT, P])
        s1, g = sb("s1_e", [P, 2, DE]), sb("g_e", [P, 2, DE])
        gT = sb("gT_e", [P, 2, FT, P])
        yo = sb("y_e", [P, 2, D])
        tp = ps("tp_e", [P, 2, BANK])
        h1, h3, gp = ps("h1_e", [P, DE]), ps("h3_e", [P, DE]), ps("gp_e", [P, FT, P])
        yp = ps("yp_e", [P, 2, BANK])
        ident_in, named, stored = sem("ex_id"), sem("ex_named"), sem("ex_stored")
        wa_in, wb_in, wc_in, x_in, y_out = [[sem(f"ex_{n}{k}") for k in range(2)] for n in ("w1", "w3", "w2", "x", "yo")]
        idxd, tpd, xTd, m1, m3, sd, gd, gtp, gTd, ym, yd, ye = [
            sem(f"ex_{n}") for n in ("idx", "tp", "xT", "m1", "m3", "s", "g", "gtp", "gT", "ym", "yd", "ye")]
        block = ctx.enter_context(nc.Block())

        def used(eng):
            return eng.value_load(blocks[0:1, NBLK:NBLK + 1], min_val=NE, max_val=NBLK)

        def run(eng, body):
            total = used(eng)
            for n in range(2):
                body(n, n, 0, True, total)
            with eng.Fori(1, NBLK // 2) as i:
                for n in range(2):
                    q = i * 2 + n
                    with eng.If(q < total):
                        body(q, n, i, False, total)

        @block.gpsimd
        def _(g_):
            def step(q, n, h, first, total):
                if not first:
                    g_.wait_ge(x_in[n], h * 16)
                    g_.wait_ge(tpd, q - 1)
                g_.tensor_copy(idx[:, n:n + 1], slots[:, 2, bass.ds(q, 1)]).then_inc(idxd, 1)
                g_.wait_ge(idxd, q + 1)
                g_.sem_inc(named, 1)
                g_.indirect_dma_start(out=xb[:, n], out_offset=None, in_=d.h2,
                                      in_offset=bass.IndirectOffsetOnAxis(ap=idx[:, n:n + 1], axis=0))\
                    .then_inc(x_in[n], 16)

            run(g_, step)

        @block.sync
        def _(sp):
            sp.dma_start(ident[:], d.ident).then_inc(ident_in, 16)

            def step(q, n, h, first, total):
                e = q if first else sp.value_load(blocks[0:1, bass.ds(q, 1)], min_val=0, max_val=NE - 1)
                for w, src, used_, got, k in ((wa, d.w1, m1, wa_in, DT), (wb, d.w3, m3, wb_in, DT),
                                              (wc, d.w2, ym, wc_in, FT)):
                    if not first:
                        sp.wait_ge(used_, q - 1)
                    sp.dma_start(w[:, n].rearrange("p j f -> p (j f)"),
                                 src[bass.ds(e, 1)].rearrange("a (p j) f -> (a p) (j f)", p=P)).then_inc(got[n], 16)

            run(sp, step)

        @block.tensor
        def _(pe):
            pe.wait_ge(ident_in, 16)

            def turn(q, n, h, first):
                pe.wait_ge(x_in[n], h * 16 + 16)
                if first != 0:
                    pe.wait_ge(xTd, q)
                pe.wait_ge(ident_in, 16)
                xv = xb[:, n].rearrange("p (a j) -> p j a", j=DT)
                for j in range(DT):
                    last = pe.transpose(tp[:, j // 4, (j % 4) * P:(j % 4 + 1) * P], xv[:, j], ident[:])
                last.then_inc(tpd, 1)

            def body(q, n, h, first, total):
                pe.wait_ge(xTd, q + 1)
                for acc, w, got, free, done in ((h1, wa, wa_in, sd, m1), (h3, wb, wb_in, gd, m3)):
                    pe.wait_ge(got[n], h * 16 + 16)
                    if not first or n:
                        pe.wait_ge(free, q)
                    for j in range(DT):
                        last = pe.matmul(acc[:], xT[:, n, j], w[:, n, j], start=(j == 0), stop=(j == DT - 1))
                    last.then_inc(done, 1)
                if first:
                    turn(q + 1, 1 - n, (h, 1)[n], 1)
                else:
                    with pe.If(q + 1 < total):
                        turn(q + 1, 1 - n, (h, h + 1)[n], 1)
                pe.wait_ge(gd, q + 1)
                if not first or n:
                    pe.wait_ge(gTd, q)
                pe.wait_ge(ident_in, 16)
                gv = g[:, n].rearrange("p (a j) -> p j a", j=FT)
                for j in range(FT):
                    last = pe.transpose(gp[:, j], gv[:, j], ident[:])
                last.then_inc(gtp, 1)
                pe.wait_ge(gTd, q + 1)
                pe.wait_ge(wc_in[n], h * 16 + 16)
                if not first or n:
                    pe.wait_ge(yd, q)
                    pe.wait_ge(ye, q)
                for c in range(2):
                    for j in range(FT):
                        last = pe.matmul(yp[:, c], gT[:, n, j], wc[:, n, j, c * BANK:(c + 1) * BANK], start=(j == 0),
                                         stop=(j == FT - 1))
                last.then_inc(ym, 1)

            turn(0, 0, 0, 0)
            run(pe, body)

        @block.scalar
        def _(s):
            def step(q, n, h, first, total):
                if not first:
                    s.wait_ge(m3, q - 1)
                s.wait_ge(tpd, q + 1)
                s.activation(xT[:, n].rearrange("p j t -> p (j t)"), tp[:].rearrange("p a b -> p (a b)"), ACT.Copy)\
                    .then_inc(xTd, 1)
                s.wait_ge(m1, q + 1)
                if not first:
                    s.wait_ge(gd, q - 1)
                s.activation(s1[:, n], h1[:], ACT.Silu).then_inc(sd, 1)
                s.wait_ge(ym, q + 1)
                if not first:
                    s.wait_ge(y_out[n], h * 16)
                s.activation(yo[:, n, 0:BANK], yp[:, 0], ACT.Copy).then_inc(yd, 1)
                s.wait_ge(yd, q + 1)
                s.wait_ge(ye, q + 1)
                s.dma_start(d.yb[bass.ds(q * P, P), :], yo[:, n]).then_inc(y_out[n], 16)

            run(s, step)
            total = used(s)
            for n in range(2):
                s.wait_ge(y_out[n], ((total + (1 - n)) >> 1) * 16)
                s.sem_inc(stored, 1)

        @block.vector
        def _(v):
            def step(q, n, h, first, total):
                v.wait_ge(m3, q + 1)
                v.wait_ge(sd, q + 1)
                if not first:
                    v.wait_ge(gtp, q - 1)
                v.tensor_tensor(g[:, n], s1[:, n], h3[:], ALU.mult).then_inc(gd, 1)
                v.wait_ge(gtp, q + 1)
                if not first:
                    v.wait_ge(ym, q - 1)
                v.tensor_copy(gT[:, n], gp[:]).then_inc(gTd, 1)
                v.wait_ge(ym, q + 1)
                if not first:
                    v.wait_ge(y_out[n], h * 16)
                v.tensor_copy(yo[:, n, BANK:D], yp[:, 1]).then_inc(ye, 1)

            run(v, step)


def combine(nc, d, gates, slots):
    with ExitStack() as ctx:
        sb, _, sem = pools(nc, ctx)
        idx = sb("idx_c", [P, 2, 2], I32)
        yr = sb("yr_c", [P, 2, 2, D])
        gcur = sb("gate_c", [P, 2, 2])
        x1, o = sb("x1_c", [P, 2, D]), sb("out_c", [P, 2, D])
        ga, gf = sb("ga2_row", [P, D]), sb("gf_row", [P, D])
        t = sb("t_c", [P, 2, D])
        sq = sb("sq_c", [P, D])
        ms, rt, rs = sb("ms_c", [P, 2]), sb("rt_c", [P, 2]), sb("rs_c", [P, 2])
        row_in, named = sem("cb_row"), sem("cb_named")
        x_in, y_in, out_done = [[sem(f"cb_{n}{k}") for k in range(2)] for n in ("x", "y", "o")]
        idxd, a, b, c, xd, ssd_, msd, rtd, rsd, od = [sem(f"cb_{n}") for n in
                                                      ("idx", "a", "b", "c", "xd", "ss", "ms", "rt", "rs", "od")]
        block = ctx.enter_context(nc.Block())

        def tiles(eng, body):
            for n in range(2):
                body(n, n, 0, True)
            with eng.Fori(1, NTX // 2) as i:
                for n in range(2):
                    body(i * 2 + n, n, i, False)

        @block.gpsimd
        def _(g):
            def step(k, n, h, first):
                if not first:
                    g.wait_ge(y_in[n], h * 32)
                    g.wait_ge(b, k - 1)
                g.tensor_copy(idx[:, n], slots[:, 0:2, bass.ds(k, 1)].rearrange("p a o -> p (a o)")).then_inc(idxd, 1)
                g.wait_ge(idxd, k + 1)
                g.sem_inc(named, 1)
                for q in range(2):
                    g.indirect_dma_start(out=yr[:, n, q], out_offset=None, in_=d.yb,
                                         in_offset=bass.IndirectOffsetOnAxis(ap=idx[:, n, q:q + 1], axis=0))\
                        .then_inc(y_in[n], 16)

            tiles(g, step)

        @block.sync
        def _(sp):
            row = lambda r: r.rearrange("(o n) -> o n", o=1).broadcast_to([P, D])
            sp.dma_start(ga[:], row(d.mod[0, 5 * D:6 * D])).then_inc(row_in, 16)
            sp.dma_start(gf[:], row(d.g_final)).then_inc(row_in, 16)
            for n in range(2):
                sp.dma_start(x1[:, n], d.x1[n * P:(n + 1) * P, :]).then_inc(x_in[n], 16)

            def store(k, n):
                sp.wait_ge(od, k + 1)
                sp.dma_start(d.out[bass.ds(k * P, P), :], o[:, n]).then_inc(out_done[n], 16)

            with sp.Fori(1, NTX // 2) as i:
                for n in range(2):
                    store(i * 2 + (n - 2), n)
                    sp.dma_start(x1[:, n], d.x1[bass.ds((i * 2 + n) * P, P), :]).then_inc(x_in[n], 16)
            for n in range(2):
                store(NTX - 2 + n, n)
            for n in range(2):
                sp.wait_ge(out_done[n], 16 * (NTX // 2))

        @block.scalar
        def _(s):
            def step(k, n, h, first):
                s.wait_ge(y_in[n], h * 32 + 32)
                s.wait_ge(row_in, 32)
                if not first:
                    s.wait_ge(xd, k - 1)
                s.activation(t[:, n], yr[:, n, 0], ACT.Copy, scale=gates[:, 0, bass.ds(k, 1)]).then_inc(a, 1)
                s.wait_ge(xd, k + 1)
                if not first or n:
                    s.wait_ge(ssd_, k)
                s.activation(sq[:], x1[:, n], ACT.Square, accum_out=ms[:, n:n + 1]).then_inc(ssd_, 1)
                s.wait_ge(msd, k + 1)
                s.activation(rt[:, n:n + 1], ms[:, n:n + 1], ACT.Sqrt).then_inc(rtd, 1)

            tiles(s, step)

        @block.vector
        def _(v):
            v.wait_ge(row_in, 32)

            def step(k, n, h, first):
                v.wait_ge(a, k + 1)
                v.scalar_tensor_tensor(out=t[:, n], in0=yr[:, n, 1], scalar=gates[:, 1, bass.ds(k, 1)], in1=t[:, n],
                                       op0=ALU.mult, op1=ALU.add).then_inc(b, 1)
                v.wait_ge(b, k + 1)
                v.tensor_tensor(t[:, n], t[:, n], ga[:], ALU.mult).then_inc(c, 1)
                v.wait_ge(c, k + 1)
                v.wait_ge(x_in[n], h * 16 + 16)
                v.tensor_tensor(x1[:, n], t[:, n], x1[:, n], ALU.add).then_inc(xd, 1)
                v.wait_ge(ssd_, k + 1)
                v.tensor_scalar(ms[:, n:n + 1], ms[:, n:n + 1], 1.0 / D, EPS, ALU.mult, ALU.add).then_inc(msd, 1)
                v.wait_ge(rtd, k + 1)
                v.reciprocal(rs[:, n:n + 1], rt[:, n:n + 1]).then_inc(rsd, 1)
                v.wait_ge(rsd, k + 1)
                if not first:
                    v.wait_ge(out_done[n], h * 16)
                v.scalar_tensor_tensor(out=o[:, n], in0=x1[:, n], scalar=rs[:, n:n + 1], in1=gf[:], op0=ALU.mult,
                                       op1=ALU.mult).then_inc(od, 1)

            tiles(v, step)


def moe(nc, d):
    with ExitStack() as ctx:
        sb, _, _ = pools(nc, ctx)
        gates = sb("gates", [P, 2, NTX])
        slots = sb("slots", [P, 3, NBLK], I32)
        blocks = sb("blocks", [1, NBLK + 1], I32)
        with ExitStack() as inner:
            logits = inner.enter_context(nc.sbuf_tensor("logits", [P, NTX, MG + NE], F32))
            out_proj(nc, d, logits)
            dispatch(nc, d, logits, gates, slots, blocks)
        experts(nc, d, slots, blocks)
        combine(nc, d, gates, slots)


def constants():
    c = {}
    c["ident"] = np.eye(P, dtype=np.float32)
    fwd = np.arange(L)
    bwd = np.where(fwd == 0, 0, L - fwd)
    bands = np.linspace(1e-4, BANDS - 1, BANDS, dtype=np.float32)
    feats = []
    for pos in (fwd, bwd):
        ang = (np.float32(2 * math.pi / L) * pos[:, None].astype(np.float32)) * bands[None, :]
        t = (pos.astype(np.float32) / np.float32(L - 1))[:, None]
        feats.append(np.concatenate([t, np.cos(ang), -np.sin(ang)], axis=1).T)
    c["feats"] = np.concatenate(feats).astype(np.float32)
    pos = np.concatenate([fwd, bwd]).astype(np.float32) / np.float32(L - 1)
    c["t_col"] = np.ascontiguousarray(-pos.reshape(P, N2)).astype(np.float32)
    c["delta"] = np.abs(np.linspace(math.log(TARGET) / SLOW, math.log(TARGET) / FAST, DH, dtype=np.float32))
    N = 2 * L
    n1, n2 = np.arange(P), np.arange(N2)
    k1 = np.arange(1, NB1)
    ph = 2 * np.pi * ((N2 * n1[None, :, None] + n2[:, None, None]) * k1 % N) / N
    f1 = np.zeros((N2, P, P))
    f1[:, :, 0] = 1
    f1[:, :, 1] = (-1.0) ** n1
    f1[:, :, 2::2] = np.cos(ph)
    f1[:, :, 3::2] = -np.sin(ph)
    c["f1"] = f1.astype(np.float32)
    g1 = np.zeros((P, N2, NB1))
    half = ph[:, :NB1]
    g1[0] = 1
    g1[1] = (-1.0) ** n1[:NB1]
    g1[2::2] = 2 * np.cos(half).transpose(2, 0, 1)
    g1[3::2] = -2 * np.sin(half).transpose(2, 0, 1)
    c["g1"] = (g1 / N).astype(np.float32)
    th = 2 * np.pi * np.outer(n2, n2) / N2
    co, si = np.cos(th), np.sin(th)
    tw = 2 * np.pi * n2 / 64
    O = np.zeros((N2, N2))
    rr, ir, ri, ii = co, si, -si, co
    one = {"A": [[rr, ri], [ir, ii]], "B": [[ri, rr], [ii, ir]],
           "kA": [[rr, rr], [ir, ir]], "kB": [[-ri, ri], [-ii, ii]]}
    c64, s64 = np.cos(th + tw[:, None]), np.sin(th + tw[:, None])
    m2 = np.zeros((15, P, P))
    H = P // 2
    for n, name in enumerate(("A", "B", "kA", "kB")):
        b = np.block(one[name])
        m2[n, :H, :H] = m2[n, H:, H:] = b
        for row, (cc, ss) in enumerate(((co, si), (c64, s64))):
            real, imag = cc, -ss
            parts = {"A": (real, imag), "B": (imag, real), "kA": (real, real), "kB": (-imag, imag)}[name]
            m2[5 + n, row * N2:(row + 1) * N2, row * H:(row + 1) * H] = np.concatenate(parts, axis=1)
        m2[10 + n, H:, :H] = b
    inv = np.block([[co, si], [-si, co]])
    m2[4, :H, :H] = m2[4, H:, H:] = inv
    m2[9, 0:N2, 0:N2], m2[9, N2:H, 0:N2] = co, -si
    ci, s_i = np.cos(th + tw[None, :]), np.sin(th + tw[None, :])
    m2[9, H:H + N2, N2:H], m2[9, H + N2:, N2:H] = ci, -s_i
    m2[14, :H, H:] = inv
    j, l = np.arange(P)[:, None], np.arange(P)[None, :]
    c["tri"] = np.stack([j <= l, j >= l, j > l, j < l, j + l >= 0], axis=1).astype(np.float32)
    c["mask"] = np.where(np.stack([l >= j, l <= j], axis=1), 0.0, -1e30).astype(np.float32)
    c["iota"] = np.arange(NE, dtype=np.float32)
    c["mult"] = (P * np.arange(1, MAXB + 1)).astype(np.float32)
    c["desc"] = np.arange(EPG, 0, -1).astype(np.float32)
    c["i_own"] = np.arange(NE, dtype=np.int32)
    c["m2"] = np.ascontiguousarray(m2.transpose(1, 0, 2)).astype(np.float32)
    return c


SCRATCH = {
    "mod": [2, 6 * D],
    "uT": [HYT, P, L],
    "zT": [ZT, P, L],
    "sT": [XBCT, P, TOK],
    "Tk": [ORDER, P, N2, DH],
    "Tz": [P, N2, DH],
    "V": [P, N2, DH],
    "yT": [2 * CT, P, L],
    "cumT": [NT * 2 * HEADS, P],
    "Hb": [NT, P, D_SSD],
    "x1": [L, D],
    "h2": [L, D],
    "i_slot": [P * NBLK, 1],
    "yb": [NBLK * P, D],
    "dt_a": [P, 2, NT, 2 * HEADS],
}


def program(nc, d):
    adaln(nc, d)
    with ExitStack() as hctx:
        hT = hctx.enter_context(nc.sbuf_tensor("hT", [P, DT, TOK], F32))
        norm_in(nc, d, hT)
        in_proj(nc, d, hT)
    hyena(nc, d)
    ssd(nc, d)
    moe(nc, d)


NAMES = ["x", "c", "ctx", "c_ctx", "w_ada", "b_ada", "g_norm1", "g_norm2", "w_in", "hy_conv_w", "hy_conv_b",
         "hy_f_w1", "hy_f_b1", "hy_f_freq", "hy_f_w2", "hy_f_b2", "hy_f_w3", "hy_bias", "ssd_conv_w", "ssd_conv_b",
         "ssd_a_log", "ssd_dt_bias", "ssd_d", "ssd_norm_g", "w_out", "w_group", "b_group", "w_expert", "b_expert",
         "w1", "w3", "w2", "g_final"]


def layout(name, a):
    return a if name in ("c_ctx", "g_final") else a[0]


def kernel(**inputs):
    import concourse.bacc as _bacc
    from concourse.bass_utils import run_bass_kernel_spmd as _run

    nc = _bacc.Bacc("TRN2", target_bir_lowering=False, num_devices=1)
    arrays, put = {}, {}
    host = {n: np.ascontiguousarray(layout(n, inputs[n])) for n in NAMES}
    host.update(constants())
    for name, a in host.items():
        arrays[f"in_{name}"] = a
        put[name] = nc.dram_tensor(f"in_{name}", a.shape, mybir.dt.from_np(a.dtype), kind="ExternalInput").ap()
    put["out"] = nc.dram_tensor("out_0", (L, D), F32, kind="ExternalOutput").ap()
    for name, shape in SCRATCH.items():
        put[name] = nc.dram_tensor(f"s_{name}", shape, I32 if name.startswith("i_") else F32, kind="Internal").ap()
    program(nc, namedtuple("Arrays", sorted(put))(**put))
    r = _run(nc, [arrays], core_ids=[0])
    return r.results[0]["out_0"].reshape(1, L, D)
```

```python
import math
from collections import namedtuple
from contextlib import ExitStack

import numpy as np

import concourse.bass as bass
from concourse import mybir

F32 = mybir.dt.float32
F32R = mybir.dt.float32r
I32 = mybir.dt.int32
ALU = mybir.AluOpType
ACT = mybir.ActivationFunctionType
AX = mybir.AxisListType

P = 128
D = 1024
DT = D // P
L = 2048
LC = 256
TOK = LC + L
NTX = L // P
NTC = LC // P
NT = NTX + NTC
GRID = 64
EPS = 1e-6
BANK = 512
DH = 512
CT = DH // P
HYT = 12
ZT = 4
XBCT = 8
COLT = HYT + ZT + XBCT
HEADS = 8
MG, EPG = 8, 8
NE = MG * EPG
DE = 512
NOV = 2 * L // P
NBLK = NE + NOV
MAXB = L // P - 1
HD = 64
HPG = HEADS // 2
D_SSD = HEADS * HD
SSD_DT = HEADS
ORDER = 2
BANDS = 8
EMB = 1 + 2 * BANDS
HID = 64
FAST, SLOW, TARGET = 0.3, 1.5, 1e-2
N2 = 2 * L // P
NB1 = L // N2


def pools(nc, ctx):
    def sb(name, shape, dt=F32):
        return ctx.enter_context(nc.sbuf_tensor(name, shape, dt))

    def ps(name, shape, dt=F32):
        return ctx.enter_context(nc.psum_tensor(name, shape, dt))

    held = []

    def sem(name):
        held.append(nc.alloc_semaphore(name))
        return held[-1]

    def release():
        if held:
            nc.clear_and_free_semaphores(held)
            nc.all_engine_barrier()

    ctx.callback(release)
    return sb, ps, sem


def split_pair(nc, ctx, name, shape):
    at = -(-nc.sbuf_base // 32) * 32
    whole = ctx.enter_context(nc.sbuf_tensor(name, shape, F32))
    return whole, nc.alloc_sbuf_tensor_at(f"{name}_lo", shape, F32R, offset=at)


class Steps:

    def __init__(self, eng, sem):
        self.eng, self.sem, self.n = eng, sem, 0

    def done(self, ins):
        ins.then_inc(self.sem, 1)
        self.n += 1
        return ins

    def join(self, base=0):
        self.eng.wait_ge(self.sem, base + self.n)

    def link(self, ins, base=0):
        self.done(ins)
        self.join(base)


def adaln(nc, d):
    NCH = 6 * D // BANK
    with ExitStack() as ctx:
        sb, ps, sem = pools(nc, ctx)
        cond = sb("cond", [P, 2, DT])
        act = sb("cond_silu", [P, DT, 2])
        w = sb("w_ada_sb", [P, 2, DT, BANK])
        bias = sb("b_ada_sb", [2, 6 * D])
        mod = sb("mod_sb", [2, 6 * D])
        acc = ps("mod_ps", [P, 2, BANK])
        cond_in, bias_in, silu_done, out_done = sem("cond_in"), sem("bias_in"), sem("silu_done"), sem("mod_out")
        w_in = [sem("w_ada_in0"), sem("w_ada_in1")]
        w_used, mm_done, mod_done = sem("w_ada_used"), sem("mod_mm"), sem("mod_done")
        wv = d.w_ada.rearrange("(p j) n -> p j n", p=P)
        block = ctx.enter_context(nc.Block())

        @block.sync
        def _(sp):
            sp.dma_start(cond[:, 0, :], d.c.rearrange("(p j) -> p j", p=P)).then_inc(cond_in, 16)
            sp.dma_start(cond[:, 1, :], d.c_ctx.rearrange("(p j) -> p j", p=P)).then_inc(cond_in, 16)
            for v in range(2):
                sp.dma_start(bias[v:v + 1, :], d.b_ada.rearrange("(a n) -> a n", a=1)).then_inc(bias_in, 16)
            for n in range(2):
                sp.dma_start(w[:, n], wv[:, :, n * BANK:(n + 1) * BANK]).then_inc(w_in[n], 16)
            with sp.Fori(1, NCH // 2) as i:
                for n in range(2):
                    sp.wait_ge(mm_done, i * 2 + (n - 1))
                    sp.dma_start(w[:, n], wv[:, :, bass.ds((i * 2 + n) * BANK, BANK)]).then_inc(w_in[n], 16)
            sp.wait_ge(mod_done, NCH)
            sp.dma_start(d.mod, mod[:, :]).then_inc(out_done, 16)
            sp.wait_ge(out_done, 16)

        @block.scalar
        def _(s):
            s.wait_ge(cond_in, 32)
            s.activation(act[:].rearrange("p j v -> p v j"), cond[:], ACT.Silu).then_inc(silu_done, 1)

        @block.tensor
        def _(pe):
            pe.wait_ge(silu_done, 1)
            for n in range(2):
                pe.wait_ge(w_in[n], 16)
                for j in range(DT):
                    last = pe.matmul(acc[0:2, n, :], act[:, j, :], w[:, n, j, :], start=(j == 0), stop=(j == DT - 1))
                last.then_inc(mm_done, 1)
            with pe.Fori(1, NCH // 2) as i:
                for n in range(2):
                    pe.wait_ge(w_in[n], i * 16 + 16)
                    pe.wait_ge(mod_done, i * 2 + (n - 1))
                    for j in range(DT):
                        last = pe.matmul(acc[0:2, n, :], act[:, j, :], w[:, n, j, :],
                                         start=(j == 0), stop=(j == DT - 1))
                    last.then_inc(mm_done, 1)

        @block.vector
        def _(v):
            v.wait_ge(bias_in, 32)
            with v.Fori(0, NCH // 2) as i:
                for n in range(2):
                    v.wait_ge(mm_done, i * 2 + (n + 1))
                    at = bass.ds((i * 2 + n) * BANK, BANK)
                    v.tensor_tensor(mod[:, at], acc[0:2, n, :], bias[:, at], ALU.add).then_inc(mod_done, 1)


def norm_in(nc, d, hT):
    with ExitStack() as ctx:
        sb, ps, sem = pools(nc, ctx)
        x = sb("x_tok", [P, NT, D])
        sq = sb("x_sq", [P, D])
        ms = sb("x_ms", [P, NT])
        rms = sb("x_rms", [P, NT])
        rstd = sb("x_rstd", [P, NT])
        xn = sb("x_n", [P, 2, D])
        ident = sb("ident", [P, P])
        m = sb("mod_cols", [P, 2, 2, DT])
        g = sb("g1_cols", [P, DT])
        gs = sb("g1_scale", [P, 2, DT])
        tp = ps("x_tp", [P, 2, 2, 4, P])
        x_in, small_in = sem("x_in"), sem("nin_small")
        ss_done, rs, scale_ready = sem("nin_ss"), sem("nin_rs"), sem("nin_scale")
        xn_done, tp_done, evac = sem("nin_xn"), sem("nin_tp"), sem("nin_evac")
        block = ctx.enter_context(nc.Block())

        @block.sync
        def _(sp):
            sp.dma_start(x[:, 0:NTC, :], d.ctx.rearrange("(t p) n -> p t n", p=P)).then_inc(x_in, 16)
            for q in range(4):
                a = q * 4
                sp.dma_start(x[:, NTC + a:NTC + a + 4, :], d.x.rearrange("(t p) n -> p t n", p=P)[:, a:a + 4, :])\
                    .then_inc(x_in, 16)

        @block.gpsimd
        def _(g_):
            g_.dma_start(ident[:], d.ident).then_inc(small_in, 16)
            with nc.allow_non_contiguous_dma(reason="modulation vectors as columns"):
                g_.dma_start(g[:], d.g_norm1.rearrange("(j p) -> p j", p=P)).then_inc(small_in, 16)
                for v in range(2):
                    for s in range(2):
                        g_.dma_start(m[:, v, s, :], d.mod[v, s * D:(s + 1) * D].rearrange("(j p) -> p j", p=P))\
                            .then_inc(small_in, 16)

        @block.scalar
        def _(s):
            s.wait_ge(x_in, 80)
            with s.Fori(0, NT) as t:
                s.activation(sq[:], x[:, bass.ds(t, 1), :], ACT.Square, accum_out=ms[:, bass.ds(t, 1)])\
                    .then_inc(ss_done, 1)
                s.wait_ge(ss_done, t + 1)
            s.wait_ge(rs, 1)
            s.activation(rms[:], ms[:], ACT.Sqrt).then_inc(rs, 1)
            s.wait_ge(scale_ready, 2)
            for v, t0, t1 in ((1, 0, NTC // 2), (0, NTC // 2, NT // 2)):
                with s.Fori(t0, t1) as i:
                    for n in range(2):
                        s.wait_ge(tp_done, (i * 2 + n) + 1)
                        s.wait_ge(scale_ready, 2)
                        for j in range(DT):
                            last = s.activation(hT[:, j, bass.ds((i * 2 + n) * P, P)], tp[:, n, j // 4, j % 4, :],
                                                ACT.Identity, bias=m[:, v, 0, j:j + 1], scale=gs[:, v, j:j + 1])
                        last.then_inc(evac, 1)

        @block.vector
        def _(v):
            st = Steps(v, scale_ready)
            v.wait_ge(small_in, 96)
            for k in range(2):
                v.scalar_tensor_tensor(out=gs[:, k, :], in0=m[:, k, 1, :], scalar=1.0, in1=g[:], op0=ALU.add,
                                       op1=ALU.mult).then_inc(scale_ready, 1)
            v.wait_ge(ss_done, NT)
            v.tensor_scalar(ms[:], ms[:], 1.0 / D, EPS, ALU.mult, ALU.add).then_inc(rs, 1)
            v.wait_ge(rs, 2)
            v.reciprocal(rstd[:], rms[:]).then_inc(rs, 1)
            v.wait_ge(rs, 3)
            for n in range(2):
                v.tensor_scalar(xn[:, n, :], x[:, n, :], rstd[:, n:n + 1], None, ALU.mult).then_inc(xn_done, 1)
            with v.Fori(1, NT // 2) as i:
                for n in range(2):
                    v.wait_ge(tp_done, i * 2 + (n - 1))
                    v.tensor_scalar(xn[:, n, :], x[:, bass.ds(i * 2 + n, 1), :], rstd[:, bass.ds(i * 2 + n, 1)], None,
                                    ALU.mult).then_inc(xn_done, 1)

        @block.tensor
        def _(pe):
            pe.wait_ge(small_in, 96)

            def tile(n):
                for j in range(DT):
                    last = pe.transpose(tp[:, n, j // 4, j % 4, :], xn[:, n, j * P:(j + 1) * P], ident[:])
                last.then_inc(tp_done, 1)

            for n in range(2):
                pe.wait_ge(xn_done, n + 1)
                tile(n)
            with pe.Fori(1, NT // 2) as i:
                for n in range(2):
                    pe.wait_ge(xn_done, i * 2 + (n + 1))
                    pe.wait_ge(evac, i * 2 + (n - 1))
                    tile(n)


def in_proj(nc, d, hT, hl, hh):
    NC4 = L // BANK
    ROWS = BANK // GRID
    with ExitStack() as ctx:
        sb, ps, sem = pools(nc, ctx)
        (w, wl), wh = split_pair(nc, ctx, "w_in_sb", [P, 2, DT, P]), sb("w_in_hi", [P, 2, DT, P], F32R)
        y = sb("proj_sb", [P, 2, NC4, BANK])
        cw = sb("conv_cols", [P, 4, COLT])
        mid = sb("conv_mid", [P, 2, 2])
        acc = ps("proj_ps", [P, 2, NC4, BANK])
        small_in = sem("ip_small")
        w_in = [sem("ip_w0"), sem("ip_w1")]
        mm_done = sem("ip_mm")
        act_done, conv_step, bank_done, silu_done = sem("ip_act"), sem("ip_conv"), sem("ip_bank"), sem("ip_silu")
        z_done, mid_done = sem("ip_z"), sem("ip_mid")
        st_done = [sem("ip_st0"), sem("ip_st1")]
        whd, wld, hhd, hld = [sem(f"ip_{n}") for n in ("wh", "wl", "hh", "hl")]
        CHUNKS = [slice(LC + c * BANK, LC + (c + 1) * BANK) for c in range(NC4)] + [slice(0, LC)]
        wv = d.w_in.rearrange("(j p) n -> p j n", p=P)
        XT = 6
        H2, Z2, S2, X2 = HYT // 2, (HYT + ZT) // 2, COLT // 2, (COLT + XT) // 2
        block = ctx.enter_context(nc.Block())

        @block.gpsimd
        def _(g):
            with nc.allow_non_contiguous_dma(reason="per-column convolution weights as columns"):
                for k in range(3):
                    g.dma_start(cw[:, k, 0:HYT], d.hy_conv_w[k].rearrange("(j p) -> p j", p=P)).then_inc(small_in, 16)
                    g.dma_start(cw[:, k, HYT + ZT:COLT], d.ssd_conv_w[k].rearrange("(j p) -> p j", p=P))\
                        .then_inc(small_in, 16)
                g.dma_start(cw[:, 3, 0:HYT], d.hy_conv_b.rearrange("(j p) -> p j", p=P)).then_inc(small_in, 16)
                g.dma_start(cw[:, 3, HYT + ZT:COLT], d.ssd_conv_b.rearrange("(j p) -> p j", p=P)).then_inc(small_in, 16)

        @block.sync
        def _(sp):
            for n in range(2):
                sp.dma_start(w[:, n], wv[:, :, n * P:(n + 1) * P]).then_inc(w_in[n], 16)

            def pair(i, store, load, done=lambda i, n: i * (2 * NC4) + (n + 1) * NC4):
                for n in range(2):
                    if load:
                        sp.wait_ge(mm_done, done(i, n))
                        sp.dma_start(w[:, n], wv[:, :, bass.ds(load(i, n) * P, P)]).then_inc(w_in[n], 16)
                    store(i, n)

            def store_h(i, n):
                sp.wait_ge(bank_done, i * (2 * NC4) + (n + 1) * NC4)
                sp.dma_start(d.uT[bass.ds(i * 2 + n, 1)].rearrange("a p t -> (a p) t"),
                             y[:, n].rearrange("p a b -> p (a b)")).then_inc(st_done[n], 16)

            def store_z(i, n):
                sp.wait_ge(z_done, (i - H2) * (2 * NC4) + (n + 1) * NC4)
                sp.dma_start(d.zT[bass.ds(i * 2 + (n - HYT), 1)].rearrange("a p t -> (a p) t"),
                             y[:, n].rearrange("p a b -> p (a b)")).then_inc(st_done[n], 16)

            def store_s(i, n):
                sp.wait_ge(silu_done, (i - Z2) * 2 + (n + 1))
                sp.dma_start(d.sT[bass.ds(i * 2 + (n - HYT - ZT), 1), :, LC:TOK].rearrange("a p t -> (a p) t"),
                             y[:, n].rearrange("p a b -> p (a b)")).then_inc(st_done[n], 16)

            def store_x(i, n):
                sp.wait_ge(silu_done, (i - Z2) * 2 + (n + 1))
                sp.dma_start(d.sT[bass.ds(i * 2 + (n - COLT), 1), :, 0:LC].rearrange("a p t -> (a p) t"),
                             y[:, n, 0, 0:LC]).then_inc(st_done[n], 16)

            nxt = lambda i, n: i * 2 + (n + 2)
            for a, b, store in ((0, H2, store_h), (H2, Z2, store_z), (Z2, S2 - 1, store_s)):
                with sp.Fori(a, b) as i:
                    pair(i, store, nxt)
            pair(S2 - 1, store_s, lambda i, n: HYT + ZT + n)
            with sp.Fori(S2, X2 - 1) as i:
                pair(i, store_x, lambda i, n: i * 2 + (n + 2 - COLT + HYT + ZT),
                     lambda i, n: COLT * NC4 + (i - S2) * 2 + (n + 1))
            pair(X2 - 1, store_x, None)
            for n in range(2):
                sp.wait_ge(st_done[n], 16 * X2)

        @block.tensor
        def _(pe):
            def products(out, n, at):
                for j in range(DT):
                    pe.matmul(out, wh[:, n, j, :], hh[:, j, at], start=(j == 0), stop=False)
                    pe.matmul(out, wh[:, n, j, :], hl[:, j, at], start=False, stop=False)
                    last = pe.matmul(out, wl[:, n, j, :], hh[:, j, at], start=False, stop=(j == DT - 1))
                last.then_inc(mm_done, 1)

            def tile(i, n, read=None, off=0):
                pe.wait_ge(wld, i * 2 + (n + 1))
                for c in range(NC4):
                    if read is not None:
                        pe.wait_ge(read, (i - 1 - off) * (2 * NC4) + (n * NC4 + c + 1))
                    elif n == 0:
                        pe.wait_ge(hld, c + 1)
                    products(acc[:, n, c, :], n, CHUNKS[c])

            for n in range(2):
                tile(0, n)
            for a, b, read, off in ((1, H2 + 1, bank_done, 0), (H2 + 1, Z2 + 1, z_done, H2),
                                    (Z2 + 1, S2, bank_done, Z2 - H2)):
                with pe.Fori(a, b) as i:
                    for n in range(2):
                        tile(i, n, read, off)
            pe.wait_ge(hld, NC4 + 1)
            with pe.Fori(S2, X2) as i:
                for n in range(2):
                    pe.wait_ge(wld, i * 2 + (n + 1))
                    pe.wait_ge(bank_done, (COLT - ZT) * NC4 + (i - S2) * 2 + (n - 1))
                    products(acc[:, n, 0, 0:LC], n, CHUNKS[NC4])

        @block.scalar
        def _(s):
            s.wait_ge(small_in, 128)

            def lead(n, h):
                s.wait_ge(w_in[n], h * 16 + 16)
                s.activation(wh[:, n], w[:, n], ACT.Copy).then_inc(whd, 1)

            def split(i, n):
                lead(1 - n, i + n)

            lead(0, 0)
            for at in CHUNKS:
                s.activation(hh[:, :, at], hT[:, :, at], ACT.Copy).then_inc(hhd, 1)

            def centre(i, n, first, skip=0):
                split(i, n)
                s.activation(mid[:, n, :], cw[:, 1:4:2, bass.ds(i * 2 + n, 1)], ACT.Copy).then_inc(mid_done, 1)
                s.wait_ge(mid_done, (i - skip) * 2 + (n + 1))
                if not first:
                    s.wait_ge(st_done[n], i * 16)
                for c in range(NC4):
                    s.wait_ge(mm_done, i * (2 * NC4) + (n * NC4 + c + 1))
                    s.activation(y[:, n, c, :], acc[:, n, c, :], ACT.Identity, bias=mid[:, n, 1:2],
                                 scale=mid[:, n, 0:1]).then_inc(act_done, 1)

            centre(0, 0, True)
            centre(0, 1, True)
            with s.Fori(1, H2) as i:
                for n in range(2):
                    centre(i, n, False)
            with s.Fori(H2, Z2) as i:
                for n in range(2):
                    split(i, n)
                    s.wait_ge(st_done[n], i * 16)
                    for c in range(NC4):
                        s.wait_ge(mm_done, i * (2 * NC4) + (n * NC4 + c + 1))
                        s.activation(y[:, n, c, :], acc[:, n, c, :], ACT.Silu).then_inc(z_done, 1)
            with s.Fori(Z2, S2) as i:
                for n in range(2):
                    centre(i, n, False, Z2 - H2)
                    s.wait_ge(bank_done, (i - (Z2 - H2)) * (2 * NC4) + (n + 1) * NC4)
                    s.activation(y[:, n], y[:, n], ACT.Silu).then_inc(silu_done, 1)

            def context(i, n, more=True):
                if more:
                    split(i, n)
                s.activation(mid[:, n, :], cw[:, 1:4:2, bass.ds(i * 2 + (n - COLT + HYT + ZT), 1)], ACT.Copy)\
                    .then_inc(mid_done, 1)
                s.wait_ge(mid_done, (i - (Z2 - H2)) * 2 + (n + 1))
                s.wait_ge(st_done[n], i * 16)
                s.wait_ge(mm_done, COLT * NC4 + (i - S2) * 2 + (n + 1))
                s.activation(y[:, n, 0, 0:LC], acc[:, n, 0, 0:LC], ACT.Identity, bias=mid[:, n, 1:2],
                             scale=mid[:, n, 0:1]).then_inc(act_done, 1)
                s.wait_ge(bank_done, (COLT - ZT) * NC4 + (i - S2) * 2 + (n + 1))
                s.activation(y[:, n, 0, 0:LC], y[:, n, 0, 0:LC], ACT.Silu).then_inc(silu_done, 1)

            with s.Fori(S2, X2 - 1) as i:
                for n in range(2):
                    context(i, n)
            for n in range(2):
                context(X2 - 1, n, n == 0)

        @block.vector
        def _(v):
            v.wait_ge(small_in, 128)

            def trail(n, k):
                v.wait_ge(whd, k + 1)
                v.tensor_tensor(wl[:, n], w[:, n], wh[:, n].bitcast(F32), ALU.subtract).then_inc(wld, 1)

            def split(i, n):
                trail(1 - n, i * 2 + (n + 1))

            trail(0, 0)
            for c, at in enumerate(CHUNKS):
                v.wait_ge(hhd, c + 1)
                v.tensor_tensor(hl[:, :, at], hT[:, :, at], hh[:, :, at].bitcast(F32), ALU.subtract)\
                    .then_inc(hld, 1)

            def taps(i, n, c, k, rows, width, act_at, conv_at):
                pv = acc[:, n, c, 0:rows * width].rearrange("p (r t) -> p r t", t=width)
                yv = y[:, n, c, 0:rows * width].rearrange("p (r t) -> p r t", t=width)
                v.wait_ge(act_done, act_at)
                v.scalar_tensor_tensor(out=yv[:, :, 1:], in0=pv[:, :, :-1], scalar=cw[:, 0, k], in1=yv[:, :, 1:],
                                       op0=ALU.mult, op1=ALU.add).then_inc(conv_step, 1)
                v.wait_ge(conv_step, conv_at)
                v.scalar_tensor_tensor(out=yv[:, :, :-1], in0=pv[:, :, 1:], scalar=cw[:, 2, k], in1=yv[:, :, :-1],
                                       op0=ALU.mult, op1=ALU.add).then_inc(bank_done, 1)

            def convolve(a, b, off):
                with v.Fori(a, b) as i:
                    for n in range(2):
                        split(i, n)
                        for c in range(NC4):
                            at = i * (2 * NC4) + (n * NC4 + c + 1 - off)
                            taps(i, n, c, bass.ds(i * 2 + n, 1), ROWS, GRID, at, at)

            convolve(0, H2, 0)
            with v.Fori(H2, Z2) as i:
                for n in range(2):
                    split(i, n)
            convolve(Z2, S2, (Z2 - H2) * 2 * NC4)
            base = (COLT - ZT) * NC4

            def context(i, n, more=True):
                if more:
                    split(i, n)
                at = (i - S2) * 2 + (n + 1 + base)
                taps(i, n, 0, bass.ds(i * 2 + (n - COLT + HYT + ZT), 1), 1, LC, at, at)

            with v.Fori(S2, X2 - 1) as i:
                for n in range(2):
                    context(i, n)
            for n in range(2):
                context(X2 - 1, n, n == 0)


def step_sizes(nc, d, hl, hh):
    NC5 = -(-TOK // BANK)
    NB = 2 * SSD_DT
    with ExitStack() as ctx:
        sb, ps, sem = pools(nc, ctx)
        w, wl, wh = sb("w_dt", [P, DT, NB]), sb("w_dt_lo", [P, DT, NB], F32R), sb("w_dt_hi", [P, DT, NB], F32R)
        dtb = sb("dt_bias_col", [NB, 1])
        alog = sb("a_log_row", [P, NB])
        arow = sb("a_row", [P, NB])
        dtT = sb("dt_T", [NB, TOK])
        ident = sb("ident2", [P, P])
        xr, ax, e, u, ln, dd, iz, r = [sb(f"sp_{n}", [P, NT * NB]) for n in ("x", "abs", "e", "u", "ln", "d", "z", "r")]
        dta = sb("dt_a", [P, 2, NT * NB])
        acc = ps("dt_ps", [NB, 2, BANK])
        xps = ps("dt_x_ps", [P, BANK])
        wdt_in, whd, wld, mm, ev, turned, xrd, arowd, axd, ed, ud, lnd, dtd, ad, out_done, chain = [
            sem(f"dt_{n}") for n in ("in", "wh", "wl", "mm", "ev", "tp", "xr", "arow", "ax", "e", "u", "ln", "dt",
                                     "a", "out", "chain")]
        block = ctx.enter_context(nc.Block())

        @block.sync
        def _(sp):
            with nc.allow_non_contiguous_dma(reason="16 columns of the projection"):
                sp.dma_start(w[:], d.w_in.rearrange("(j p) n -> p j n", p=P)[:, :, COLT * P:COLT * P + NB])\
                    .then_inc(wdt_in, 16)
            sp.dma_start(ident[:], d.ident).then_inc(wdt_in, 16)
            sp.dma_start(dtb[:], d.ssd_dt_bias.rearrange("a (h o) -> (a h) o", o=1)).then_inc(wdt_in, 16)
            sp.dma_start(alog[:], d.ssd_a_log.rearrange("(o a) h -> o (a h)", o=1).broadcast_to([P, NB]))\
                .then_inc(wdt_in, 16)
            sp.wait_ge(ad, 1)
            sp.dma_start(d.dt_a, dta[:].rearrange("p k (t h) -> p k t h", t=NT)).then_inc(out_done, 16)
            sp.wait_ge(out_done, 16)

        @block.tensor
        def _(pe):
            pe.wait_ge(wdt_in, 64)
            pe.wait_ge(wld, 1)
            for c in range(NC5):
                at = slice(c * BANK, min(TOK, (c + 1) * BANK))
                out = acc[:, c % 2, 0:at.stop - at.start]
                if c >= 2:
                    pe.wait_ge(ev, c - 1)
                for j in range(DT):
                    pe.matmul(out, wh[:, j, :], hh[:, j, at], start=(j == 0), stop=False)
                    pe.matmul(out, wh[:, j, :], hl[:, j, at], start=False, stop=False)
                    last = pe.matmul(out, wl[:, j, :], hh[:, j, at], start=False, stop=(j == DT - 1))
                last.then_inc(mm, 1)
            pe.wait_ge(ev, NC5)
            for t in range(NT):
                last = pe.transpose(xps[:, t * NB:(t + 1) * NB], dtT[:, t * P:(t + 1) * P], ident[0:NB, 0:NB])
            last.then_inc(turned, 1)

        @block.scalar
        def _(s):
            s.wait_ge(wdt_in, 64)
            s.activation(wh[:], w[:], ACT.Copy).then_inc(whd, 1)
            s.activation(arow[:], alog[:], ACT.Exp).then_inc(arowd, 1)
            s.wait_ge(xrd, 1)
            s.activation(ax[:], xr[:], ACT.Abs).then_inc(axd, 1)
            s.wait_ge(axd, 1)
            s.activation(e[:], ax[:], ACT.Exp, scale=-1.0).then_inc(ed, 1)
            s.wait_ge(ud, 1)
            s.activation(ln[:], u[:], ACT.Ln).then_inc(lnd, 1)

        @block.vector
        def _(v):
            v.wait_ge(wdt_in, 64)
            v.wait_ge(whd, 1)
            v.tensor_tensor(wl[:], w[:], wh[:].bitcast(F32), ALU.subtract).then_inc(wld, 1)
            for c in range(NC5):
                t0, t1 = c * BANK, min(TOK, (c + 1) * BANK)
                v.wait_ge(mm, c + 1)
                v.tensor_scalar(dtT[:, t0:t1], acc[:, c % 2, 0:t1 - t0], dtb[:, 0:1], None, ALU.add).then_inc(ev, 1)
            v.wait_ge(turned, 1)
            v.tensor_copy(xr[:], xps[:, 0:NT * NB]).then_inc(xrd, 1)
            v.wait_ge(ed, 1)
            v.tensor_scalar(u[:], e[:], 1.0, None, ALU.add).then_inc(ud, 1)
            v.wait_ge(ud, 1)
            st = Steps(v, chain)
            st.link(v.tensor_scalar(dd[:], u[:], -1.0, None, ALU.add))
            st.link(v.tensor_scalar(iz[:], dd[:], 0.0, None, ALU.is_equal))
            st.link(v.tensor_tensor(dd[:], dd[:], iz[:], ALU.add))
            st.link(v.reciprocal(r[:], dd[:]))
            v.wait_ge(lnd, 1)
            st.link(v.tensor_tensor(ln[:], ln[:], r[:], ALU.mult))
            st.link(v.tensor_tensor(ln[:], ln[:], iz[:], ALU.add))
            st.link(v.tensor_tensor(ln[:], ln[:], e[:], ALU.mult))
            v.wait_ge(xrd, 1)
            v.scalar_tensor_tensor(out=dta[:, 0, :], in0=xr[:], scalar=0.0, in1=ln[:], op0=ALU.max, op1=ALU.add)\
                .then_inc(dtd, 1)
            v.wait_ge(dtd, 1)
            v.wait_ge(arowd, 1)
            v.scalar_tensor_tensor(out=dta[:, 1, :].rearrange("p (t h) -> p t h", t=NT),
                                   in0=dta[:, 0, :].rearrange("p (t h) -> p t h", t=NT), scalar=-1.0,
                                   in1=arow[:].rearrange("p (o h) -> p o h", o=1).broadcast_to([P, NT, NB]),
                                   op0=ALU.mult, op1=ALU.mult).then_inc(ad, 1)


def hyena_filters(nc, d):
    NCH = L // BANK
    TWO_PI = 2 * math.pi
    C1 = 6.28125
    C2 = TWO_PI - C1
    MAGIC = 1.5 * 2.0 ** 23
    F2 = HID * 2
    with ExitStack() as ctx:
        sb, ps, sem = pools(nc, ctx)
        feats = sb("feats", [2 * EMB, L])
        w1 = sb("f_w1_diag", [2 * EMB, F2])
        w2 = sb("f_w2_diag", [F2, F2])
        w3 = sb("f_w3", [F2, ORDER, DH])
        cols = sb("f_cols", [F2, 3])
        fb = sb("f_fb", [F2, 2])
        h1 = sb("f_h1", [F2, L])
        h2 = sb("f_h2", [F2, L])
        x, k, r = sb("sin_x", [F2, 2, BANK]), sb("sin_k", [F2, BANK]), sb("sin_r", [F2, 2, BANK])
        tcol = sb("t_col", [P, N2])
        drow = sb("delta_row", [P, DH])
        win = sb("window", [P, 2, DH])
        stat = sb("h_stat", [F2, 2, P])
        blank = sb("blank", [P, D])
        f1 = sb("f1_sb", [P, 2, P])
        kf = sb("k_sb", [P, 2, ORDER, DH])
        tb = sb("tk_sb", [P, 2, ORDER, DH])
        kp = ps("k_ps", [P, 2, ORDER, DH])
        tp = ps("tk_ps", [P, 2, ORDER, DH])
        small_in, zeroed, pre = sem("hf_in"), sem("hf_zero"), sem("hf_pre")
        blanked, blank_out = sem("hf_blank"), sem("hf_blank_out")
        mm, sarg, sined = sem("hf_mm"), sem("hf_arg"), sem("hf_sin")
        f1_in = [sem("hf_f10"), sem("hf_f11")]
        st_out = [sem("hf_st0"), sem("hf_st1")]
        statd, kmm, wind, kfd, tmm, tev = (sem("hf_stat"), sem("hf_kmm"), sem("hf_win"), sem("hf_kf"), sem("hf_tmm"),
                                           sem("hf_tev"))
        step = sem("hf_step")
        block = ctx.enter_context(nc.Block())

        @block.gpsimd
        def _(g):
            g.memset(w1[:], 0.0).then_inc(zeroed, 1)
            g.memset(w2[:], 0.0).then_inc(zeroed, 1)
            g.memset(stat[:], 0.0).then_inc(zeroed, 1)
            g.memset(blank[:], 0.0).then_inc(blanked, 1)
            g.dma_start(feats[:], d.feats).then_inc(small_in, 16)
            g.wait_ge(zeroed, 3)
            for q in range(2):
                g.dma_start(w1[q * EMB:(q + 1) * EMB, q * HID:(q + 1) * HID], d.hy_f_w1).then_inc(small_in, 16)
                g.dma_start(w2[q * HID:(q + 1) * HID, q * HID:(q + 1) * HID], d.hy_f_w2).then_inc(small_in, 16)
                g.dma_start(w3[q * HID:(q + 1) * HID], d.hy_f_w3.rearrange("h (o q c) -> q h o c", o=ORDER, q=2)[q])\
                    .then_inc(small_in, 16)
                for n, a in enumerate((d.hy_f_b1, d.hy_f_b2, d.hy_f_freq)):
                    g.dma_start(cols[q * HID:(q + 1) * HID, n:n + 1], a.rearrange("(h o) -> h o", o=1))\
                        .then_inc(small_in, 16)
            g.dma_start(tcol[:], d.t_col).then_inc(small_in, 16)
            g.dma_start(drow[:], d.delta.rearrange("(o c) -> o c", o=1).broadcast_to([P, DH])).then_inc(small_in, 16)
            g.wait_ge(blanked, 1)
            g.dma_start(d.yb[NE * P:NBLK * P, :].rearrange("(p b) c -> p b c", p=P),
                        blank[:].unsqueeze(1).broadcast_to([P, NOV, D])).then_inc(blank_out, 16)
            g.wait_ge(blank_out, 16)

        @block.sync
        def _(sp):
            for n in range(2):
                sp.dma_start(f1[:, n], d.f1[n]).then_inc(f1_in[n], 16)
            with sp.Fori(0, N2 // 2 - 1) as i:
                for n in range(2):
                    sp.wait_ge(tmm, i * 2 + (n + 1))
                    sp.dma_start(f1[:, n], d.f1[bass.ds(i * 2 + (n + 2), 1)].rearrange("a p m -> (a p) m"))\
                        .then_inc(f1_in[n], 16)
                    sp.wait_ge(tev, i * 2 + (n + 1))
                    sp.dma_start(d.Tk[:, :, bass.ds(i * 2 + n, 1), :].rearrange("o p a c -> p o (a c)"), tb[:, n])\
                        .then_inc(st_out[n], 16)
            for n in range(2):
                sp.wait_ge(tev, N2 - 1 + n)
                sp.dma_start(d.Tk[:, :, N2 - 2 + n, :].rearrange("o p c -> p o c"), tb[:, n]).then_inc(st_out[n], 16)
            for n in range(2):
                sp.wait_ge(st_out[n], 16 * (N2 // 2))

        @block.tensor
        def _(pe):
            pe.wait_ge(small_in, 16 * 15)
            for c in range(NCH):
                if c >= 2:
                    pe.wait_ge(sarg, c - 1)
                pe.matmul(kp[:, c % 2, 0, :], w1[:], feats[:, c * BANK:(c + 1) * BANK], start=True, stop=True)\
                    .then_inc(mm, 1)
            for c in range(NCH):
                pe.wait_ge(sined, c + 1)
                pe.wait_ge(sarg, NCH + c - 1)
                pe.matmul(kp[:, c % 2, 0, :], w2[:], h1[:, c * BANK:(c + 1) * BANK], start=True, stop=True)\
                    .then_inc(mm, 1)
            with pe.Fori(0, N2 // 2) as i:
                for n in range(2):
                    pe.wait_ge(statd, i * 2 + (n + 1))
                    for o in range(ORDER):
                        last = pe.matmul(kp[:, n, o, :], stat[:, n], w3[:, o], start=True, stop=True)
                    last.then_inc(kmm, 1)
                for n in range(2):
                    pe.wait_ge(kfd, i * 2 + (n + 1))
                    pe.wait_ge(f1_in[n], i * 16 + 16)
                    for o in range(ORDER):
                        last = pe.matmul(tp[:, n, o, :], f1[:, n], kf[:, n, o], start=True, stop=True)
                    last.then_inc(tmm, 1)

        @block.vector
        def _(v):
            st = Steps(v, step)
            v.wait_ge(small_in, 16 * 15)
            for n in range(2):
                v.tensor_tensor(fb[:, n:n + 1], cols[:, n:n + 1], cols[:, 2:3], ALU.mult).then_inc(pre, 1)
            v.wait_ge(pre, 2)
            for q in range(2 * NCH):
                layer, c = q // NCH, q % NCH
                v.wait_ge(mm, q + 1)
                if q >= 2:
                    v.wait_ge(sined, q - 1)
                st.link(v.tensor_scalar(x[:, q % 2], kp[:, c % 2, 0, :], cols[:, 2:3], fb[:, layer:layer + 1],
                                        ALU.mult, ALU.add))
                st.link(v.tensor_scalar(k[:], x[:, q % 2], 1.0 / TWO_PI, MAGIC, ALU.mult, ALU.add))
                st.link(v.tensor_scalar(k[:], k[:], -MAGIC, None, ALU.add))
                st.link(v.scalar_tensor_tensor(out=r[:, q % 2], in0=k[:], scalar=-C1, in1=x[:, q % 2], op0=ALU.mult,
                                               op1=ALU.add))
                st.link(v.scalar_tensor_tensor(out=r[:, q % 2], in0=k[:], scalar=-C2, in1=r[:, q % 2], op0=ALU.mult,
                                               op1=ALU.add))
                v.tensor_scalar(r[:, q % 2], r[:, q % 2], 3.1415925, -3.1415925, ALU.min, ALU.max).then_inc(sarg, 1)
                v.wait_ge(sarg, q + 1)
            v.wait_ge(sined, 2 * NCH)
            v.memset(h2[HID:F2, 0:1], 0.0).then_inc(pre, 1)
            v.wait_ge(pre, 3)
            v.wait_ge(zeroed, 3)

            hv = h2[:].rearrange("p (a b) -> p a b", b=N2)

            def stationary(i, n, first):
                if not first:
                    v.wait_ge(kmm, i * 2 + (n - 1))
                v.tensor_copy(stat[0:HID, n, 0:HID], hv[0:HID, :, bass.ds(i * 2 + n, 1)]).then_inc(step, 1)
                v.tensor_copy(stat[HID:F2, n, HID:P], hv[HID:F2, :, bass.ds(i * 2 + n, 1)]).then_inc(statd, 1)

            def windowed(i, n, first):
                if not first:
                    v.wait_ge(tmm, i * 2 + (n - 1))
                v.wait_ge(kmm, i * 2 + (n + 1))
                v.wait_ge(wind, i * 2 + (n + 1))
                for o in range(ORDER):
                    last = v.tensor_tensor(kf[:, n, o], kp[:, n, o, :], win[:, n], ALU.mult)
                last.then_inc(kfd, 1)

            for n in range(2):
                stationary(0, n, True)
            for n in range(2):
                windowed(0, n, True)
            with v.Fori(1, N2 // 2) as i:
                for n in range(2):
                    stationary(i, n, False)
                for n in range(2):
                    windowed(i, n, False)

        @block.scalar
        def _(s):
            for q in range(2 * NCH):
                layer, c = q // NCH, q % NCH
                s.wait_ge(sarg, q + 1)
                s.activation((h1, h2)[layer][:, c * BANK:(c + 1) * BANK], r[:, q % 2], ACT.Sin).then_inc(sined, 1)

            def step_(i, n, first):
                if not first:
                    s.wait_ge(kfd, i * 2 + (n - 1))
                s.wait_ge(small_in, 16 * 15)
                s.activation(win[:, n], drow[:], ACT.Exp, scale=tcol[:, bass.ds(i * 2 + n, 1)]).then_inc(wind, 1)

            def evac(i, n, first):
                if not first:
                    s.wait_ge(st_out[n], i * 16)
                s.wait_ge(tmm, i * 2 + (n + 1))
                s.activation(tb[:, n], tp[:, n], ACT.Copy).then_inc(tev, 1)

            for n in range(2):
                step_(0, n, True)
            for n in range(2):
                evac(0, n, True)
            with s.Fori(1, N2 // 2) as i:
                for n in range(2):
                    step_(i, n, False)
                for n in range(2):
                    evac(i, n, False)


def hyena_forward(nc, d, z, tag):
    NPAIR = N2 // 2
    with ExitStack() as ctx:
        sb, ps, sem = pools(nc, ctx)
        ident = sb(f"ident_{tag}", [P, P])
        zc = sb(f"zc_{tag}", [P, 2, CT, 2, NB1])
        zs = sb(f"zs_{tag}", [P, 2, DH])
        f1 = sb(f"f1z_{tag}", [P, 2, P])
        tb = sb(f"tz_sb_{tag}", [P, 2, 2, DH])
        zt = ps(f"zt_ps_{tag}", [P, 2, DH])
        tp = ps(f"tz_ps_{tag}", [P, 2, 2, DH])
        small_in = sem(f"zf_in_{tag}")
        f1_in = [sem(f"zf_f10_{tag}"), sem(f"zf_f11_{tag}")]
        st_out = [sem(f"zf_st0_{tag}"), sem(f"zf_st1_{tag}")]
        picked, turned, zsd, tmm, tev = [sem(f"zf_{n}_{tag}") for n in ("pick", "turn", "zs", "mm", "ev")]
        block = ctx.enter_context(nc.Block())
        zv = z[:].rearrange("p c (a b) -> p c b a", b=N2)

        def pairs(eng, body):
            for n in range(2):
                body(n, n, 0, True)
            with eng.Fori(1, NPAIR // 2) as i:
                for n in range(2):
                    body(i * 2 + n, n, i, False)

        @block.sync
        def _(sp):
            sp.dma_start(ident[:], d.ident).then_inc(small_in, 16)

            def load(p, n):
                for k in range(2):
                    sp.dma_start(f1[k * NB1:(k + 1) * NB1, n],
                                 d.f1[bass.ds(p * 2 + k, 1), 0:NB1].rearrange("a p m -> (a p) m")).then_inc(f1_in[n], 16)

            def store(p, n):
                sp.wait_ge(tev, p + 1)
                sp.dma_start(d.Tz[:, bass.ds(p * 2, 2), :], tb[:, n]).then_inc(st_out[n], 16)

            for n in range(2):
                load(n, n)
            with sp.Fori(1, NPAIR // 2) as i:
                for n in range(2):
                    sp.wait_ge(tmm, i * 2 + (n - 1))
                    load(i * 2 + n, n)
                    store(i * 2 + (n - 2), n)
            for n in range(2):
                store(NPAIR - 2 + n, n)
            for n in range(2):
                sp.wait_ge(st_out[n], 16 * (NPAIR // 2))

        @block.scalar
        def _(s):
            def evac(p, n, h, first):
                s.wait_ge(tmm, p + 1)
                if not first:
                    s.wait_ge(st_out[n], h * 16)
                s.activation(tb[:, n], tp[:, n], ACT.Copy).then_inc(tev, 1)

            pairs(s, evac)

        @block.gpsimd
        def _(g):
            def pick(p, n, h, first):
                if not first:
                    g.wait_ge(turned, p - 1)
                for k in range(2):
                    last = g.tensor_copy(zc[:, n, :, k, :], zv[:, :, bass.ds(p * 2 + k, 1), :]
                                         .rearrange("p c o a -> p c (o a)"))
                last.then_inc(picked, 1)

            pairs(g, pick)

        @block.tensor
        def _(pe):
            pe.wait_ge(small_in, 16)

            def turn(p, n):
                pe.wait_ge(picked, p + 1)
                for c in range(CT):
                    last = pe.transpose(zt[:, n, c * P:(c + 1) * P], zc[:, n, c].rearrange("p a b -> p (a b)"), ident[:])
                last.then_inc(turned, 1)

            def stage(p, n, h, first):
                if first and n == 0:
                    turn(0, 0)
                turn(p + 1, 1 - n)
                pe.wait_ge(zsd, p + 1)
                pe.wait_ge(f1_in[n], h * 32 + 32)
                if not first:
                    pe.wait_ge(tev, p - 1)
                for k in range(2):
                    at = slice(k * NB1, (k + 1) * NB1)
                    last = pe.matmul(tp[:, n, k], f1[at, n], zs[at, n], start=True, stop=True)
                last.then_inc(tmm, 1)

            for n in range(2):
                stage(n, n, 0, True)
            with pe.Fori(1, NPAIR // 2 - 1) as i:
                for n in range(2):
                    stage(i * 2 + n, n, i, False)
            stage(NPAIR - 2, 0, NPAIR // 2 - 1, False)
            pe.wait_ge(zsd, NPAIR)
            pe.wait_ge(f1_in[1], 16 * NPAIR)
            pe.wait_ge(tev, NPAIR - 2)
            for k in range(2):
                at = slice(k * NB1, (k + 1) * NB1)
                last = pe.matmul(tp[:, 1, k], f1[at, 1], zs[at, 1], start=True, stop=True)
            last.then_inc(tmm, 1)

        @block.vector
        def _(v):
            def evac(p, n, h, first):
                v.wait_ge(turned, p + 1)
                if not first:
                    v.wait_ge(tmm, p - 1)
                v.tensor_copy(zs[:, n], zt[:, n]).then_inc(zsd, 1)

            pairs(v, evac)


def hyena_spectrum(nc, d, z, zb, gate, g1, o, tag):
    NS = N2 + 1
    NBUF = 4
    with ExitStack() as ctx:
        sb, ps, sem = pools(nc, ctx)
        m2 = sb(f"m2_{tag}", [P, 15, P])
        zi = sb(f"zi_{tag}", [P, NBUF, DH])
        ki = sb(f"ki_{tag}", [P, NBUF, DH])
        hb = sb(f"hb_{tag}", [P, CT])
        ks = sb(f"ks_{tag}", [P, 2, 2, DH])
        m = sb(f"prod_{tag}", [P, 2, 2, DH])
        pr = sb(f"spec_{tag}", [P, 2, DH])
        vb = sb(f"v_sb_{tag}", [P, 2, DH])
        za = ps(f"za_ps_{tag}", [P, 2, 2, DH])
        ka = ps(f"ka_ps_{tag}", [P, 2, DH])
        vp = ps(f"v_ps_{tag}", [P, 2, DH])
        m2_in = sem(f"sp_m2_{tag}")
        in_ = [sem(f"sp_in{n}_{tag}") for n in range(NBUF)]
        late_in, hb_in, zbd = sem(f"sp_late_{tag}"), sem(f"sp_hb_{tag}"), sem(f"sp_zb_{tag}")
        st_out = [sem(f"sp_st0_{tag}"), sem(f"sp_st1_{tag}")]
        fwd, kmm, ksd, mul, prd, inv, vev = [sem(f"sp_{n}_{tag}") for n in
                                             ("fwd", "kmm", "ks", "mul", "pr", "inv", "vev")]
        zt = d.Tz.rearrange("(b j) n c -> b (j n) c", j=4)
        kt = d.Tk[o].rearrange("(b j) n c -> b (j n) c", j=4)
        vt = d.V.rearrange("(b j) n c -> b (j n) c", j=4)
        block = ctx.enter_context(nc.Block())
        FIRST = NBUF + 1
        VAR = {0: (1, 0, P // 2), 1: (2, P // 2, P)}

        def loop(eng, body):
            with eng.Fori(1, NS // NBUF) as i:
                for k in range(1, NBUF + 1):
                    body(i * NBUF + k, k % 2, (i + k // NBUF, k % NBUF), None)

        def lead(body):
            for q in range(FIRST):
                body(q, q % 2, (q // NBUF, q % NBUF), q)

        @block.sync
        def _(sp):
            sp.dma_start(m2[:], d.m2).then_inc(m2_in, 16)

            def load(q, n, h, known):
                if known is None or known >= NBUF:
                    sp.wait_ge(kmm, q + (1 - NBUF))
                b = q - 1 if known is None else max(known - 1, 0)
                for t, src in ((zi, zt), (ki, kt)):
                    sp.dma_start(t[:, h[1]], src[bass.ds(b, 1)].rearrange("a p c -> (a p) c")).then_inc(in_[h[1]], 16)

            lead(load)
            if o == 0:
                sp.dma_start(g1[:], d.g1).then_inc(late_in, 16)
            sp.dma_start(gate[:], d.uT[CT * (o + 1):CT * (o + 2)].rearrange("c p t -> p c t")).then_inc(late_in, 16)
            loop(sp, load)
            sp.wait_ge(late_in, 32 if o == 0 else 16)

        @block.gpsimd
        def _(g):
            with nc.allow_non_contiguous_dma(reason="bias as columns"):
                g.dma_start(hb[:], d.hy_bias[o].rearrange("(j p) -> p j", p=P)).then_inc(hb_in, 16)

            def store(q, n, h, known):
                g.wait_ge(vev, q + 1)
                lo, hi = VAR[known][1:] if known in VAR else (0, P)
                b = q - 1 if known is None else max(known - 1, 0)
                g.dma_start(vt[bass.ds(b, 1), lo:hi].rearrange("a p c -> (a p) c"), vb[lo:hi, n])\
                    .then_inc(st_out[n], 16)

            lead(store)
            loop(g, store)
            g.wait_ge(st_out[0], 16 * (NS // 2 + 1))
            g.wait_ge(st_out[1], 16 * (NS // 2))

        @block.tensor
        def _(pe):
            pe.wait_ge(m2_in, 16)

            def forward(q, n, h, known):
                v = VAR[known][0] if known in VAR else 0
                pe.wait_ge(in_[h[1]], h[0] * 32 + 32)
                if known is None or known >= 2:
                    pe.wait_ge(mul, q - 1)
                for k in range(2):
                    last = pe.matmul(za[:, n, k], m2[:, v * 5 + k], zi[:, h[1]], start=True, stop=True)
                last.then_inc(fwd, 1)
                if known is None or known >= 1:
                    pe.wait_ge(ksd, q)
                for k in range(2):
                    last = pe.matmul(ka[:, k], m2[:, v * 5 + 2 + k], ki[:, h[1]], start=True, stop=True)
                last.then_inc(kmm, 1)

            def inverse(q, n, known):
                v = VAR[known][0] if known in VAR else 0
                pe.wait_ge(prd, q + 1)
                if known is None or known >= 2:
                    pe.wait_ge(vev, q - 1)
                pe.matmul(vp[:, n], m2[:, v * 5 + 4], pr[:, n], start=True, stop=True).then_inc(inv, 1)

            def both(q, n, h, known):
                forward(q, n, h, known)
                if known != 0:
                    inverse(q - 1, 1 - n, None if known is None else known - 1)

            lead(both)
            loop(pe, both)
            inverse(NS - 1, 0, None)

        @block.scalar
        def _(s):
            def filters(q, n, h, known):
                s.wait_ge(kmm, q + 1)
                if known is None or known >= 2:
                    s.wait_ge(mul, q - 1)
                s.activation(ks[:, n], ka[:], ACT.Copy).then_inc(ksd, 1)

            def evac(q, n, h, known):
                s.wait_ge(inv, q + 1)
                if known is None or known >= 2:
                    s.wait_ge(st_out[n], h * 16)
                s.activation(vb[:, n], vp[:, n], ACT.Copy).then_inc(vev, 1)

            def both(q, n, h, known):
                filters(q, n, h, known)
                if known != 0:
                    k = (h[1] - 1) % NBUF
                    earlier = h[0] * 2 + (k // 2 if h[1] else -1)
                    evac(q - 1, 1 - n, earlier, None if known is None else known - 1)

            lead(both)
            s.wait_ge(hb_in, 16)
            for c in range(CT):
                s.activation(zb[:, c], z[:, c], ACT.Copy, scale=hb[:, c:c + 1]).then_inc(zbd, 1)
            loop(s, both)
            evac(NS - 1, 0, NS // 2, None)
            s.wait_ge(zbd, CT)

        @block.vector
        def _(v):
            def product(q, n, h, known):
                v.wait_ge(fwd, q + 1)
                v.wait_ge(ksd, q + 1)
                v.tensor_tensor(m[:, n], za[:, n], ks[:, n], ALU.mult).then_inc(mul, 1)
                v.wait_ge(mul, q + 1)
                if known is None or known >= 2:
                    v.wait_ge(inv, q - 1)
                v.tensor_tensor(pr[:, n], m[:, n, 0], m[:, n, 1], ALU.add).then_inc(prd, 1)

            lead(product)
            loop(v, product)


def hyena_inverse(nc, d, z, zb, gate, g1, tag):
    with ExitStack() as ctx:
        sb, ps, sem = pools(nc, ctx)
        vi = sb(f"vi_{tag}", [P, 4, 2, DH])
        tmp = sb(f"y_tmp_{tag}", [P, 2, 2, CT, NB1])
        yp = ps(f"y_ps_{tag}", [P, 2, 2, CT, NB1])
        v_in = [sem(f"hi_v{n}_{tag}") for n in range(4)]
        mm, added, gated = [sem(f"hi_{n}_{tag}") for n in ("mm", "add", "gate_done")]
        ND = N2 // 2
        block = ctx.enter_context(nc.Block())

        @block.sync
        def _(sp):
            for k in range(4):
                sp.dma_start(vi[:, k], d.V[:, 2 * k:2 * k + 2, :]).then_inc(v_in[k], 16)
            with sp.Fori(1, ND // 4) as i:
                for k in range(4):
                    sp.wait_ge(mm, i * 4 + (k - 3))
                    sp.dma_start(vi[:, k], d.V[:, bass.ds(i * 8 + 2 * k, 2), :]).then_inc(v_in[k], 16)

        @block.tensor
        def _(pe):
            def pair(i, k, first):
                n = k % 2
                pe.wait_ge(v_in[k], i * 16 + 16)
                if not first or k >= 2:
                    pe.wait_ge(added, i * 4 + (k - 1))
                for a in range(2):
                    for c in range(CT):
                        last = pe.matmul(yp[:, n, a, c, :], vi[:, k, a, c * P:(c + 1) * P],
                                         g1[:, bass.ds(i * 8 + (2 * k + a), 1), :], start=True, stop=True)
                last.then_inc(mm, 1)

            for k in range(4):
                pair(0, k, True)
            with pe.Fori(1, ND // 4) as i:
                for k in range(4):
                    pair(i, k, False)

        @block.vector
        def _(v):
            zv, bv, gv = [t[:].rearrange("p c (a b) -> p c a b", b=N2) for t in (z, zb, gate)]
            with v.Fori(0, ND // 2) as i:
                for n in range(2):
                    v.wait_ge(mm, i * 2 + (n + 1))
                    for k in range(2):
                        last = v.tensor_tensor(tmp[:, n, k], yp[:, n, k], bv[:, :, :, bass.ds(i * 4 + (2 * n + k), 1)],
                                               ALU.add)
                    last.then_inc(added, 1)
                    v.wait_ge(added, i * 2 + (n + 1))
                    for k in range(2):
                        at = bass.ds(i * 4 + (2 * n + k), 1)
                        last = v.tensor_tensor(zv[:, :, :, at], tmp[:, n, k], gv[:, :, :, at], ALU.mult)
                    last.then_inc(gated, 1)
            v.wait_ge(gated, ND)


def hyena(nc, d):
    hyena_filters(nc, d)
    with ExitStack() as ctx:
        z, zb, gate = [ctx.enter_context(nc.sbuf_tensor(f"{n}_hy", [P, CT, L], F32)) for n in ("z", "zb", "gate")]
        g1 = ctx.enter_context(nc.sbuf_tensor("g1_hy", [P, N2, NB1], F32))
        move(nc, z[:], d.uT[0:CT].rearrange("c p t -> p c t"), "zin")
        for o in range(ORDER):
            hyena_forward(nc, d, z, f"a{o}")
            hyena_spectrum(nc, d, z, zb, gate, g1, o, f"b{o}")
            hyena_inverse(nc, d, z, zb, gate, g1, f"c{o}")
        move(nc, d.yT[0:CT].rearrange("c p t -> p c t"), z[:], "zout")


def move(nc, dst, src, tag):
    with ExitStack() as ctx:
        done = ctx.enter_context(nc.semaphore(f"moved_{tag}"))
        block = ctx.enter_context(nc.Block())

        @block.sync
        def _(sp):
            sp.dma_start(dst, src).then_inc(done, 16)
            sp.wait_ge(done, 16)


def ssd_weights(nc, d, dta, cum, wend, dec):
    NB = 2 * HEADS
    with ExitStack() as ctx:
        sb, ps, sem = pools(nc, ctx)
        tri = sb("tri", [P, 5, P])
        ident = sb("ident_w", [P, P])
        cT = sb("cum_T", [P, 3, P])
        cp = ps("cum_ps", [P, BANK])
        ep = ps("end_ps", [P, BANK])
        tp = ps("tot_ps", [P, BANK])
        ct = ps("cumT_ps", [P, 3, P])
        ins, mm, cumd, turned, wstep, out_done, evd = (sem("sw_in"), sem("sw_mm"), sem("sw_cum"), sem("sw_turn"),
                                                       sem("sw_step"), sem("sw_out"), sem("sw_ev"))
        block = ctx.enter_context(nc.Block())
        W = NT * NB

        @block.sync
        def _(sp):
            sp.dma_start(tri[:], d.tri).then_inc(ins, 16)
            sp.dma_start(ident[:], d.ident).then_inc(ins, 16)
            sp.dma_start(dta[:], d.dt_a).then_inc(ins, 16)
            sp.wait_ge(evd, 1)
            for k in range(3):
                rows = min(P, W - k * P)
                sp.dma_start(d.cumT[k * P:k * P + rows, :], cT[0:rows, k, :]).then_inc(out_done, 16)
            sp.wait_ge(out_done, 48)

        @block.tensor
        def _(pe):
            pe.wait_ge(ins, 48)
            av = dta[:, 1]
            for k, (acc, lo) in enumerate(((cp, 0), (cp, HEADS), (ep, 0), (ep, HEADS))):
                v = acc[:, 0:W].rearrange("p (t h) -> p t h", h=NB)[:, :, lo:lo + HEADS]
                pe.matmul(v, tri[:, k, :], av[:, :, lo:lo + HEADS], start=True, stop=True)
            pe.matmul(tp[:, 0:W], tri[:, 4, :], av.rearrange("p t h -> p (t h)"), start=True, stop=True).then_inc(mm, 1)
            pe.wait_ge(cumd, 1)
            for k in range(3):
                rows = min(P, W - k * P)
                last = pe.transpose(ct[0:rows, k, :], cum[:].rearrange("p t h -> p (t h)")[:, k * P:k * P + rows],
                                    ident[:])
            last.then_inc(turned, 1)

        @block.vector
        def _(v):
            v.wait_ge(mm, 1)
            v.tensor_copy(cum[:].rearrange("p t h -> p (t h)"), cp[:, 0:W]).then_inc(cumd, 1)
            v.wait_ge(wstep, 1)
            v.tensor_tensor(wend[:], wend[:], dta[:, 0], ALU.mult).then_inc(wstep, 1)
            v.wait_ge(turned, 1)
            v.tensor_copy(cT[:, 0:2], ct[:, 0:2])
            v.tensor_copy(cT[0:W - 2 * P, 2], ct[0:W - 2 * P, 2]).then_inc(evd, 1)

        @block.scalar
        def _(s):
            s.wait_ge(mm, 1)
            s.activation(dec[:].rearrange("p t h -> p (t h)"), tp[:, 0:W], ACT.Exp)
            s.activation(wend[:].rearrange("p t h -> p (t h)"), ep[:, 0:W], ACT.Exp).then_inc(wstep, 1)


def ssd_states(nc, d, H, dirn, wend, dec, lead, many, tag):
    N = len(lead) + (NTX if many else 0)
    W = D_SSD
    with ExitStack() as ctx:
        sb, ps, sem = pools(nc, ctx)
        ident = sb(f"ident_{tag}", [P, P])
        ch = sb(f"ch_{tag}", [P, 2, 6, P])
        bn = sb(f"bn_{tag}", [P, 2, 2 * P])
        xw = sb(f"xw_{tag}", [P, 2, W])
        th = sb(f"th_{tag}", [P, W])
        xp = ps(f"xp_{tag}", [P, 2, W])
        bp = ps(f"bp_{tag}", [P, 2, W])
        sp_ = ps(f"s_{tag}", [P, 2, W])
        small_in = sem(f"st_small_{tag}")
        in_ = [sem(f"st_in0_{tag}"), sem(f"st_in1_{tag}")]
        tp, bnd, xwd, smm, thd, hd = [sem(f"st_{n}_{tag}") for n in ("tp", "bn", "xw", "smm", "th", "h")]
        h_out = [sem(f"st_h0_{tag}"), sem(f"st_h1_{tag}")]
        block = ctx.enter_context(nc.Block())
        h0 = dirn * HEADS

        def run(eng, body):
            for k, c in enumerate(lead):
                body(k, k % 2, 0, c, False)
            if many:
                with eng.Fori(1, N // 2) as i:
                    for n in range(2):
                        body(i * 2 + n, n, i, eng.snap(i * -2 + (NT + 1 - n)), True)

        @block.sync
        def _(sp):
            sp.dma_start(ident[:], d.ident).then_inc(small_in, 16)
            src = d.sT.rearrange("j p t -> p j t")

            def step(k, n, h, c, many_):
                if many_:
                    sp.wait_ge(tp, k - 1)
                at = bass.ds(c * P, P)
                sp.dma_start(ch[:, n], src[:, 0:6, at]).then_inc(in_[n], 16)
                if many:
                    sp.wait_ge(hd, k + 1)
                    sp.dma_start(d.Hb[bass.ds(c, 1)].rearrange("a p w -> (a p) w"), H[:, n]).then_inc(h_out[n], 16)

            run(sp, step)
            if many:
                for n in range(2):
                    sp.wait_ge(h_out[n], 16 * (NT // 2))

        @block.tensor
        def _(pe):
            def step(k, n, h, c, many_):
                pe.wait_ge(in_[n], h * 16 + 16)
                if many_:
                    pe.wait_ge(xwd, k - 1)
                    pe.wait_ge(bnd, k - 1)
                pe.wait_ge(small_in, 16)
                for j in range(4):
                    pe.transpose(xp[:, n, j * P:(j + 1) * P], ch[:, n, j, :], ident[:])
                for j in range(2):
                    last = pe.transpose(bp[:, n, j * P:(j + 1) * P], ch[:, n, 4 + j, :], ident[:])
                last.then_inc(tp, 1)
                pe.wait_ge(xwd, k + 1)
                pe.wait_ge(bnd, k + 1)
                if many_:
                    pe.wait_ge(hd, k)
                for g in range(2):
                    last = pe.matmul(sp_[:, n, g * (W // 2):(g + 1) * (W // 2)], bn[:, n, g * P:(g + 1) * P],
                                     xw[:, n, g * (W // 2):(g + 1) * (W // 2)], start=True, stop=True)
                last.then_inc(smm, 1)

            run(pe, step)

        @block.scalar
        def _(s):
            def step(k, n, h, c, many_):
                s.wait_ge(tp, k + 1)
                if many_:
                    s.wait_ge(smm, k - 1)
                s.activation(bn[:, n], bp[:, n, 0:2 * P], ACT.Copy).then_inc(bnd, 1)

            run(s, step)

        @block.vector
        def _(v):
            v.memset(H[:, 0], 0.0).then_inc(hd, 1)

            def step(k, n, h, c, many_):
                v.wait_ge(tp, k + 1)
                if many_:
                    v.wait_ge(smm, k - 1)
                hs = [t[:, bass.ds(c, 1), h0:h0 + HEADS].rearrange("p a h -> p (a h)").unsqueeze(2)
                      .broadcast_to([P, HEADS, HD]) for t in (wend, dec)]
                v.tensor_tensor(xw[:, n].rearrange("p (h q) -> p h q", q=HD),
                                xp[:, n].rearrange("p (h q) -> p h q", q=HD), hs[0], ALU.mult).then_inc(xwd, 1)
                v.wait_ge(hd, k + 1)
                v.tensor_tensor(th[:].rearrange("p (h q) -> p h q", q=HD),
                                H[:, n].rearrange("p (h q) -> p h q", q=HD), hs[1], ALU.mult).then_inc(thd, 1)
                v.wait_ge(thd, k + 1)
                v.wait_ge(smm, k + 1)
                if many and (many_ or k > 0):
                    v.wait_ge(h_out[1 - n], (h + n) * 16)
                v.tensor_tensor(H[:, 1 - n], th[:], sp_[:, n], ALU.add).then_inc(hd, 1)

            run(v, step)


def ssd_main(nc, d, H, y, cum, wend, dec):
    W = D_SSD
    NB = 2 * HEADS
    NBUF = 4
    with ExitStack() as ctx:
        sb, ps, sem = pools(nc, ctx)
        ident = sb("ident_m", [P, P])
        mask = sb("mask_m", [P, 2, P])
        dta = sb("dta_m", [P, NT, NB])
        dsk = sb("dskip_m", [P, CT])
        ch = sb("ch_m", [P, NBUF, 8, P])
        zc = sb("z_m", [P, NBUF, CT, P])
        bc = sb("bc_m", [P, NBUF, NB, P])
        hb = sb("hb_m", [P, NBUF, W])
        xn, bn = sb("xn_m", [P, 2, W]), sb("bn_m", [P, 2, 2 * P])
        E = sb("E_m", [P, NB, P])
        Wt = sb("W_m", [P, 2, HEADS, P])
        eb = sb("eb_m", [P, NB, P])
        cs = sb("cs_m", [P, 2, NB, P])
        xw, th = sb("xw_m", [P, 2, W]), sb("th_m", [P, W])
        yt = sb("yt_m", [P, CT, P])
        xp = ps("xp_m", [P, 2, W])
        bp = ps("bp_m", [P, W])
        cbp = ps("cb_m", [P, 2, W])
        s_ps = ps("s_m", [P, W])
        yp = ps("yp_m", [P, 2, CT, P])
        small_in, dsk_in = sem("sm_small"), sem("sm_dsk")
        in_ = [sem(f"sm_in{n}") for n in range(NBUF)]
        tp, xnd, bnd, segd, expd, ebd, csd, xwd, smm, hd, wd, ymm, ytd, yd, vstep = [
            sem(f"sm_{n}") for n in ("tp", "xn", "bn", "seg", "exp", "eb", "cs", "xw", "smm", "h", "w", "ymm", "yt", "y",
                                     "step")]
        block = ctx.enter_context(nc.Block())

        def chunks(eng, body):
            for k in range(NBUF):
                body(k, k % 2, (0, k), k < 2)
            with eng.Fori(1, NTX // NBUF) as i:
                for k in range(NBUF):
                    body(i * NBUF + k, k % 2, (i, k), False)

        @block.sync
        def _(sp):
            sp.dma_start(ident[:], d.ident).then_inc(small_in, 16)
            sp.dma_start(mask[:], d.mask).then_inc(small_in, 16)
            sp.dma_start(dta[:], d.dt_a[:, 0]).then_inc(small_in, 16)

            def step(k, n, h, first):
                h, b = h
                if not isinstance(k, int) or k >= NBUF:
                    sp.wait_ge(yd, k + (1 - NBUF))
                    sp.wait_ge(csd, k + (1 - NBUF))
                    sp.wait_ge(segd, k + (1 - NBUF))
                sp.dma_start(ch[:, b], d.sT.rearrange("j p t -> p j t")[:, :, bass.ds(LC + k * P, P)])\
                    .then_inc(in_[b], 16)
                sp.dma_start(zc[:, b], d.zT.rearrange("j p t -> p j t")[:, :, bass.ds(k * P, P)]).then_inc(in_[b], 16)
                sp.dma_start(bc[:, b].rearrange("p a b -> p (a b)"),
                             d.cumT[bass.ds((k + NTC) * NB, NB), :].rearrange("(o a) b -> o (a b)", o=1)
                             .broadcast_to([P, NB * P])).then_inc(in_[b], 16)
                sp.dma_start(hb[:, b], d.Hb[bass.ds(k + NTC, 1)].rearrange("a p w -> (a p) w")).then_inc(in_[b], 16)

            chunks(sp, step)

        @block.gpsimd
        def _(g):
            for c in range(CT):
                for a in range(2):
                    g.dma_start(dsk[a * HD:(a + 1) * HD, c:c + 1],
                                d.ssd_d[2 * c + a:2 * c + a + 1].rearrange("(o a) -> o a", o=1).broadcast_to([HD, 1]))\
                        .then_inc(dsk_in, 16)

            def step(k, n, h, first):
                g.wait_ge(ebd, k + 1)
                if not first:
                    g.wait_ge(ymm, k - 1)
                cv = cs[:, n].rearrange("p (v h) t -> p v h t", v=2)
                ev = eb[:].rearrange("p (v h) t -> p v h t", v=2)
                for q in range(2):
                    hs = slice(q * HPG, (q + 1) * HPG)
                    c_ = ch[:, h[1], 6 + q, :].unsqueeze(1).unsqueeze(1).broadcast_to([P, 2, HPG, P])
                    last = g.tensor_tensor(cv[:, :, hs, :], ev[:, :, hs, :], c_, ALU.mult)
                last.then_inc(csd, 1)

            chunks(g, step)

        @block.tensor
        def _(pe):
            pe.wait_ge(small_in, 16 * 3)

            def turn(k, n, h, first):
                pe.wait_ge(in_[h[1]], h[0] * 64 + 64)
                if not first:
                    pe.wait_ge(xnd, k - 1)
                    pe.wait_ge(wd, k - 1)
                if not first or k > 0:
                    pe.wait_ge(bnd, k)
                pe.wait_ge(small_in, 16 * 3)
                for j in range(4):
                    pe.transpose(xp[:, n, j * P:(j + 1) * P], ch[:, h[1], j, :], ident[:])
                for j in range(2):
                    pe.transpose(bp[:, j * P:(j + 1) * P], ch[:, h[1], 4 + j, :], ident[:])
                for j in range(2):
                    last = pe.matmul(cbp[:, n, j * P:(j + 1) * P], ch[:, h[1], 4 + j, :], ch[:, h[1], 6 + j, :],
                                     start=True, stop=True)
                last.then_inc(tp, 1)

            def out(k, n, b, first):
                pe.wait_ge(wd, k + 1)
                pe.wait_ge(csd, k + 1)
                pe.wait_ge(xnd, k + 1)
                pe.wait_ge(hd, k + 1)
                if not first:
                    pe.wait_ge(ytd, k)
                for a in range(HEADS):
                    dst = yp[(a % 2) * HD:(a % 2 + 1) * HD, n, a // 2, :]
                    hs = slice(a * HD, (a + 1) * HD)
                    pe.matmul(dst, xn[:, n, hs], Wt[:, n, a, :], start=True, stop=False, skip_group_check=True)
                    pe.matmul(dst, H[:, n, hs], cs[:, n, a, :], start=False, stop=False, skip_group_check=True)
                    last = pe.matmul(dst, hb[:, b, hs], cs[:, n, HEADS + a, :], start=False, stop=True,
                                     skip_group_check=True)
                last.then_inc(ymm, 1)

            def states(k, n):
                pe.wait_ge(xwd, k + 1)
                pe.wait_ge(bnd, k + 1)
                pe.wait_ge(hd, k + 1)
                for g in range(2):
                    hs = slice(g * (W // 2), (g + 1) * (W // 2))
                    last = pe.matmul(s_ps[:, hs], bn[:, n, g * P:(g + 1) * P], xw[:, n, hs], start=True, stop=True)
                last.then_inc(smm, 1)

            def step(k, n, h, first):
                turn(k, n, h, first)
                if not isinstance(k, int) or k:
                    out(k - 1, 1 - n, (h[1] - 1) % NBUF, isinstance(k, int) and k == 1)
                states(k, n)

            chunks(pe, step)
            out(NTX - 1, 1, NBUF - 1, False)

        @block.scalar
        def _(s):
            def step(k, n, h, first):
                s.wait_ge(in_[h[1]], h[0] * 64 + 64)
                if not first:
                    s.wait_ge(csd, k)
                elif k > 0:
                    s.wait_ge(csd, k)
                s.activation(eb[:], bc[:, h[1]], ACT.Exp).then_inc(ebd, 1)
                s.wait_ge(tp, k + 1)
                if not first:
                    s.wait_ge(ymm, k - 1)
                s.activation(xn[:, n], xp[:, n], ACT.Copy).then_inc(xnd, 1)
                if not first:
                    s.wait_ge(smm, k - 1)
                s.activation(bn[:, n], bp[:, 0:2 * P], ACT.Copy).then_inc(bnd, 1)
                s.wait_ge(segd, k + 1)
                s.activation(E[:], E[:], ACT.Exp).then_inc(expd, 1)

            chunks(s, step)

        @block.vector
        def _(v):
            v.wait_ge(small_in, 16 * 3)
            v.wait_ge(dsk_in, 16 * 2 * CT)

            def spread(t, k, lo, inner):
                return t[:, bass.ds(k + NTC, 1), lo:lo + HEADS].rearrange("p a h -> p (a h)").unsqueeze(2)\
                    .broadcast_to([P, HEADS, inner])

            def post(k, n, b, first):
                v.wait_ge(ymm, k + 1)
                if not first:
                    v.wait_ge(yd, k)
                for c in range(CT):
                    last = v.scalar_tensor_tensor(out=yt[:, c, :], in0=ch[:, b, c, :], scalar=dsk[:, c:c + 1],
                                                  in1=yp[:, n, c, :], op0=ALU.mult, op1=ALU.add)
                last.then_inc(ytd, 1)
                v.wait_ge(ytd, k + 1)
                v.tensor_tensor(y[:, :, bass.ds(k * P, P)], yt[:], zc[:, b], ALU.mult).then_inc(yd, 1)

            def step(k, n, h, first):
                v.wait_ge(in_[h[1]], h[0] * 64 + 64)
                if first is False or k:
                    v.wait_ge(wd, k)
                for a in range(NB):
                    last = v.scalar_tensor_tensor(out=E[:, a, :], in0=bc[:, h[1], a, :],
                                                  scalar=cum[:, bass.ds(k + NTC, 1), a], in1=mask[:, a // HEADS, :],
                                                  op0=ALU.subtract, op1=ALU.min)
                last.then_inc(segd, 1)
                v.wait_ge(xnd, k + 1)
                if not first:
                    v.wait_ge(smm, k - 1)
                v.tensor_tensor(xw[:, n].rearrange("p (h q) -> p h q", q=HD),
                                xn[:, n].rearrange("p (h q) -> p h q", q=HD), spread(wend, k, 0, HD), ALU.mult)\
                    .then_inc(xwd, 1)
                v.wait_ge(hd, k + 1)
                v.tensor_tensor(th[:].rearrange("p (h q) -> p h q", q=HD),
                                H[:, n].rearrange("p (h q) -> p h q", q=HD), spread(dec, k, 0, HD), ALU.mult)\
                    .then_inc(vstep, 1)
                v.wait_ge(expd, k + 1)
                for q in range(2):
                    last = v.tensor_tensor(E[:, q * HEADS:(q + 1) * HEADS, :], E[:, q * HEADS:(q + 1) * HEADS, :],
                                           spread(dta, k, q * HEADS, P), ALU.mult)
                last.then_inc(vstep, 1)
                v.wait_ge(vstep, k * 3 + 2)
                v.tensor_tensor(E[:, 0:HEADS, :], E[:, 0:HEADS, :], E[:, HEADS:NB, :], ALU.add).then_inc(vstep, 1)
                v.wait_ge(vstep, k * 3 + 3)
                if not first:
                    v.wait_ge(ymm, k - 1)
                for g in range(2):
                    hs = slice(g * HPG, (g + 1) * HPG)
                    cb = cbp[:, n, g * P:(g + 1) * P].unsqueeze(1).broadcast_to([P, HPG, P])
                    last = v.tensor_tensor(Wt[:, n, hs, :], E[:, hs, :], cb, ALU.mult)
                last.then_inc(wd, 1)

            def update(k, n):
                v.wait_ge(smm, k + 1)
                v.tensor_tensor(H[:, 1 - n], th[:], s_ps[:], ALU.add).then_inc(hd, 1)

            def both(k, n, h, first):
                step(k, n, h, first)
                if not isinstance(k, int) or k:
                    post(k - 1, 1 - n, (h[1] - 1) % NBUF, isinstance(k, int) and k == 1)
                update(k, n)

            v.sem_inc(hd, 1)
            chunks(v, both)
            post(NTX - 1, 1, NBUF - 1, False)
            v.wait_ge(yd, NTX)


def ssd_norm(nc, d, y):
    with ExitStack() as ctx:
        sb, ps, sem = pools(nc, ctx)
        ones = sb("ones_n", [P, P])
        gn = sb("gn_n", [P, CT])
        sq = sb("sq_n", [P, 2, CT, BANK])
        ms = sb("ms_n", [P, 2, 2, BANK])
        rs = sb("rs_n", [P, 2, 2, BANK])
        acc = ps("acc_n", [P, 2, 2, BANK])
        small_in, sqd, mm, msd, rtd, rcd, yd, out_done = [
            sem(f"sn_{n}") for n in ("in", "sq", "mm", "ms", "rt", "rc", "y", "out")]
        NC4 = L // BANK
        block = ctx.enter_context(nc.Block())

        @block.sync
        def _(sp):
            sp.dma_start(ones[:], d.tri[:, 4, :]).then_inc(small_in, 16)
            with nc.allow_non_contiguous_dma(reason="norm weight as columns"):
                sp.dma_start(gn[:], d.ssd_norm_g.rearrange("(j p) -> p j", p=P)).then_inc(small_in, 16)
            for c in range(NC4):
                sp.wait_ge(yd, c + 1)
                at = slice(c * BANK, (c + 1) * BANK)
                sp.dma_start(d.yT[CT:2 * CT, :, at].rearrange("j p t -> p j t"), y[:, :, at]).then_inc(out_done, 16)
            sp.wait_ge(out_done, 16 * NC4)

        @block.scalar
        def _(s):
            for c in range(NC4):
                if c >= 2:
                    s.wait_ge(mm, c - 1)
                s.activation(sq[:, c % 2], y[:, :, c * BANK:(c + 1) * BANK], ACT.Square).then_inc(sqd, 1)
            for c in range(NC4):
                s.wait_ge(msd, c + 1)
                s.activation(rs[:, c % 2], ms[:, c % 2], ACT.Sqrt).then_inc(rtd, 1)

        @block.tensor
        def _(pe):
            pe.wait_ge(small_in, 32)
            for c in range(NC4):
                pe.wait_ge(sqd, c + 1)
                if c >= 2:
                    pe.wait_ge(msd, c - 1)
                for g in range(2):
                    for j in range(2):
                        last = pe.matmul(acc[:, c % 2, g], ones[:], sq[:, c % 2, 2 * g + j], start=(j == 0), stop=(j == 1))
                last.then_inc(mm, 1)

        @block.vector
        def _(v):
            v.wait_ge(small_in, 32)
            for c in range(NC4):
                n = c % 2
                v.wait_ge(mm, c + 1)
                v.tensor_scalar(ms[:, n], acc[:, n], 2.0 / D_SSD, EPS, ALU.mult, ALU.add).then_inc(msd, 1)
                v.wait_ge(rtd, c + 1)
                v.reciprocal(rs[:, n], rs[:, n]).then_inc(rcd, 1)
                v.wait_ge(rcd, c + 1)
                for j in range(CT):
                    yv = y[:, j, c * BANK:(c + 1) * BANK]
                    last = v.scalar_tensor_tensor(out=yv, in0=yv, scalar=gn[:, j:j + 1], in1=rs[:, n, j // 2],
                                                  op0=ALU.mult, op1=ALU.mult)
                last.then_inc(yd, 1)


def ssd(nc, d):
    NB = 2 * HEADS
    with ExitStack() as ctx:
        sb, _, _ = pools(nc, ctx)
        cum, wend, dec = sb("cum", [P, NT, NB]), sb("wend", [P, NT, NB]), sb("dec", [P, NT, NB])
        H = sb("H_state", [P, 2, D_SSD])
        y = sb("y_ssd", [P, CT, L])
        with ExitStack() as inner:
            dta = inner.enter_context(nc.sbuf_tensor("dta_w", [P, 2, NT, NB], F32))
            ssd_weights(nc, d, dta, cum, wend, dec)
        ssd_states(nc, d, H, 1, wend, dec, [1, 0], True, "bwd")
        ssd_states(nc, d, H, 0, wend, dec, [0, 1], False, "fwd")
        ssd_main(nc, d, H, y, cum, wend, dec)
        ssd_norm(nc, d, y)


def out_proj(nc, d, logits):
    NR = MG + NE
    with ExitStack() as ctx:
        sb, ps, sem = pools(nc, ctx)
        wo = sb("w_out_sb", [P, DT, D])
        wr = sb("w_router", [P, DT, NR])
        br = sb("b_router", [P, NR])
        ga, gs, sh = sb("gate1_row", [P, D]), sb("gs2_row", [P, D]), sb("sh2_row", [P, D])
        g2 = sb("g2_row", [P, D])
        ident = sb("ident_o", [P, P])
        yk = sb("yk", [P, 2, DT, P])
        x = sb("x_o", [P, 2, D])
        t1, x1, h, sq = sb("t_o", [P, D]), sb("x1_o", [P, 2, D]), sb("h2_o", [P, 2, D]), sb("sq_o", [P, D])
        ms, rt, rs = sb("ms_o", [P, 2]), sb("rt_o", [P, 2]), sb("rs_o", [P, 2])
        hT = sb("hT_o", [P, 2, DT, P])
        op = ps("o_ps", [P, 2, 2, BANK])
        tp = ps("h_tp", [P, 2, BANK])
        rp = ps("r_ps", [P, BANK])
        wo_in, row_in, row_done = sem("op_wo"), sem("op_row"), sem("op_rowd")
        in_ = [sem("op_in0"), sem("op_in1")]
        x1_out = [sem("op_x10"), sem("op_x11")]
        h_out = [sem("op_h0"), sem("op_h1")]
        mm, gated, x1d, ssd_, msd, rtd, rsd, nd, hd, h2d, tpd, hTd, rmm, lgd = [
            sem(f"op_{n}") for n in ("mm", "gated", "x1", "ss", "ms", "rt", "rs", "n", "hm", "h", "tp", "hT", "rmm",
                                     "lg")]
        block = ctx.enter_context(nc.Block())

        def tiles(eng, body):
            for n in range(2):
                body(n, n, 0, True)
            with eng.Fori(1, NTX // 2) as i:
                for n in range(2):
                    body(i * 2 + n, n, i, False)

        @block.gpsimd
        def _(g):
            row = lambda a: a.rearrange("(o n) -> o n", o=1)
            for dst, src in ((ga, d.mod[0, 2 * D:3 * D]), (sh, d.mod[0, 3 * D:4 * D]), (gs, d.mod[0, 4 * D:5 * D]),
                             (g2, d.g_norm2)):
                g.dma_start(dst[:], row(src).broadcast_to([P, D])).then_inc(row_in, 16)
            g.dma_start(br[:, 0:MG], row(d.b_group).broadcast_to([P, MG])).then_inc(row_in, 16)
            g.dma_start(br[:, MG:NR], row(d.b_expert).broadcast_to([P, NE])).then_inc(row_in, 16)
            g.dma_start(ident[:], d.ident).then_inc(row_in, 16)
            g.dma_start(wr[:, :, 0:MG], d.w_group.rearrange("(j p) n -> p j n", p=P)).then_inc(row_in, 16)
            g.dma_start(wr[:, :, MG:NR], d.w_expert.rearrange("(j p) n -> p j n", p=P)).then_inc(row_in, 16)

        @block.sync
        def _(sp):
            yv = d.yT.rearrange("j p t -> p j t")

            def load(t, n, h_, first):
                if not first:
                    sp.wait_ge(mm, t - 1)
                    sp.wait_ge(x1d, t - 1)
                at = bass.ds(t * P, P)
                sp.dma_start(yk[:, n], yv[:, :, at]).then_inc(in_[n], 16)
                sp.dma_start(x[:, n], d.x[at, :]).then_inc(in_[n], 16)

            def store(t, n):
                at = bass.ds(t * P, P)
                sp.wait_ge(x1d, t + 1)
                sp.dma_start(d.x1[at, :], x1[:, n]).then_inc(x1_out[n], 16)
                sp.wait_ge(h2d, t + 1)
                sp.dma_start(d.h2[at, :], h[:, n]).then_inc(h_out[n], 16)

            load(0, 0, 0, True)
            sp.dma_start(wo[:, 0:DT // 2], d.w_out.rearrange("(j p) n -> p j n", p=P)[:, 0:DT // 2]).then_inc(wo_in, 16)
            sp.dma_start(wo[:, DT // 2:], d.w_out.rearrange("(j p) n -> p j n", p=P)[:, DT // 2:]).then_inc(wo_in, 16)
            load(1, 1, 0, True)
            with sp.Fori(1, NTX // 2) as i:
                for n in range(2):
                    load(i * 2 + n, n, i, False)
                    store(i * 2 + (n - 2), n)
            for n in range(2):
                store(NTX - 2 + n, n)
            for n in range(2):
                sp.wait_ge(x1_out[n], 16 * (NTX // 2))
                sp.wait_ge(h_out[n], 16 * (NTX // 2))

        @block.tensor
        def _(pe):
            pe.wait_ge(wo_in, 32)
            pe.wait_ge(row_in, 16 * 9)

            def project(t, n, h_, first):
                pe.wait_ge(in_[n], h_ * 32 + 32)
                if not first:
                    pe.wait_ge(gated, t - 1)
                for c in range(2):
                    for j in range(DT):
                        last = pe.matmul(op[:, n, c], yk[:, n, j], wo[:, j, c * BANK:(c + 1) * BANK], start=(j == 0),
                                         stop=(j == DT - 1))
                last.then_inc(mm, 1)

            def route(t, n, first):
                pe.wait_ge(h2d, t + 1)
                if not first:
                    pe.wait_ge(hTd, t)
                pe.wait_ge(wo_in, 32)
                for j in range(DT):
                    last = pe.transpose(tp[:, j // 4, (j % 4) * P:(j % 4 + 1) * P], h[:, n, j * P:(j + 1) * P], ident[:])
                last.then_inc(tpd, 1)
                pe.wait_ge(hTd, t + 1)
                if not first:
                    pe.wait_ge(lgd, t)
                for j in range(DT):
                    last = pe.matmul(rp[:, 0:NR], hT[:, n, j], wr[:, j], start=(j == 0), stop=(j == DT - 1))
                last.then_inc(rmm, 1)

            project(0, 0, 0, True)
            project(1, 1, 0, True)
            route(0, 0, True)
            with pe.Fori(1, NTX // 2) as i:
                for n in range(2):
                    project(i * 2 + n, n, i, False)
                    route(i * 2 + (n - 1), 1 - n, False)
            route(NTX - 1, 1, False)

        @block.scalar
        def _(s):
            def step(t, n, h_, first):
                s.wait_ge(x1d, t + 1)
                if not first or n:
                    s.wait_ge(ssd_, t)
                s.activation(sq[:], x1[:, n], ACT.Square, accum_out=ms[:, n:n + 1]).then_inc(ssd_, 1)
                s.wait_ge(msd, t + 1)
                s.activation(rt[:, n:n + 1], ms[:, n:n + 1], ACT.Sqrt).then_inc(rtd, 1)
                s.wait_ge(tpd, t + 1)
                s.activation(hT[:, n].rearrange("p j t -> p (j t)"), tp[:].rearrange("p a b -> p (a b)"), ACT.Copy)\
                    .then_inc(hTd, 1)

            tiles(s, step)

        @block.vector
        def _(v):
            v.wait_ge(row_in, 16 * 9)
            v.scalar_tensor_tensor(out=gs[:], in0=gs[:], scalar=1.0, in1=g2[:], op0=ALU.add, op1=ALU.mult)\
                .then_inc(row_done, 1)

            def step(t, n, h_, first):
                v.wait_ge(mm, t + 1)
                if not first or n:
                    v.wait_ge(x1d, t)
                v.tensor_tensor(t1[:], op[:, n].rearrange("p a b -> p (a b)"), ga[:], ALU.mult).then_inc(gated, 1)
                v.wait_ge(gated, t + 1)
                if not first:
                    v.wait_ge(x1_out[n], h_ * 16)
                    v.wait_ge(nd, t - 1)
                    v.wait_ge(ssd_, t - 1)
                v.tensor_tensor(x1[:, n], t1[:], x[:, n], ALU.add).then_inc(x1d, 1)
                v.wait_ge(ssd_, t + 1)
                v.tensor_scalar(ms[:, n:n + 1], ms[:, n:n + 1], 1.0 / D, EPS, ALU.mult, ALU.add).then_inc(msd, 1)
                v.wait_ge(rtd, t + 1)
                v.reciprocal(rs[:, n:n + 1], rt[:, n:n + 1]).then_inc(rsd, 1)
                v.wait_ge(rsd, t + 1)
                v.wait_ge(row_done, 1)
                if not first:
                    v.wait_ge(h_out[n], h_ * 16)
                    v.wait_ge(tpd, t - 1)
                v.scalar_tensor_tensor(out=h[:, n], in0=x1[:, n], scalar=rs[:, n:n + 1], in1=gs[:], op0=ALU.mult,
                                       op1=ALU.mult).then_inc(nd, 1)
                v.wait_ge(nd, t + 1)
                v.tensor_tensor(h[:, n], h[:, n], sh[:], ALU.add).then_inc(h2d, 1)
                v.wait_ge(rmm, t + 1)
                v.tensor_tensor(logits[:, bass.ds(t, 1), :].rearrange("p a e -> p (a e)"), rp[:, 0:NR], br[:], ALU.add)\
                    .then_inc(lgd, 1)

            tiles(v, step)
            v.wait_ge(lgd, NTX)


def dispatch(nc, d, logits, gates, slots, blocks):
    T = NTX
    with ExitStack() as ctx:
        sb, ps, sem = pools(nc, ctx)
        tri = sb("tri_d", [P, 5, P])
        iot = sb("iota_d", [P, NE])
        mul = sb("mult_d", [P, MAXB])
        desc = sb("desc_d", [P, EPG])
        tok = sb("tok_d", [P, T], I32)
        zero = sb("zero_d", [P, NBLK], I32)
        s1 = [sb(f"s1_{n}", [P, T, 1]) for n in range(8)]
        m1, den, pg, mv, a1, a2, w1, w2 = s1
        gd, v8, oh, ing, o1, o2, u8 = [sb(f"s8_{n}", [P, T, EPG]) for n in range(7)]
        big = sb("big_d", [P, T, MG, EPG])
        E1, E2, Es = [sb(f"E_{n}", [P, T, NE]) for n in range(3)]
        run = sb("run_d", [P, T + 1, NE])
        cnt, nov, incl, excl, one = [sb(f"c_{n}", [P, NE]) for n in range(5)]
        cb = sb("cmp_d", [P, NE, MAXB])
        r_, e_, o_, q_, b_, f_ = [sb(f"k_{n}", [P, 2, T]) for n in range(6)]
        cq = sb("cmpq_d", [P, T, MAXB])
        idx = sb("idx_d", [P, 2, T], I32)
        ob = sb("ob_d", [1, NOV, NE])
        ov = sb("ov_d", [1, NOV])
        rank = ps("rank_ps", [P, T, NE])
        cps = ps("cnt_ps", [P, NE])
        small_in, z_out, sc_out, tbl_in, tokd = sem("di_in"), sem("di_z"), sem("di_sc"), sem("di_tbl"), sem("di_tok")
        step, gexp, dexp, eready, rmm, idxd, zd, b_in = [sem(f"di_{n}") for n in
                                                         ("step", "gexp", "dexp", "E", "rmm", "idx", "zero", "bin")]
        subd = sem("di_sub")
        block = ctx.enter_context(nc.Block())

        @block.sync
        def _(sp):
            sp.dma_start(tri[:], d.tri).then_inc(small_in, 16)
            for dst, src in ((iot, d.iota), (mul, d.mult), (desc, d.desc)):
                sp.dma_start(dst[:], src.rearrange("(o n) -> o n", o=1).broadcast_to([P, src.shape[0]]))\
                    .then_inc(small_in, 16)
            sp.dma_start(blocks[0:1, 0:NE], d.i_own.rearrange("(o n) -> o n", o=1)).then_inc(b_in, 16)
            sp.wait_ge(b_in, 16)

        @block.gpsimd
        def _(g):
            g.memset(zero[:], 0).then_inc(zd, 1)
            g.iota(tok[:], pattern=[[P, T]], base=0, channel_multiplier=1).then_inc(tokd, 1)
            g.wait_ge(zd, 1)
            g.dma_start(d.i_slot.rearrange("(p b) o -> p (b o)", p=P), zero[:]).then_inc(z_out, 16)
            g.wait_ge(z_out, 16)
            g.wait_ge(tokd, 1)
            g.wait_ge(idxd, 2)
            for k in range(2):
                for t in range(T):
                    g.indirect_dma_start(out=d.i_slot, out_offset=bass.IndirectOffsetOnAxis(ap=idx[:, k, t:t + 1], axis=0),
                                         in_=tok[:, t:t + 1], in_offset=None).then_inc(sc_out, 16)
            g.wait_ge(sc_out, 16 * 2 * T)
            g.dma_start(slots[:, 2], d.i_slot.rearrange("(p b) o -> p (b o)", p=P)).then_inc(tbl_in, 16)
            g.wait_ge(tbl_in, 16)

        @block.scalar
        def _(s):
            s.wait_ge(subd, 1)
            s.activation(gd[:], gd[:], ACT.Exp).then_inc(gexp, 1)
            s.wait_ge(subd, 2)
            s.activation(a2[:], a1[:], ACT.Exp).then_inc(dexp, 1)

        @block.tensor
        def _(pe):
            pe.wait_ge(eready, 1)
            pe.wait_ge(small_in, 64)
            HT = T // 2
            for q in range(2):
                at = slice(q * HT, (q + 1) * HT)
                pe.matmul(rank[:, at], tri[:, 3], Es[:, at], start=True, stop=False)
                pe.matmul(rank[:, at], tri[:, 4], run[:, at], start=False, stop=True)
            pe.matmul(cps[:], tri[:, 4], run[:, T], start=True, stop=True).then_inc(rmm, 1)

        @block.vector
        def _(v):
            st = Steps(v, step)
            link = st.link
            v.wait_ge(small_in, 64)
            gl = logits[:, :, 0:MG]
            el = logits[:, :, MG:MG + NE].rearrange("p t (g e) -> p t g e", g=MG)
            wide = lambda a, n: a[:].broadcast_to([P, T, n])
            dsc = desc[:].unsqueeze(1).broadcast_to([P, T, EPG])

            def first_of(out, val, m):
                link(v.tensor_tensor(out[:], val, wide(m, EPG), ALU.is_equal))
                link(v.tensor_tensor(out[:], out[:], dsc, ALU.mult))
                link(v.tensor_reduce(mv[:], out[:], AX.X, ALU.max))
                link(v.tensor_tensor(out[:], out[:], wide(mv, EPG), ALU.is_equal))

            link(v.tensor_reduce(m1[:], gl, AX.X, ALU.max))
            v.tensor_tensor(gd[:], gl, wide(m1, MG), ALU.subtract).then_inc(subd, 1)
            first_of(oh, gl, m1)
            link(v.tensor_tensor(big[:], el, oh[:].unsqueeze(3).broadcast_to([P, T, MG, EPG]), ALU.mult))
            link(v.tensor_reduce(ing[:], big[:].rearrange("p t g e -> p t e g"), AX.X, ALU.add))
            link(v.tensor_reduce(m1[:], ing[:], AX.X, ALU.max))
            first_of(o1, ing[:], m1)
            link(v.scalar_tensor_tensor(out=u8[:], in0=o1[:], scalar=-1e30, in1=ing[:], op0=ALU.mult, op1=ALU.add))
            link(v.tensor_reduce(a1[:], u8[:], AX.X, ALU.max))
            first_of(o2, u8[:], a1)
            link(v.tensor_tensor(a1[:], a1[:], m1[:], ALU.subtract))
            v.tensor_scalar(a1[:], a1[:], 0.0, None, ALU.add).then_inc(subd, 1)
            v.wait_ge(gexp, 1)
            link(v.tensor_reduce(den[:], gd[:], AX.X, ALU.add))
            link(v.reciprocal(pg[:], den[:]))
            v.wait_ge(dexp, 1)
            link(v.tensor_scalar(w1[:], a2[:], 1.0, None, ALU.add))
            link(v.reciprocal(w1[:], w1[:]))
            link(v.tensor_tensor(w2[:], w1[:], a2[:], ALU.mult))
            for k, w in enumerate((w1, w2)):
                link(v.tensor_tensor(gates[:, k], w[:].rearrange("p t o -> p (t o)"), pg[:].rearrange("p t o -> p (t o)"),
                                     ALU.mult))
            for E, o in ((E1, o1), (E2, o2)):
                link(v.tensor_tensor(E[:].rearrange("p t (g e) -> p t g e", g=MG),
                                     oh[:].unsqueeze(3).broadcast_to([P, T, MG, EPG]),
                                     o[:].unsqueeze(2).broadcast_to([P, T, MG, EPG]), ALU.mult))
            link(v.tensor_tensor(Es[:], E1[:], E2[:], ALU.add))
            link(v.memset(run[:, 0], 0.0))
            for t in range(T):
                link(v.tensor_tensor(run[:, t + 1], run[:, t], Es[:, t], ALU.add))
            v.memset(one[:], 1.0).then_inc(eready, 1)
            v.wait_ge(eready, 1)
            v.wait_ge(rmm, 1)
            link(v.tensor_copy(cnt[:], cps[:]))
            link(v.tensor_tensor(cb[:], cnt[:].unsqueeze(2).broadcast_to([P, NE, MAXB]),
                                 mul[:].unsqueeze(1).broadcast_to([P, NE, MAXB]), ALU.is_gt))
            link(v.tensor_reduce(nov[:], cb[:], AX.X, ALU.add))
            link(v.tensor_tensor_scan(incl[:], one[:], nov[:], 0.0, ALU.mult, ALU.add))
            link(v.tensor_tensor(excl[:], incl[:], nov[:], ALU.subtract))
            row = lambda a: a[:].unsqueeze(1).broadcast_to([P, T, NE])
            bigf = big[:].rearrange("p t g e -> p t (g e)")
            for k, E in enumerate((E1, E2)):
                for dst, src in ((r_, rank[:]), (e_, row(iot)), (o_, row(excl))):
                    link(v.tensor_tensor(bigf, E[:], src, ALU.mult))
                    link(v.tensor_reduce(dst[:, k], bigf, AX.X, ALU.add))
                link(v.tensor_tensor(cq[:], r_[:, k].unsqueeze(2).broadcast_to([P, T, MAXB]),
                                     mul[:].unsqueeze(1).broadcast_to([P, T, MAXB]), ALU.is_ge))
                link(v.tensor_reduce(q_[:, k], cq[:], AX.X, ALU.add))
            link(v.tensor_tensor(o_[:], o_[:], q_[:], ALU.add))
            link(v.scalar_tensor_tensor(out=o_[:], in0=o_[:], scalar=float(NE - 1), in1=e_[:], op0=ALU.add,
                                        op1=ALU.subtract))
            link(v.tensor_scalar(f_[:], q_[:], 0.0, None, ALU.is_gt))
            link(v.tensor_tensor(o_[:], o_[:], f_[:], ALU.mult))
            link(v.tensor_tensor(b_[:], e_[:], o_[:], ALU.add))
            link(v.scalar_tensor_tensor(out=r_[:], in0=q_[:], scalar=-float(P), in1=r_[:], op0=ALU.mult, op1=ALU.add))
            link(v.scalar_tensor_tensor(out=f_[:], in0=r_[:], scalar=float(NBLK), in1=b_[:], op0=ALU.mult, op1=ALU.add))
            v.tensor_copy(idx[:], f_[:]).then_inc(idxd, 1)
            link(v.scalar_tensor_tensor(out=q_[:], in0=b_[:], scalar=float(P), in1=r_[:], op0=ALU.mult, op1=ALU.add))
            v.tensor_copy(slots[:, 0:2, 0:T], q_[:]).then_inc(idxd, 1)
            link(v.tensor_tensor(ob[:], incl[0:1, :].unsqueeze(1).broadcast_to([1, NOV, NE]),
                                 iot[0:1, 0:NOV].unsqueeze(2).broadcast_to([1, NOV, NE]), ALU.is_le))
            link(v.tensor_reduce(ov[:], ob[:], AX.X, ALU.add))
            link(v.tensor_scalar(ov[:], ov[:], float(NE - 1), None, ALU.min))
            link(v.tensor_copy(blocks[0:1, NE:NBLK], ov[:]))
            link(v.tensor_scalar(blocks[0:1, NBLK:NBLK + 1], incl[0:1, NE - 1:NE], float(NE), None, ALU.add))


def experts(nc, d, slots, blocks):
    FT = DE // P
    UNITS = 6
    UW = DT * DE // 2
    with ExitStack() as ctx:
        sb, ps, sem = pools(nc, ctx)
        ident = sb("ident_e", [P, P])
        (w, wl), wh = split_pair(nc, ctx, "w_e", [P, UNITS, UW]), sb("w_hi", [P, UNITS, UW], F32R)
        idx = sb("idx_e", [P, 2], I32)
        xb = sb("xb", [P, 2, D])
        xh, xl = [sb(f"xT_{n}", [P, 2, DT, P], F32R) for n in ("hi", "lo")]
        s1, g = sb("s1_e", [P, 2, DE]), sb("g_e", [P, 2, DE])
        gh, gl = [sb(f"gT_{n}", [P, 2, FT, P], F32R) for n in ("hi", "lo")]
        yo = sb("y_e", [P, 2, D])
        tp = ps("tp_e", [P, 2, BANK])
        h1, h3, gp = ps("h1_e", [P, DE]), ps("h3_e", [P, DE]), ps("gp_e", [P, FT, P])
        yp = ps("yp_e", [P, 2, BANK])
        ident_in, named, stored = sem("ex_id"), sem("ex_named"), sem("ex_stored")
        w_in = [sem(f"ex_w{u}") for u in range(UNITS)]
        x_in, y_out = [[sem(f"ex_{n}{k}") for k in range(2)] for n in ("x", "yo")]
        idxd, tpd, xhd, xld, m1, m3, sd, gd, gtp, ghd, gld, ym, yd, ye, whd, wld = [
            sem(f"ex_{n}") for n in ("idx", "tp", "xh", "xl", "m1", "m3", "s", "g", "gtp", "gh", "gl", "ym", "yd", "ye",
                                     "wh", "wl")]
        block = ctx.enter_context(nc.Block())

        def used(eng):
            return eng.value_load(blocks[0:1, NBLK:NBLK + 1], min_val=NE, max_val=NBLK)

        def run(eng, body):
            total = used(eng)
            for n in range(2):
                body(n, n, 0, True, total)
            with eng.Fori(1, NBLK // 2) as i:
                for n in range(2):
                    q = i * 2 + n
                    with eng.If(q < total):
                        body(q, n, i, False, total)

        def ahead(eng, q, first, total, body):
            if first:
                body()
            else:
                with eng.If(q + 1 < total):
                    body()

        @block.gpsimd
        def _(g_):
            def step(q, n, h, first, total):
                if not first:
                    g_.wait_ge(x_in[n], h * 16)
                    g_.wait_ge(tpd, q - 1)
                g_.tensor_copy(idx[:, n:n + 1], slots[:, 2, bass.ds(q, 1)]).then_inc(idxd, 1)
                g_.wait_ge(idxd, q + 1)
                g_.sem_inc(named, 1)
                g_.indirect_dma_start(out=xb[:, n], out_offset=None, in_=d.h2,
                                      in_offset=bass.IndirectOffsetOnAxis(ap=idx[:, n:n + 1], axis=0))\
                    .then_inc(x_in[n], 16)

            run(g_, step)

        @block.sync
        def _(sp):
            sp.dma_start(ident[:], d.ident).then_inc(ident_in, 16)

            def step(q, n, h, first, total):
                e = q if first else sp.value_load(blocks[0:1, bass.ds(q, 1)], min_val=0, max_val=NE - 1)
                for u in range(UNITS):
                    src, read = ((d.w1, m1), (d.w3, m3), (d.w2, ym))[u // 2]
                    if not first or n:
                        sp.wait_ge(read, q * 2 + (u % 2 - 1))
                    v = src[bass.ds(e, 1)].rearrange("a (p j) f -> (a p) (j f)", p=P)
                    sp.dma_start(w[:, u], v[:, u % 2 * UW:(u % 2 + 1) * UW]).then_inc(w_in[u], 16)

            run(sp, step)

        @block.tensor
        def _(pe):
            pe.wait_ge(ident_in, 16)

            def products(acc, hi, lo, u, j, width, at, start, stop):
                a, b = [t[:, u].rearrange("p (j f) -> p j f", f=width)[:, j, at:at + BANK] for t in (wh, wl)]
                pe.matmul(acc, hi, a, start=start, stop=False)
                pe.matmul(acc, hi, b, start=False, stop=False)
                return pe.matmul(acc, lo, a, start=False, stop=stop)

            def turn(q, n, h, some, half):
                if half == 0:
                    pe.wait_ge(x_in[n], h * 16 + 16)
                    if some:
                        pe.wait_ge(xld, q)
                    pe.wait_ge(ident_in, 16)
                xv = xb[:, n].rearrange("p (a j) -> p j a", j=DT)
                for j in range(half * 4, half * 4 + 4):
                    last = pe.transpose(tp[:, j // 4, (j % 4) * P:(j % 4 + 1) * P], xv[:, j], ident[:])
                if half:
                    last.then_inc(tpd, 1)

            def body(q, n, h, first, total):
                pe.wait_ge(xld, q + 1)
                for acc, u0, free, done in ((h1, 0, sd, m1), (h3, 2, gd, m3)):
                    if not first or n:
                        pe.wait_ge(free, q)
                    for j in range(DT):
                        if j % 4 == 0:
                            pe.wait_ge(wld, q * UNITS + (u0 + j // 4 + 1))
                        last = products(acc[:], xh[:, n, j], xl[:, n, j], u0 + j // 4, j % 4, DE, 0, j == 0, j == DT - 1)
                        if j % 4 == 3:
                            last.then_inc(done, 1)
                ahead(pe, q, first, total, lambda: turn(q + 1, 1 - n, h + n, True, 0))
                pe.wait_ge(gd, q + 1)
                if not first or n:
                    pe.wait_ge(gld, q)
                pe.wait_ge(ident_in, 16)
                gv = g[:, n].rearrange("p (a j) -> p j a", j=FT)
                for j in range(FT):
                    last = pe.transpose(gp[:, j], gv[:, j], ident[:])
                last.then_inc(gtp, 1)
                ahead(pe, q, first, total, lambda: turn(q + 1, 1 - n, h + n, True, 1))
                pe.wait_ge(gld, q + 1)
                if not first or n:
                    pe.wait_ge(yd, q)
                    pe.wait_ge(ye, q)
                for j in range(FT):
                    if j % 2 == 0:
                        pe.wait_ge(wld, q * UNITS + (4 + j // 2 + 1))
                    for c in range(2):
                        last = products(yp[:, c], gh[:, n, j], gl[:, n, j], 4 + j // 2, j % 2, D, c * BANK, j == 0,
                                        j == FT - 1)
                    if j % 2:
                        last.then_inc(ym, 1)

            turn(0, 0, 0, False, 0)
            turn(0, 0, 0, False, 1)
            run(pe, body)

        @block.scalar
        def _(s):
            def split(q, u):
                s.wait_ge(w_in[u], q * 16 + 16)
                s.activation(wh[:, u], w[:, u], ACT.Copy).then_inc(whd, 1)

            def turned(q, n, some):
                if some:
                    s.wait_ge(m3, q * 2 - 2)
                s.wait_ge(tpd, q + 1)
                s.activation(xh[:, n].rearrange("p j t -> p (j t)"), tp[:].rearrange("p a b -> p (a b)"), ACT.Copy)\
                    .then_inc(xhd, 1)

            def step(q, n, h, first, total):
                s.wait_ge(m1, q * 2 + 2)
                if not first:
                    s.wait_ge(gd, q - 1)
                s.activation(s1[:, n], h1[:], ACT.Silu).then_inc(sd, 1)
                split(q, 5)
                ahead(s, q, first, total, lambda: split(q + 1, 0))
                s.wait_ge(gtp, q + 1)
                if not first:
                    s.wait_ge(ym, q * 2 - 2)
                s.activation(gh[:, n], gp[:], ACT.Copy).then_inc(ghd, 1)

                def next_block():
                    turned(q + 1, 1 - n, not first or n == 1)
                    for u in range(1, 4):
                        split(q + 1, u)

                ahead(s, q, first, total, next_block)
                s.wait_ge(ym, q * 2 + 2)
                if not first:
                    s.wait_ge(y_out[n], h * 16)
                s.activation(yo[:, n, 0:BANK], yp[:, 0], ACT.Copy).then_inc(yd, 1)
                s.wait_ge(yd, q + 1)
                s.wait_ge(ye, q + 1)
                s.dma_start(d.yb[bass.ds(q * P, P), :], yo[:, n]).then_inc(y_out[n], 16)
                ahead(s, q, first, total, lambda: split(q + 1, 4))

            split(0, 0)
            turned(0, 0, False)
            for u in range(1, 5):
                split(0, u)
            run(s, step)
            total = used(s)
            for n in range(2):
                s.wait_ge(y_out[n], ((total + (1 - n)) >> 1) * 16)
                s.sem_inc(stored, 1)

        @block.vector
        def _(v):
            def split(q, u):
                v.wait_ge(whd, q * UNITS + (u + 1))
                v.tensor_tensor(wl[:, u], w[:, u], wh[:, u].bitcast(F32), ALU.subtract).then_inc(wld, 1)

            def turned(q, n, some):
                if some:
                    v.wait_ge(m3, q * 2 - 2)
                v.wait_ge(xhd, q + 1)
                v.tensor_tensor(xl[:, n].rearrange("p j t -> p (j t)"), tp[:].rearrange("p a b -> p (a b)"),
                                xh[:, n].rearrange("p j t -> p (j t)").bitcast(F32), ALU.subtract).then_inc(xld, 1)

            def step(q, n, h, first, total):
                split(q, 5)
                v.wait_ge(m3, q * 2 + 2)
                v.wait_ge(sd, q + 1)
                if not first:
                    v.wait_ge(gtp, q - 1)
                v.tensor_tensor(g[:, n], s1[:, n], h3[:], ALU.mult).then_inc(gd, 1)
                ahead(v, q, first, total, lambda: split(q + 1, 0))
                v.wait_ge(ghd, q + 1)
                if not first:
                    v.wait_ge(ym, q * 2 - 2)
                v.tensor_tensor(gl[:, n], gp[:], gh[:, n].bitcast(F32), ALU.subtract).then_inc(gld, 1)

                def next_block():
                    turned(q + 1, 1 - n, not first or n == 1)
                    for u in range(1, 4):
                        split(q + 1, u)

                ahead(v, q, first, total, next_block)
                v.wait_ge(ym, q * 2 + 2)
                if not first:
                    v.wait_ge(y_out[n], h * 16)
                v.tensor_copy(yo[:, n, BANK:D], yp[:, 1]).then_inc(ye, 1)
                ahead(v, q, first, total, lambda: split(q + 1, 4))

            split(0, 0)
            turned(0, 0, False)
            for u in range(1, 5):
                split(0, u)
            run(v, step)


def combine(nc, d, gates, slots):
    with ExitStack() as ctx:
        sb, _, sem = pools(nc, ctx)
        idx = sb("idx_c", [P, 2, 2], I32)
        yr = sb("yr_c", [P, 2, 2, D])
        gcur = sb("gate_c", [P, 2, 2])
        x1, o = sb("x1_c", [P, 2, D]), sb("out_c", [P, 2, D])
        ga, gf = sb("ga2_row", [P, D]), sb("gf_row", [P, D])
        t = sb("t_c", [P, 2, D])
        sq = sb("sq_c", [P, D])
        ms, rt, rs = sb("ms_c", [P, 2]), sb("rt_c", [P, 2]), sb("rs_c", [P, 2])
        row_in, named = sem("cb_row"), sem("cb_named")
        x_in, y_in, out_done = [[sem(f"cb_{n}{k}") for k in range(2)] for n in ("x", "y", "o")]
        idxd, a, b, c, xd, ssd_, msd, rtd, rsd, od = [sem(f"cb_{n}") for n in
                                                      ("idx", "a", "b", "c", "xd", "ss", "ms", "rt", "rs", "od")]
        block = ctx.enter_context(nc.Block())

        def tiles(eng, body):
            for n in range(2):
                body(n, n, 0, True)
            with eng.Fori(1, NTX // 2) as i:
                for n in range(2):
                    body(i * 2 + n, n, i, False)

        @block.gpsimd
        def _(g):
            def step(k, n, h, first):
                if not first:
                    g.wait_ge(y_in[n], h * 32)
                    g.wait_ge(b, k - 1)
                g.tensor_copy(idx[:, n], slots[:, 0:2, bass.ds(k, 1)].rearrange("p a o -> p (a o)")).then_inc(idxd, 1)
                g.wait_ge(idxd, k + 1)
                g.sem_inc(named, 1)
                for q in range(2):
                    g.indirect_dma_start(out=yr[:, n, q], out_offset=None, in_=d.yb,
                                         in_offset=bass.IndirectOffsetOnAxis(ap=idx[:, n, q:q + 1], axis=0))\
                        .then_inc(y_in[n], 16)

            tiles(g, step)

        @block.sync
        def _(sp):
            row = lambda r: r.rearrange("(o n) -> o n", o=1).broadcast_to([P, D])
            sp.dma_start(ga[:], row(d.mod[0, 5 * D:6 * D])).then_inc(row_in, 16)
            sp.dma_start(gf[:], row(d.g_final)).then_inc(row_in, 16)
            for n in range(2):
                sp.dma_start(x1[:, n], d.x1[n * P:(n + 1) * P, :]).then_inc(x_in[n], 16)

            def store(k, n):
                sp.wait_ge(od, k + 1)
                sp.dma_start(d.out[bass.ds(k * P, P), :], o[:, n]).then_inc(out_done[n], 16)

            with sp.Fori(1, NTX // 2) as i:
                for n in range(2):
                    store(i * 2 + (n - 2), n)
                    sp.dma_start(x1[:, n], d.x1[bass.ds((i * 2 + n) * P, P), :]).then_inc(x_in[n], 16)
            for n in range(2):
                store(NTX - 2 + n, n)
            for n in range(2):
                sp.wait_ge(out_done[n], 16 * (NTX // 2))

        @block.scalar
        def _(s):
            def step(k, n, h, first):
                s.wait_ge(y_in[n], h * 32 + 32)
                s.wait_ge(row_in, 32)
                if not first:
                    s.wait_ge(xd, k - 1)
                s.activation(t[:, n], yr[:, n, 0], ACT.Copy, scale=gates[:, 0, bass.ds(k, 1)]).then_inc(a, 1)
                s.wait_ge(xd, k + 1)
                if not first or n:
                    s.wait_ge(ssd_, k)
                s.activation(sq[:], x1[:, n], ACT.Square, accum_out=ms[:, n:n + 1]).then_inc(ssd_, 1)
                s.wait_ge(msd, k + 1)
                s.activation(rt[:, n:n + 1], ms[:, n:n + 1], ACT.Sqrt).then_inc(rtd, 1)

            tiles(s, step)

        @block.vector
        def _(v):
            v.wait_ge(row_in, 32)

            def step(k, n, h, first):
                v.wait_ge(a, k + 1)
                v.scalar_tensor_tensor(out=t[:, n], in0=yr[:, n, 1], scalar=gates[:, 1, bass.ds(k, 1)], in1=t[:, n],
                                       op0=ALU.mult, op1=ALU.add).then_inc(b, 1)
                v.wait_ge(b, k + 1)
                v.tensor_tensor(t[:, n], t[:, n], ga[:], ALU.mult).then_inc(c, 1)
                v.wait_ge(c, k + 1)
                v.wait_ge(x_in[n], h * 16 + 16)
                v.tensor_tensor(x1[:, n], t[:, n], x1[:, n], ALU.add).then_inc(xd, 1)
                v.wait_ge(ssd_, k + 1)
                v.tensor_scalar(ms[:, n:n + 1], ms[:, n:n + 1], 1.0 / D, EPS, ALU.mult, ALU.add).then_inc(msd, 1)
                v.wait_ge(rtd, k + 1)
                v.reciprocal(rs[:, n:n + 1], rt[:, n:n + 1]).then_inc(rsd, 1)
                v.wait_ge(rsd, k + 1)
                if not first:
                    v.wait_ge(out_done[n], h * 16)
                v.scalar_tensor_tensor(out=o[:, n], in0=x1[:, n], scalar=rs[:, n:n + 1], in1=gf[:], op0=ALU.mult,
                                       op1=ALU.mult).then_inc(od, 1)

            tiles(v, step)


def moe(nc, d):
    with ExitStack() as ctx:
        sb, _, _ = pools(nc, ctx)
        gates = sb("gates", [P, 2, NTX])
        slots = sb("slots", [P, 3, NBLK], I32)
        blocks = sb("blocks", [1, NBLK + 1], I32)
        with ExitStack() as inner:
            logits = inner.enter_context(nc.sbuf_tensor("logits", [P, NTX, MG + NE], F32))
            out_proj(nc, d, logits)
            dispatch(nc, d, logits, gates, slots, blocks)
        experts(nc, d, slots, blocks)
        combine(nc, d, gates, slots)


def constants():
    c = {}
    c["ident"] = np.eye(P, dtype=np.float32)
    fwd = np.arange(L)
    bwd = np.where(fwd == 0, 0, L - fwd)
    bands = np.linspace(1e-4, BANDS - 1, BANDS, dtype=np.float32)
    feats = []
    for pos in (fwd, bwd):
        ang = (np.float32(2 * math.pi / L) * pos[:, None].astype(np.float32)) * bands[None, :]
        t = (pos.astype(np.float32) / np.float32(L - 1))[:, None]
        feats.append(np.concatenate([t, np.cos(ang), -np.sin(ang)], axis=1).T)
    c["feats"] = np.concatenate(feats).astype(np.float32)
    pos = np.concatenate([fwd, bwd]).astype(np.float32) / np.float32(L - 1)
    c["t_col"] = np.ascontiguousarray(-pos.reshape(P, N2)).astype(np.float32)
    c["delta"] = np.abs(np.linspace(math.log(TARGET) / SLOW, math.log(TARGET) / FAST, DH, dtype=np.float32))
    N = 2 * L
    n1, n2 = np.arange(P), np.arange(N2)
    k1 = np.arange(1, NB1)
    ph = 2 * np.pi * ((N2 * n1[None, :, None] + n2[:, None, None]) * k1 % N) / N
    f1 = np.zeros((N2, P, P))
    f1[:, :, 0] = 1
    f1[:, :, 1] = (-1.0) ** n1
    f1[:, :, 2::2] = np.cos(ph)
    f1[:, :, 3::2] = -np.sin(ph)
    c["f1"] = f1.astype(np.float32)
    g1 = np.zeros((P, N2, NB1))
    half = ph[:, :NB1]
    g1[0] = 1
    g1[1] = (-1.0) ** n1[:NB1]
    g1[2::2] = 2 * np.cos(half).transpose(2, 0, 1)
    g1[3::2] = -2 * np.sin(half).transpose(2, 0, 1)
    c["g1"] = (g1 / N).astype(np.float32)
    th = 2 * np.pi * np.outer(n2, n2) / N2
    co, si = np.cos(th), np.sin(th)
    tw = 2 * np.pi * n2 / 64
    O = np.zeros((N2, N2))
    rr, ir, ri, ii = co, si, -si, co
    one = {"A": [[rr, ri], [ir, ii]], "B": [[ri, rr], [ii, ir]],
           "kA": [[rr, rr], [ir, ir]], "kB": [[-ri, ri], [-ii, ii]]}
    c64, s64 = np.cos(th + tw[:, None]), np.sin(th + tw[:, None])
    m2 = np.zeros((15, P, P))
    H = P // 2
    for n, name in enumerate(("A", "B", "kA", "kB")):
        b = np.block(one[name])
        m2[n, :H, :H] = m2[n, H:, H:] = b
        for row, (cc, ss) in enumerate(((co, si), (c64, s64))):
            real, imag = cc, -ss
            parts = {"A": (real, imag), "B": (imag, real), "kA": (real, real), "kB": (-imag, imag)}[name]
            m2[5 + n, row * N2:(row + 1) * N2, row * H:(row + 1) * H] = np.concatenate(parts, axis=1)
        m2[10 + n, H:, :H] = b
    inv = np.block([[co, si], [-si, co]])
    m2[4, :H, :H] = m2[4, H:, H:] = inv
    m2[9, 0:N2, 0:N2], m2[9, N2:H, 0:N2] = co, -si
    ci, s_i = np.cos(th + tw[None, :]), np.sin(th + tw[None, :])
    m2[9, H:H + N2, N2:H], m2[9, H + N2:, N2:H] = ci, -s_i
    m2[14, :H, H:] = inv
    j, l = np.arange(P)[:, None], np.arange(P)[None, :]
    c["tri"] = np.stack([j <= l, j >= l, j > l, j < l, j + l >= 0], axis=1).astype(np.float32)
    c["mask"] = np.where(np.stack([l >= j, l <= j], axis=1), 0.0, -1e30).astype(np.float32)
    c["iota"] = np.arange(NE, dtype=np.float32)
    c["mult"] = (P * np.arange(1, MAXB + 1)).astype(np.float32)
    c["desc"] = np.arange(EPG, 0, -1).astype(np.float32)
    c["i_own"] = np.arange(NE, dtype=np.int32)
    c["m2"] = np.ascontiguousarray(m2.transpose(1, 0, 2)).astype(np.float32)
    return c


SCRATCH = {
    "mod": [2, 6 * D],
    "uT": [HYT, P, L],
    "zT": [ZT, P, L],
    "sT": [XBCT, P, TOK],
    "Tk": [ORDER, P, N2, DH],
    "Tz": [P, N2, DH],
    "V": [P, N2, DH],
    "yT": [2 * CT, P, L],
    "cumT": [NT * 2 * HEADS, P],
    "Hb": [NT, P, D_SSD],
    "x1": [L, D],
    "h2": [L, D],
    "i_slot": [P * NBLK, 1],
    "yb": [NBLK * P, D],
    "dt_a": [P, 2, NT, 2 * HEADS],
}


def program(nc, d):
    adaln(nc, d)
    with ExitStack() as hctx:
        hT, hl = split_pair(nc, hctx, "hT", [P, DT, TOK])
        norm_in(nc, d, hT)
        with ExitStack() as split:
            hh = split.enter_context(nc.sbuf_tensor("hT_hi", [P, DT, TOK], F32R))
            in_proj(nc, d, hT, hl, hh)
            step_sizes(nc, d, hl, hh)
    hyena(nc, d)
    ssd(nc, d)
    moe(nc, d)


NAMES = ["x", "c", "ctx", "c_ctx", "w_ada", "b_ada", "g_norm1", "g_norm2", "w_in", "hy_conv_w", "hy_conv_b",
         "hy_f_w1", "hy_f_b1", "hy_f_freq", "hy_f_w2", "hy_f_b2", "hy_f_w3", "hy_bias", "ssd_conv_w", "ssd_conv_b",
         "ssd_a_log", "ssd_dt_bias", "ssd_d", "ssd_norm_g", "w_out", "w_group", "b_group", "w_expert", "b_expert",
         "w1", "w3", "w2", "g_final"]


def layout(name, a):
    return a if name in ("c_ctx", "g_final") else a[0]


def kernel(**inputs):
    import concourse.bacc as _bacc
    from concourse.bass_utils import run_bass_kernel_spmd as _run

    nc = _bacc.Bacc("TRN2", target_bir_lowering=False, num_devices=1)
    arrays, put = {}, {}
    host = {n: np.ascontiguousarray(layout(n, inputs[n])) for n in NAMES}
    host.update(constants())
    for name, a in host.items():
        arrays[f"in_{name}"] = a
        put[name] = nc.dram_tensor(f"in_{name}", a.shape, mybir.dt.from_np(a.dtype), kind="ExternalInput").ap()
    put["out"] = nc.dram_tensor("out_0", (L, D), F32, kind="ExternalOutput").ap()
    for name, shape in SCRATCH.items():
        put[name] = nc.dram_tensor(f"s_{name}", shape, I32 if name.startswith("i_") else F32, kind="Internal").ap()
    program(nc, namedtuple("Arrays", sorted(put))(**put))
    r = _run(nc, [arrays], core_ids=[0])
    return r.results[0]["out_0"].reshape(1, L, D)
```

```python
import math
from collections import namedtuple
from contextlib import ExitStack

import numpy as np

import concourse.bass as bass
from concourse import mybir

F32 = mybir.dt.float32
F32R = mybir.dt.float32r
I32 = mybir.dt.int32
ALU = mybir.AluOpType
ACT = mybir.ActivationFunctionType
AX = mybir.AxisListType

P = 128
D = 1024
DT = D // P
L = 2048
LC = 256
TOK = LC + L
NTX = L // P
NTC = LC // P
NT = NTX + NTC
GRID = 64
EPS = 1e-6
BANK = 512
DH = 512
CT = DH // P
HYT = 12
ZT = 4
XBCT = 8
COLT = HYT + ZT + XBCT
HEADS = 8
MG, EPG = 8, 8
NE = MG * EPG
DE = 512
NOV = 2 * L // P
NBLK = NE + NOV
MAXB = L // P - 1
HD = 64
HPG = HEADS // 2
D_SSD = HEADS * HD
SSD_DT = HEADS
ORDER = 2
BANDS = 8
EMB = 1 + 2 * BANDS
HID = 64
FAST, SLOW, TARGET = 0.3, 1.5, 1e-2
N2 = 2 * L // P
NB1 = L // N2


def pools(nc, ctx):
    def sb(name, shape, dt=F32):
        return ctx.enter_context(nc.sbuf_tensor(name, shape, dt))

    def ps(name, shape, dt=F32):
        return ctx.enter_context(nc.psum_tensor(name, shape, dt))

    held = []

    def sem(name):
        held.append(nc.alloc_semaphore(name))
        return held[-1]

    def release():
        if held:
            nc.clear_and_free_semaphores(held)
            nc.all_engine_barrier()

    ctx.callback(release)
    return sb, ps, sem


def split_pair(nc, ctx, name, shape):
    at = -(-nc.sbuf_base // 32) * 32
    whole = ctx.enter_context(nc.sbuf_tensor(name, shape, F32))
    return whole, nc.alloc_sbuf_tensor_at(f"{name}_lo", shape, F32R, offset=at)


class Steps:

    def __init__(self, eng, sem):
        self.eng, self.sem, self.n = eng, sem, 0

    def done(self, ins):
        ins.then_inc(self.sem, 1)
        self.n += 1
        return ins

    def join(self, base=0):
        self.eng.wait_ge(self.sem, base + self.n)

    def link(self, ins, base=0):
        self.done(ins)
        self.join(base)


def adaln(nc, d, x, ms):
    NCH = 6 * D // BANK
    HALF = DT // 2
    with ExitStack() as ctx:
        sb, ps, sem = pools(nc, ctx)
        cond = sb("cond", [P, 2, DT])
        act = sb("cond_silu", [P, DT, 2])
        ah, al = [sb(f"cond_{n}", [P, DT, 2], F32R) for n in ("hi", "lo")]
        (w, wl), wh = split_pair(nc, ctx, "w_ada_sb", [P, 4, HALF, BANK]), sb("w_ada_hi", [P, 4, HALF, BANK], F32R)
        bias = sb("b_ada_sb", [2, 6 * D])
        mod = sb("mod_sb", [2, 6 * D])
        sq = sb("x_sq", [P, D])
        acc = ps("mod_ps", [P, 2, BANK])
        cond_in, bias_in, silu_done, x_in, ss_done = [sem(f"ada_{n}") for n in ("cond", "bias", "silu", "x", "ss")]
        w_in, out_done = [sem(f"ada_w{k}") for k in range(4)], sem("ada_out")
        mm_done, mod_done, whd, wld, ahd, ald = [sem(f"ada_{n}") for n in ("mm", "mod", "wh", "wl", "ah", "al")]
        wv = d.w_ada.rearrange("(p j) n -> p j n", p=P)
        SQ = NT // (NCH // 2)
        block = ctx.enter_context(nc.Block())

        @block.sync
        def _(sp):
            sp.dma_start(cond[:, 0, :], d.c.rearrange("(p j) -> p j", p=P)).then_inc(cond_in, 16)
            sp.dma_start(cond[:, 1, :], d.c_ctx.rearrange("(p j) -> p j", p=P)).then_inc(cond_in, 16)
            def load(i, k):
                at = bass.ds((i * 2 + k // 2) * BANK, BANK)
                sp.dma_start(w[:, k], wv[:, k % 2 * HALF:(k % 2 + 1) * HALF, at]).then_inc(w_in[k], 16)

            for k in range(4):
                load(0, k)
            for v in range(2):
                sp.dma_start(bias[v:v + 1, :], d.b_ada.rearrange("(a n) -> a n", a=1)).then_inc(bias_in, 16)
            with sp.Fori(1, NCH // 2) as i:
                for k in range(4):
                    sp.wait_ge(mm_done, i * 4 + (k - 3))
                    load(i, k)
            sp.wait_ge(mod_done, NCH)
            sp.dma_start(d.mod, mod[:, :]).then_inc(out_done, 16)
            sp.wait_ge(out_done, 16)

        @block.gpsimd
        def _(g):
            g.dma_start(x[:, 0:NTC, :], d.ctx.rearrange("(t p) n -> p t n", p=P)).then_inc(x_in, 16)
            for q in range(4):
                a = q * 4
                g.dma_start(x[:, NTC + a:NTC + a + 4, :], d.x.rearrange("(t p) n -> p t n", p=P)[:, a:a + 4, :])\
                    .then_inc(x_in, 16)

        @block.scalar
        def _(s):
            s.wait_ge(cond_in, 32)
            s.activation(act[:].rearrange("p j v -> p v j"), cond[:], ACT.Silu).then_inc(silu_done, 1)
            s.wait_ge(silu_done, 1)
            s.activation(ah[:], act[:], ACT.Copy).then_inc(ahd, 1)

            def lead(n, h):
                s.wait_ge(w_in[n], h * 16 + 16)
                s.activation(wh[:, n], w[:, n], ACT.Copy).then_inc(whd, 1)

            def squares(i, first):
                for k in range(SQ):
                    if not first or k:
                        s.wait_ge(ss_done, i * SQ + k)
                    at = bass.ds(i * SQ + k, 1)
                    s.activation(sq[:], x[:, at, :], ACT.Square, accum_out=ms[:, at]).then_inc(ss_done, 1)

            for h in range(2):
                for k in range(4):
                    lead(k, h)
            s.wait_ge(x_in, 80)
            squares(0, True)
            with s.Fori(2, NCH // 2) as i:
                for k in range(4):
                    lead(k, i)
                squares(i - 1, False)
            squares(NCH // 2 - 1, False)
            s.wait_ge(ss_done, NT)

        @block.tensor
        def _(pe):
            pe.wait_ge(ald, 1)

            def chunk(i, n, first):
                if not first:
                    pe.wait_ge(mod_done, i * 2 + (n - 1))
                for j in range(DT):
                    k, r = 2 * n + j // HALF, j % HALF
                    if r == 0:
                        pe.wait_ge(wld, i * 4 + (k + 1))
                    pe.matmul(acc[0:2, n, :], ah[:, j, :], wh[:, k, r, :], start=(j == 0), stop=False)
                    pe.matmul(acc[0:2, n, :], ah[:, j, :], wl[:, k, r, :], start=False, stop=False)
                    last = pe.matmul(acc[0:2, n, :], al[:, j, :], wh[:, k, r, :], start=False, stop=(j == DT - 1))
                    if r == HALF - 1:
                        last.then_inc(mm_done, 1)

            for n in range(2):
                chunk(0, n, True)
            with pe.Fori(1, NCH // 2) as i:
                for n in range(2):
                    chunk(i, n, False)

        @block.vector
        def _(v):
            v.wait_ge(ahd, 1)
            v.tensor_tensor(al[:], act[:], ah[:].bitcast(F32), ALU.subtract).then_inc(ald, 1)

            def trail(n, k):
                v.wait_ge(whd, k + 1)
                v.tensor_tensor(wl[:, n], w[:, n], wh[:, n].bitcast(F32), ALU.subtract).then_inc(wld, 1)

            def add(i, n):
                v.wait_ge(mm_done, i * 4 + (2 * n + 2))
                at = bass.ds((i * 2 + n) * BANK, BANK)
                v.tensor_tensor(mod[:, at], acc[0:2, n, :], bias[:, at], ALU.add).then_inc(mod_done, 1)

            for k in range(4):
                trail(k, k)
            v.wait_ge(bias_in, 32)
            with v.Fori(1, NCH // 2) as i:
                for n in range(2):
                    add(i - 1, n)
                    for k in range(2 * n, 2 * n + 2):
                        trail(k, i * 4 + k)
            for n in range(2):
                add(NCH // 2 - 1, n)


def norm_in(nc, d, x, ms, hT):
    with ExitStack() as ctx:
        sb, ps, sem = pools(nc, ctx)
        rms = sb("x_rms", [P, NT])
        rstd = sb("x_rstd", [P, NT])
        xn = sb("x_n", [P, 2, D])
        ident = sb("ident", [P, P])
        m = sb("mod_cols", [P, 2, 2, DT])
        g = sb("g1_cols", [P, DT])
        gs = sb("g1_scale", [P, 2, DT])
        tp = ps("x_tp", [P, 2, 2, 4, P])
        small_in = sem("nin_small")
        rs, scale_ready = sem("nin_rs"), sem("nin_scale")
        xn_done, tp_done, evac, evac2 = sem("nin_xn"), sem("nin_tp"), sem("nin_evac"), sem("nin_evac2")
        block = ctx.enter_context(nc.Block())

        @block.gpsimd
        def _(g_):
            g_.dma_start(ident[:], d.ident).then_inc(small_in, 16)
            with nc.allow_non_contiguous_dma(reason="modulation vectors as columns"):
                g_.dma_start(g[:], d.g_norm1.rearrange("(j p) -> p j", p=P)).then_inc(small_in, 16)
                for v in range(2):
                    for s in range(2):
                        g_.dma_start(m[:, v, s, :], d.mod[v, s * D:(s + 1) * D].rearrange("(j p) -> p j", p=P))\
                            .then_inc(small_in, 16)

        @block.scalar
        def _(s):
            s.wait_ge(rs, 1)
            s.activation(rms[:], ms[:], ACT.Sqrt).then_inc(rs, 1)
            s.wait_ge(scale_ready, 2)
            for v, t0, t1 in ((1, 0, NTC // 2), (0, NTC // 2, NT // 2)):
                with s.Fori(t0, t1) as i:
                    for n in range(2):
                        s.wait_ge(tp_done, (i * 2 + n) + 1)
                        s.wait_ge(scale_ready, 2)
                        for j in range(DT // 2):
                            last = s.activation(hT[:, j, bass.ds((i * 2 + n) * P, P)], tp[:, n, j // 4, j % 4, :],
                                                ACT.Identity, bias=m[:, v, 0, j:j + 1], scale=gs[:, v, j:j + 1])
                        last.then_inc(evac, 1)

        @block.vector
        def _(v):
            v.wait_ge(small_in, 96)
            for k in range(2):
                v.scalar_tensor_tensor(out=gs[:, k, :], in0=m[:, k, 1, :], scalar=1.0, in1=g[:], op0=ALU.add,
                                       op1=ALU.mult).then_inc(scale_ready, 1)
            v.tensor_scalar(ms[:], ms[:], 1.0 / D, EPS, ALU.mult, ALU.add).then_inc(rs, 1)
            v.wait_ge(rs, 2)
            v.reciprocal(rstd[:], rms[:]).then_inc(rs, 1)
            v.wait_ge(rs, 3)

            def scaled(t, n):
                v.tensor_scalar(xn[:, n, :], x[:, bass.ds(t, 1), :], rstd[:, bass.ds(t, 1)], None, ALU.mult)\
                    .then_inc(xn_done, 1)

            def shifted(t, n, k):
                v.wait_ge(tp_done, t + 1)
                v.wait_ge(scale_ready, 2)
                for j in range(DT // 2, DT):
                    last = v.tensor_scalar(hT[:, j, bass.ds(t * P, P)], tp[:, n, j // 4, j % 4, :], gs[:, k, j:j + 1],
                                           m[:, k, 0, j:j + 1], ALU.mult, ALU.add)
                last.then_inc(evac2, 1)

            for n in range(2):
                scaled(n, n)
            for k, t0, t1 in ((1, 0, NTC // 2), (0, NTC // 2, NT // 2 - 1)):
                with v.Fori(t0, t1) as i:
                    for n in range(2):
                        shifted(i * 2 + n, n, k)
                        scaled(i * 2 + (n + 2), n)
            for n in range(2):
                shifted(NT - 2 + n, n, 0)

        @block.tensor
        def _(pe):
            pe.wait_ge(small_in, 96)

            def tile(n):
                for j in range(DT):
                    last = pe.transpose(tp[:, n, j // 4, j % 4, :], xn[:, n, j * P:(j + 1) * P], ident[:])
                last.then_inc(tp_done, 1)

            for n in range(2):
                pe.wait_ge(xn_done, n + 1)
                tile(n)
            with pe.Fori(1, NT // 2) as i:
                for n in range(2):
                    pe.wait_ge(xn_done, i * 2 + (n + 1))
                    pe.wait_ge(evac, i * 2 + (n - 1))
                    pe.wait_ge(evac2, i * 2 + (n - 1))
                    tile(n)


def in_proj(nc, d, hT, hl, hh):
    NC4 = L // BANK
    ROWS = BANK // GRID
    with ExitStack() as ctx:
        sb, ps, sem = pools(nc, ctx)
        (w, wl), wh = split_pair(nc, ctx, "w_in_sb", [P, 2, DT, P]), sb("w_in_hi", [P, 2, DT, P], F32R)
        y = sb("proj_sb", [P, 2, NC4, BANK])
        cw = sb("conv_cols", [P, 4, COLT])
        mid = sb("conv_mid", [P, 2, 2])
        acc = ps("proj_ps", [P, 2, NC4, BANK])
        small_in = sem("ip_small")
        w_in = [sem("ip_w0"), sem("ip_w1")]
        mm_done = sem("ip_mm")
        act_done, conv_step, bank_done, silu_done = sem("ip_act"), sem("ip_conv"), sem("ip_bank"), sem("ip_silu")
        z_done, mid_done = sem("ip_z"), sem("ip_mid")
        st_done = [sem("ip_st0"), sem("ip_st1")]
        whd, wld, hhd, hld = [sem(f"ip_{n}") for n in ("wh", "wl", "hh", "hl")]
        CHUNKS = [slice(LC + c * BANK, LC + (c + 1) * BANK) for c in range(NC4)] + [slice(0, LC)]
        wv = d.w_in.rearrange("(j p) n -> p j n", p=P)
        XT = 6
        H2, Z2, S2, X2 = HYT // 2, (HYT + ZT) // 2, COLT // 2, (COLT + XT) // 2
        block = ctx.enter_context(nc.Block())

        @block.gpsimd
        def _(g):
            with nc.allow_non_contiguous_dma(reason="per-column convolution weights as columns"):
                for k in range(3):
                    g.dma_start(cw[:, k, 0:HYT], d.hy_conv_w[k].rearrange("(j p) -> p j", p=P)).then_inc(small_in, 16)
                    g.dma_start(cw[:, k, HYT + ZT:COLT], d.ssd_conv_w[k].rearrange("(j p) -> p j", p=P))\
                        .then_inc(small_in, 16)
                g.dma_start(cw[:, 3, 0:HYT], d.hy_conv_b.rearrange("(j p) -> p j", p=P)).then_inc(small_in, 16)
                g.dma_start(cw[:, 3, HYT + ZT:COLT], d.ssd_conv_b.rearrange("(j p) -> p j", p=P)).then_inc(small_in, 16)

        @block.sync
        def _(sp):
            for n in range(2):
                sp.dma_start(w[:, n], wv[:, :, n * P:(n + 1) * P]).then_inc(w_in[n], 16)

            def pair(i, store, load, done=lambda i, n: i * (2 * NC4) + (n + 1) * NC4):
                for n in range(2):
                    if load:
                        sp.wait_ge(mm_done, done(i, n))
                        sp.dma_start(w[:, n], wv[:, :, bass.ds(load(i, n) * P, P)]).then_inc(w_in[n], 16)
                    store(i, n)

            def store_h(i, n):
                sp.wait_ge(bank_done, i * (2 * NC4) + (n + 1) * NC4)
                sp.dma_start(d.uT[bass.ds(i * 2 + n, 1)].rearrange("a p t -> (a p) t"),
                             y[:, n].rearrange("p a b -> p (a b)")).then_inc(st_done[n], 16)

            def store_z(i, n):
                sp.wait_ge(z_done, (i - H2) * (2 * NC4) + (n + 1) * NC4)
                sp.dma_start(d.zT[bass.ds(i * 2 + (n - HYT), 1)].rearrange("a p t -> (a p) t"),
                             y[:, n].rearrange("p a b -> p (a b)")).then_inc(st_done[n], 16)

            def store_s(i, n):
                sp.wait_ge(silu_done, (i - Z2) * 2 + (n + 1))
                sp.dma_start(d.sT[bass.ds(i * 2 + (n - HYT - ZT), 1), :, LC:TOK].rearrange("a p t -> (a p) t"),
                             y[:, n].rearrange("p a b -> p (a b)")).then_inc(st_done[n], 16)

            def store_x(i, n):
                sp.wait_ge(silu_done, (i - Z2) * 2 + (n + 1))
                sp.dma_start(d.sT[bass.ds(i * 2 + (n - COLT), 1), :, 0:LC].rearrange("a p t -> (a p) t"),
                             y[:, n, 0, 0:LC]).then_inc(st_done[n], 16)

            nxt = lambda i, n: i * 2 + (n + 2)
            for a, b, store in ((0, H2, store_h), (H2, Z2, store_z), (Z2, S2 - 1, store_s)):
                with sp.Fori(a, b) as i:
                    pair(i, store, nxt)
            pair(S2 - 1, store_s, lambda i, n: HYT + ZT + n)
            with sp.Fori(S2, X2 - 1) as i:
                pair(i, store_x, lambda i, n: i * 2 + (n + 2 - COLT + HYT + ZT),
                     lambda i, n: COLT * NC4 + (i - S2) * 2 + (n + 1))
            pair(X2 - 1, store_x, None)
            for n in range(2):
                sp.wait_ge(st_done[n], 16 * X2)

        @block.tensor
        def _(pe):
            def products(out, n, at):
                for j in range(DT):
                    pe.matmul(out, wh[:, n, j, :], hh[:, j, at], start=(j == 0), stop=False)
                    pe.matmul(out, wh[:, n, j, :], hl[:, j, at], start=False, stop=False)
                    last = pe.matmul(out, wl[:, n, j, :], hh[:, j, at], start=False, stop=(j == DT - 1))
                last.then_inc(mm_done, 1)

            def tile(i, n, read=None, off=0):
                pe.wait_ge(wld, i * 2 + (n + 1))
                for c in range(NC4):
                    if read is not None:
                        pe.wait_ge(read, (i - 1 - off) * (2 * NC4) + (n * NC4 + c + 1))
                    elif n == 0:
                        pe.wait_ge(hld, c + 1)
                    products(acc[:, n, c, :], n, CHUNKS[c])

            for n in range(2):
                tile(0, n)
            for a, b, read, off in ((1, H2 + 1, bank_done, 0), (H2 + 1, Z2 + 1, z_done, H2),
                                    (Z2 + 1, S2, bank_done, Z2 - H2)):
                with pe.Fori(a, b) as i:
                    for n in range(2):
                        tile(i, n, read, off)
            pe.wait_ge(hld, NC4 + 1)
            with pe.Fori(S2, X2) as i:
                for n in range(2):
                    pe.wait_ge(wld, i * 2 + (n + 1))
                    pe.wait_ge(bank_done, (COLT - ZT) * NC4 + (i - S2) * 2 + (n - 1))
                    products(acc[:, n, 0, 0:LC], n, CHUNKS[NC4])

        @block.scalar
        def _(s):
            s.wait_ge(small_in, 128)

            def lead(n, h):
                s.wait_ge(w_in[n], h * 16 + 16)
                s.activation(wh[:, n], w[:, n], ACT.Copy).then_inc(whd, 1)

            def split(i, n):
                lead(1 - n, i + n)

            lead(0, 0)
            for at in CHUNKS:
                s.activation(hh[:, :, at], hT[:, :, at], ACT.Copy).then_inc(hhd, 1)

            def centre(i, n, first, skip=0):
                split(i, n)
                s.activation(mid[:, n, :], cw[:, 1:4:2, bass.ds(i * 2 + n, 1)], ACT.Copy).then_inc(mid_done, 1)
                s.wait_ge(mid_done, (i - skip) * 2 + (n + 1))
                if not first:
                    s.wait_ge(st_done[n], i * 16)
                for c in range(NC4):
                    s.wait_ge(mm_done, i * (2 * NC4) + (n * NC4 + c + 1))
                    s.activation(y[:, n, c, :], acc[:, n, c, :], ACT.Identity, bias=mid[:, n, 1:2],
                                 scale=mid[:, n, 0:1]).then_inc(act_done, 1)

            centre(0, 0, True)
            centre(0, 1, True)
            with s.Fori(1, H2) as i:
                for n in range(2):
                    centre(i, n, False)
            with s.Fori(H2, Z2) as i:
                for n in range(2):
                    split(i, n)
                    s.wait_ge(st_done[n], i * 16)
                    for c in range(NC4):
                        s.wait_ge(mm_done, i * (2 * NC4) + (n * NC4 + c + 1))
                        s.activation(y[:, n, c, :], acc[:, n, c, :], ACT.Silu).then_inc(z_done, 1)
            with s.Fori(Z2, S2) as i:
                for n in range(2):
                    centre(i, n, False, Z2 - H2)
                    s.wait_ge(bank_done, (i - (Z2 - H2)) * (2 * NC4) + (n + 1) * NC4)
                    s.activation(y[:, n], y[:, n], ACT.Silu).then_inc(silu_done, 1)

            def context(i, n, more=True):
                if more:
                    split(i, n)
                s.activation(mid[:, n, :], cw[:, 1:4:2, bass.ds(i * 2 + (n - COLT + HYT + ZT), 1)], ACT.Copy)\
                    .then_inc(mid_done, 1)
                s.wait_ge(mid_done, (i - (Z2 - H2)) * 2 + (n + 1))
                s.wait_ge(st_done[n], i * 16)
                s.wait_ge(mm_done, COLT * NC4 + (i - S2) * 2 + (n + 1))
                s.activation(y[:, n, 0, 0:LC], acc[:, n, 0, 0:LC], ACT.Identity, bias=mid[:, n, 1:2],
                             scale=mid[:, n, 0:1]).then_inc(act_done, 1)
                s.wait_ge(bank_done, (COLT - ZT) * NC4 + (i - S2) * 2 + (n + 1))
                s.activation(y[:, n, 0, 0:LC], y[:, n, 0, 0:LC], ACT.Silu).then_inc(silu_done, 1)

            with s.Fori(S2, X2 - 1) as i:
                for n in range(2):
                    context(i, n)
            for n in range(2):
                context(X2 - 1, n, n == 0)

        @block.vector
        def _(v):
            v.wait_ge(small_in, 128)

            def trail(n, k):
                v.wait_ge(whd, k + 1)
                v.tensor_tensor(wl[:, n], w[:, n], wh[:, n].bitcast(F32), ALU.subtract).then_inc(wld, 1)

            def split(i, n):
                trail(1 - n, i * 2 + (n + 1))

            trail(0, 0)
            for c, at in enumerate(CHUNKS):
                v.wait_ge(hhd, c + 1)
                v.tensor_tensor(hl[:, :, at], hT[:, :, at], hh[:, :, at].bitcast(F32), ALU.subtract)\
                    .then_inc(hld, 1)

            def taps(i, n, c, k, rows, width, act_at, conv_at):
                pv = acc[:, n, c, 0:rows * width].rearrange("p (r t) -> p r t", t=width)
                yv = y[:, n, c, 0:rows * width].rearrange("p (r t) -> p r t", t=width)
                v.wait_ge(act_done, act_at)
                v.scalar_tensor_tensor(out=yv[:, :, 1:], in0=pv[:, :, :-1], scalar=cw[:, 0, k], in1=yv[:, :, 1:],
                                       op0=ALU.mult, op1=ALU.add).then_inc(conv_step, 1)
                v.wait_ge(conv_step, conv_at)
                v.scalar_tensor_tensor(out=yv[:, :, :-1], in0=pv[:, :, 1:], scalar=cw[:, 2, k], in1=yv[:, :, :-1],
                                       op0=ALU.mult, op1=ALU.add).then_inc(bank_done, 1)

            def convolve(a, b, off):
                with v.Fori(a, b) as i:
                    for n in range(2):
                        split(i, n)
                        for c in range(NC4):
                            at = i * (2 * NC4) + (n * NC4 + c + 1 - off)
                            taps(i, n, c, bass.ds(i * 2 + n, 1), ROWS, GRID, at, at)

            convolve(0, H2, 0)
            with v.Fori(H2, Z2) as i:
                for n in range(2):
                    split(i, n)
            convolve(Z2, S2, (Z2 - H2) * 2 * NC4)
            base = (COLT - ZT) * NC4

            def context(i, n, more=True):
                if more:
                    split(i, n)
                at = (i - S2) * 2 + (n + 1 + base)
                taps(i, n, 0, bass.ds(i * 2 + (n - COLT + HYT + ZT), 1), 1, LC, at, at)

            with v.Fori(S2, X2 - 1) as i:
                for n in range(2):
                    context(i, n)
            for n in range(2):
                context(X2 - 1, n, n == 0)


def step_sizes(nc, d, hl, hh):
    NC5 = -(-TOK // BANK)
    NB = 2 * SSD_DT
    with ExitStack() as ctx:
        sb, ps, sem = pools(nc, ctx)
        w, wl, wh = sb("w_dt", [P, DT, NB]), sb("w_dt_lo", [P, DT, NB], F32R), sb("w_dt_hi", [P, DT, NB], F32R)
        dtb = sb("dt_bias_col", [NB, 1])
        alog = sb("a_log_row", [P, NB])
        arow = sb("a_row", [P, NB])
        dtT = sb("dt_T", [NB, TOK])
        ident = sb("ident2", [P, P])
        xr, ax, e, u, ln, dd, iz, r = [sb(f"sp_{n}", [P, NT * NB]) for n in ("x", "abs", "e", "u", "ln", "d", "z", "r")]
        dta = sb("dt_a", [P, 2, NT * NB])
        acc = ps("dt_ps", [NB, 2, BANK])
        xps = ps("dt_x_ps", [P, BANK])
        wdt_in, whd, wld, mm, ev, turned, xrd, arowd, axd, ed, ud, lnd, dtd, ad, out_done, chain = [
            sem(f"dt_{n}") for n in ("in", "wh", "wl", "mm", "ev", "tp", "xr", "arow", "ax", "e", "u", "ln", "dt",
                                     "a", "out", "chain")]
        block = ctx.enter_context(nc.Block())

        @block.sync
        def _(sp):
            with nc.allow_non_contiguous_dma(reason="16 columns of the projection"):
                sp.dma_start(w[:], d.w_in.rearrange("(j p) n -> p j n", p=P)[:, :, COLT * P:COLT * P + NB])\
                    .then_inc(wdt_in, 16)
            sp.dma_start(ident[:], d.ident).then_inc(wdt_in, 16)
            sp.dma_start(dtb[:], d.ssd_dt_bias.rearrange("a (h o) -> (a h) o", o=1)).then_inc(wdt_in, 16)
            sp.dma_start(alog[:], d.ssd_a_log.rearrange("(o a) h -> o (a h)", o=1).broadcast_to([P, NB]))\
                .then_inc(wdt_in, 16)
            sp.wait_ge(ad, 1)
            sp.dma_start(d.dt_a, dta[:].rearrange("p k (t h) -> p k t h", t=NT)).then_inc(out_done, 16)
            sp.wait_ge(out_done, 16)

        @block.tensor
        def _(pe):
            pe.wait_ge(wdt_in, 64)
            pe.wait_ge(wld, 1)
            for c in range(NC5):
                at = slice(c * BANK, min(TOK, (c + 1) * BANK))
                out = acc[:, c % 2, 0:at.stop - at.start]
                if c >= 2:
                    pe.wait_ge(ev, c - 1)
                for j in range(DT):
                    pe.matmul(out, wh[:, j, :], hh[:, j, at], start=(j == 0), stop=False)
                    pe.matmul(out, wh[:, j, :], hl[:, j, at], start=False, stop=False)
                    last = pe.matmul(out, wl[:, j, :], hh[:, j, at], start=False, stop=(j == DT - 1))
                last.then_inc(mm, 1)
            pe.wait_ge(ev, NC5)
            for t in range(NT):
                last = pe.transpose(xps[:, t * NB:(t + 1) * NB], dtT[:, t * P:(t + 1) * P], ident[0:NB, 0:NB])
            last.then_inc(turned, 1)

        @block.scalar
        def _(s):
            s.wait_ge(wdt_in, 64)
            s.activation(wh[:], w[:], ACT.Copy).then_inc(whd, 1)
            s.activation(arow[:], alog[:], ACT.Exp).then_inc(arowd, 1)
            s.wait_ge(xrd, 1)
            s.activation(ax[:], xr[:], ACT.Abs).then_inc(axd, 1)
            s.wait_ge(axd, 1)
            s.activation(e[:], ax[:], ACT.Exp, scale=-1.0).then_inc(ed, 1)
            s.wait_ge(ud, 1)
            s.activation(ln[:], u[:], ACT.Ln).then_inc(lnd, 1)

        @block.vector
        def _(v):
            v.wait_ge(wdt_in, 64)
            v.wait_ge(whd, 1)
            v.tensor_tensor(wl[:], w[:], wh[:].bitcast(F32), ALU.subtract).then_inc(wld, 1)
            for c in range(NC5):
                t0, t1 = c * BANK, min(TOK, (c + 1) * BANK)
                v.wait_ge(mm, c + 1)
                v.tensor_scalar(dtT[:, t0:t1], acc[:, c % 2, 0:t1 - t0], dtb[:, 0:1], None, ALU.add).then_inc(ev, 1)
            v.wait_ge(turned, 1)
            v.tensor_copy(xr[:], xps[:, 0:NT * NB]).then_inc(xrd, 1)
            v.wait_ge(ed, 1)
            v.tensor_scalar(u[:], e[:], 1.0, None, ALU.add).then_inc(ud, 1)
            v.wait_ge(ud, 1)
            st = Steps(v, chain)
            st.link(v.tensor_scalar(dd[:], u[:], -1.0, None, ALU.add))
            st.link(v.tensor_scalar(iz[:], dd[:], 0.0, None, ALU.is_equal))
            st.link(v.tensor_tensor(dd[:], dd[:], iz[:], ALU.add))
            st.link(v.reciprocal(r[:], dd[:]))
            v.wait_ge(lnd, 1)
            st.link(v.tensor_tensor(ln[:], ln[:], r[:], ALU.mult))
            st.link(v.tensor_tensor(ln[:], ln[:], iz[:], ALU.add))
            st.link(v.tensor_tensor(ln[:], ln[:], e[:], ALU.mult))
            v.wait_ge(xrd, 1)
            v.scalar_tensor_tensor(out=dta[:, 0, :], in0=xr[:], scalar=0.0, in1=ln[:], op0=ALU.max, op1=ALU.add)\
                .then_inc(dtd, 1)
            v.wait_ge(dtd, 1)
            v.wait_ge(arowd, 1)
            v.scalar_tensor_tensor(out=dta[:, 1, :].rearrange("p (t h) -> p t h", t=NT),
                                   in0=dta[:, 0, :].rearrange("p (t h) -> p t h", t=NT), scalar=-1.0,
                                   in1=arow[:].rearrange("p (o h) -> p o h", o=1).broadcast_to([P, NT, NB]),
                                   op0=ALU.mult, op1=ALU.mult).then_inc(ad, 1)


def hyena_filters(nc, d, z):
    NCH = L // BANK
    TWO_PI = 2 * math.pi
    C1 = 6.28125
    C2 = TWO_PI - C1
    MAGIC = 1.5 * 2.0 ** 23
    F2 = HID * 2
    with ExitStack() as ctx:
        sb, ps, sem = pools(nc, ctx)
        feats = sb("feats", [2 * EMB, L])
        w1 = sb("f_w1_diag", [2 * EMB, F2])
        w2 = sb("f_w2_diag", [F2, F2])
        w3 = sb("f_w3", [F2, ORDER, DH])
        cols = sb("f_cols", [F2, 3])
        fb = sb("f_fb", [F2, 2])
        h1 = sb("f_h1", [F2, L])
        h2 = sb("f_h2", [F2, L])
        x, k, r = sb("sin_x", [F2, 2, BANK]), sb("sin_k", [F2, BANK]), sb("sin_r", [F2, 2, BANK])
        tcol = sb("t_col", [P, N2])
        drow = sb("delta_row", [P, DH])
        win = sb("window", [P, 2, DH])
        stat = sb("h_stat", [F2, 2, P])
        blank = sb("blank", [P, D])
        f1 = sb("f1_sb", [P, 2, P])
        kf = sb("k_sb", [P, 2, ORDER, DH])
        tb = sb("tk_sb", [P, 2, ORDER, DH])
        kp = ps("k_ps", [P, 2, ORDER, DH])
        tp = ps("tk_ps", [P, 2, ORDER, DH])
        small_in, zeroed, pre = sem("hf_in"), sem("hf_zero"), sem("hf_pre")
        z_in = sem("hf_z")
        blanked, blank_out = sem("hf_blank"), sem("hf_blank_out")
        mm, sarg, sined = sem("hf_mm"), sem("hf_arg"), sem("hf_sin")
        f1_in = [sem("hf_f10"), sem("hf_f11")]
        st_out = [sem("hf_st0"), sem("hf_st1")]
        statd, kmm, wind, kfd, tmm, tev = (sem("hf_stat"), sem("hf_kmm"), sem("hf_win"), sem("hf_kf"), sem("hf_tmm"),
                                           sem("hf_tev"))
        step = sem("hf_step")
        block = ctx.enter_context(nc.Block())

        @block.gpsimd
        def _(g):
            g.memset(w1[:], 0.0).then_inc(zeroed, 1)
            g.memset(w2[:], 0.0).then_inc(zeroed, 1)
            g.memset(stat[:], 0.0).then_inc(zeroed, 1)
            g.memset(blank[:], 0.0).then_inc(blanked, 1)
            g.dma_start(feats[:], d.feats).then_inc(small_in, 16)
            g.wait_ge(zeroed, 3)
            for q in range(2):
                g.dma_start(w1[q * EMB:(q + 1) * EMB, q * HID:(q + 1) * HID], d.hy_f_w1).then_inc(small_in, 16)
                g.dma_start(w2[q * HID:(q + 1) * HID, q * HID:(q + 1) * HID], d.hy_f_w2).then_inc(small_in, 16)
                g.dma_start(w3[q * HID:(q + 1) * HID], d.hy_f_w3.rearrange("h (o q c) -> q h o c", o=ORDER, q=2)[q])\
                    .then_inc(small_in, 16)
                for n, a in enumerate((d.hy_f_b1, d.hy_f_b2, d.hy_f_freq)):
                    g.dma_start(cols[q * HID:(q + 1) * HID, n:n + 1], a.rearrange("(h o) -> h o", o=1))\
                        .then_inc(small_in, 16)
            g.dma_start(tcol[:], d.t_col).then_inc(small_in, 16)
            g.dma_start(drow[:], d.delta.rearrange("(o c) -> o c", o=1).broadcast_to([P, DH])).then_inc(small_in, 16)
            g.wait_ge(blanked, 1)
            g.dma_start(d.yb[NE * P:NBLK * P, :].rearrange("(p b) c -> p b c", p=P),
                        blank[:].unsqueeze(1).broadcast_to([P, NOV, D])).then_inc(blank_out, 16)
            g.wait_ge(blank_out, 16)

        @block.sync
        def _(sp):
            for n in range(2):
                sp.dma_start(f1[:, n], d.f1[n]).then_inc(f1_in[n], 16)
            sp.dma_start(z[:], d.uT[0:CT].rearrange("c p t -> p c t")).then_inc(z_in, 16)
            with sp.Fori(0, N2 // 2 - 1) as i:
                for n in range(2):
                    sp.wait_ge(tmm, i * 2 + (n + 1))
                    sp.dma_start(f1[:, n], d.f1[bass.ds(i * 2 + (n + 2), 1)].rearrange("a p m -> (a p) m"))\
                        .then_inc(f1_in[n], 16)
                    sp.wait_ge(tev, i * 2 + (n + 1))
                    sp.dma_start(d.Tk[:, :, bass.ds(i * 2 + n, 1), :].rearrange("o p a c -> p o (a c)"), tb[:, n])\
                        .then_inc(st_out[n], 16)
            for n in range(2):
                sp.wait_ge(tev, N2 - 1 + n)
                sp.dma_start(d.Tk[:, :, N2 - 2 + n, :].rearrange("o p c -> p o c"), tb[:, n]).then_inc(st_out[n], 16)
            for n in range(2):
                sp.wait_ge(st_out[n], 16 * (N2 // 2))
            sp.wait_ge(z_in, 16)

        @block.tensor
        def _(pe):
            pe.wait_ge(small_in, 16 * 15)
            for c in range(NCH):
                if c >= 2:
                    pe.wait_ge(sarg, c - 1)
                pe.matmul(kp[:, c % 2, 0, :], w1[:], feats[:, c * BANK:(c + 1) * BANK], start=True, stop=True)\
                    .then_inc(mm, 1)
            for c in range(NCH):
                pe.wait_ge(sined, c + 1)
                pe.wait_ge(sarg, NCH + c - 1)
                pe.matmul(kp[:, c % 2, 0, :], w2[:], h1[:, c * BANK:(c + 1) * BANK], start=True, stop=True)\
                    .then_inc(mm, 1)
            with pe.Fori(0, N2 // 2) as i:
                for n in range(2):
                    pe.wait_ge(statd, i * 2 + (n + 1))
                    for o in range(ORDER):
                        last = pe.matmul(kp[:, n, o, :], stat[:, n], w3[:, o], start=True, stop=True)
                    last.then_inc(kmm, 1)
                for n in range(2):
                    pe.wait_ge(kfd, i * 2 + (n + 1))
                    pe.wait_ge(f1_in[n], i * 16 + 16)
                    for o in range(ORDER):
                        last = pe.matmul(tp[:, n, o, :], f1[:, n], kf[:, n, o], start=True, stop=True)
                    last.then_inc(tmm, 1)

        @block.vector
        def _(v):
            st = Steps(v, step)
            v.wait_ge(small_in, 16 * 15)
            for n in range(2):
                v.tensor_tensor(fb[:, n:n + 1], cols[:, n:n + 1], cols[:, 2:3], ALU.mult).then_inc(pre, 1)
            v.wait_ge(pre, 2)
            for q in range(2 * NCH):
                layer, c = q // NCH, q % NCH
                v.wait_ge(mm, q + 1)
                if q >= 2:
                    v.wait_ge(sined, q - 1)
                st.link(v.tensor_scalar(x[:, q % 2], kp[:, c % 2, 0, :], cols[:, 2:3], fb[:, layer:layer + 1],
                                        ALU.mult, ALU.add))
                st.link(v.tensor_scalar(k[:], x[:, q % 2], 1.0 / TWO_PI, MAGIC, ALU.mult, ALU.add))
                st.link(v.tensor_scalar(k[:], k[:], -MAGIC, None, ALU.add))
                st.link(v.scalar_tensor_tensor(out=r[:, q % 2], in0=k[:], scalar=-C1, in1=x[:, q % 2], op0=ALU.mult,
                                               op1=ALU.add))
                st.link(v.scalar_tensor_tensor(out=r[:, q % 2], in0=k[:], scalar=-C2, in1=r[:, q % 2], op0=ALU.mult,
                                               op1=ALU.add))
                v.tensor_scalar(r[:, q % 2], r[:, q % 2], 3.1415925, -3.1415925, ALU.min, ALU.max).then_inc(sarg, 1)
                v.wait_ge(sarg, q + 1)
            v.wait_ge(sined, 2 * NCH)
            v.memset(h2[HID:F2, 0:1], 0.0).then_inc(pre, 1)
            v.wait_ge(pre, 3)
            v.wait_ge(zeroed, 3)

            hv = h2[:].rearrange("p (a b) -> p a b", b=N2)

            def stationary(i, n, first):
                if not first:
                    v.wait_ge(kmm, i * 2 + (n - 1))
                v.tensor_copy(stat[0:HID, n, 0:HID], hv[0:HID, :, bass.ds(i * 2 + n, 1)]).then_inc(step, 1)
                v.tensor_copy(stat[HID:F2, n, HID:P], hv[HID:F2, :, bass.ds(i * 2 + n, 1)]).then_inc(statd, 1)

            def windowed(i, n, first):
                if not first:
                    v.wait_ge(tmm, i * 2 + (n - 1))
                v.wait_ge(kmm, i * 2 + (n + 1))
                v.wait_ge(wind, i * 2 + (n + 1))
                for o in range(ORDER):
                    last = v.tensor_tensor(kf[:, n, o], kp[:, n, o, :], win[:, n], ALU.mult)
                last.then_inc(kfd, 1)

            for n in range(2):
                stationary(0, n, True)
            for n in range(2):
                windowed(0, n, True)
            with v.Fori(1, N2 // 2) as i:
                for n in range(2):
                    stationary(i, n, False)
                for n in range(2):
                    windowed(i, n, False)

        @block.scalar
        def _(s):
            for q in range(2 * NCH):
                layer, c = q // NCH, q % NCH
                s.wait_ge(sarg, q + 1)
                s.activation((h1, h2)[layer][:, c * BANK:(c + 1) * BANK], r[:, q % 2], ACT.Sin).then_inc(sined, 1)

            def step_(i, n, first):
                if not first:
                    s.wait_ge(kfd, i * 2 + (n - 1))
                s.wait_ge(small_in, 16 * 15)
                s.activation(win[:, n], drow[:], ACT.Exp, scale=tcol[:, bass.ds(i * 2 + n, 1)]).then_inc(wind, 1)

            def evac(i, n, first):
                if not first:
                    s.wait_ge(st_out[n], i * 16)
                s.wait_ge(tmm, i * 2 + (n + 1))
                s.activation(tb[:, n], tp[:, n], ACT.Copy).then_inc(tev, 1)

            for n in range(2):
                step_(0, n, True)
            for n in range(2):
                evac(0, n, True)
            with s.Fori(1, N2 // 2) as i:
                for n in range(2):
                    step_(i, n, False)
                for n in range(2):
                    evac(i, n, False)


def hyena_forward(nc, d, z, tag):
    NPAIR = N2 // 2
    with ExitStack() as ctx:
        sb, ps, sem = pools(nc, ctx)
        ident = sb(f"ident_{tag}", [P, P])
        zc = sb(f"zc_{tag}", [P, 2, CT, 2, NB1])
        zs = sb(f"zs_{tag}", [P, 2, DH])
        f1 = sb(f"f1z_{tag}", [P, 2, 2, P])
        tb = sb(f"tz_sb_{tag}", [P, 2, 2, DH])
        zt = ps(f"zt_ps_{tag}", [P, 2, DH])
        tp = ps(f"tz_ps_{tag}", [P, 2, 2, DH])
        small_in, zeroed = sem(f"zf_in_{tag}"), sem(f"zf_zero_{tag}")
        f1_in = [sem(f"zf_f10_{tag}"), sem(f"zf_f11_{tag}")]
        st_out = [sem(f"zf_st0_{tag}"), sem(f"zf_st1_{tag}")]
        picked, turned, zsd, tmm, tev = [sem(f"zf_{n}_{tag}") for n in ("pick", "turn", "zs", "mm", "ev")]
        block = ctx.enter_context(nc.Block())
        zv = z[:].rearrange("p c (a b) -> p c b a", b=N2)

        def pairs(eng, body):
            for n in range(2):
                body(n, n, 0, True)
            with eng.Fori(1, NPAIR // 2) as i:
                for n in range(2):
                    body(i * 2 + n, n, i, False)

        @block.sync
        def _(sp):
            sp.dma_start(ident[:], d.ident).then_inc(small_in, 16)

            def load(p, n):
                for k in range(2):
                    sp.dma_start(f1[k * NB1:(k + 1) * NB1, n, k],
                                 d.f1[bass.ds(p * 2 + k, 1), 0:NB1].rearrange("a p m -> (a p) m")).then_inc(f1_in[n], 16)

            def store(p, n):
                sp.wait_ge(tev, p + 1)
                sp.dma_start(d.Tz[:, bass.ds(p * 2, 2), :], tb[:, n]).then_inc(st_out[n], 16)

            sp.wait_ge(zeroed, 1)
            for n in range(2):
                load(n, n)
            with sp.Fori(1, NPAIR // 2) as i:
                for n in range(2):
                    sp.wait_ge(tmm, i * 2 + (n - 1))
                    load(i * 2 + n, n)
                    store(i * 2 + (n - 2), n)
            for n in range(2):
                store(NPAIR - 2 + n, n)
            for n in range(2):
                sp.wait_ge(st_out[n], 16 * (NPAIR // 2))

        @block.scalar
        def _(s):
            def evac(p, n, h, first):
                s.wait_ge(tmm, p + 1)
                if not first:
                    s.wait_ge(st_out[n], h * 16)
                s.activation(tb[:, n], tp[:, n], ACT.Copy).then_inc(tev, 1)

            pairs(s, evac)

        @block.gpsimd
        def _(g):
            def pick(p, n, h, first):
                if not first:
                    g.wait_ge(turned, p - 1)
                for k in range(2):
                    last = g.tensor_copy(zc[:, n, :, k, :], zv[:, :, bass.ds(p * 2 + k, 1), :]
                                         .rearrange("p c o a -> p c (o a)"))
                last.then_inc(picked, 1)

            g.memset(f1[:], 0.0).then_inc(zeroed, 1)
            pairs(g, pick)

        @block.tensor
        def _(pe):
            pe.wait_ge(small_in, 16)

            def turn(p, n):
                pe.wait_ge(picked, p + 1)
                for c in range(CT):
                    last = pe.transpose(zt[:, n, c * P:(c + 1) * P], zc[:, n, c].rearrange("p a b -> p (a b)"), ident[:])
                last.then_inc(turned, 1)

            def stage(p, n, h, first):
                if first and n == 0:
                    turn(0, 0)
                turn(p + 1, 1 - n)
                pe.wait_ge(zsd, p + 1)
                pe.wait_ge(f1_in[n], h * 32 + 32)
                if not first:
                    pe.wait_ge(tev, p - 1)
                for k in range(2):
                    last = pe.matmul(tp[:, n, k], f1[:, n, k], zs[:, n], start=True, stop=True)
                last.then_inc(tmm, 1)

            for n in range(2):
                stage(n, n, 0, True)
            with pe.Fori(1, NPAIR // 2 - 1) as i:
                for n in range(2):
                    stage(i * 2 + n, n, i, False)
            stage(NPAIR - 2, 0, NPAIR // 2 - 1, False)
            pe.wait_ge(zsd, NPAIR)
            pe.wait_ge(f1_in[1], 16 * NPAIR)
            pe.wait_ge(tev, NPAIR - 2)
            for k in range(2):
                last = pe.matmul(tp[:, 1, k], f1[:, 1, k], zs[:, 1], start=True, stop=True)
            last.then_inc(tmm, 1)

        @block.vector
        def _(v):
            def evac(p, n, h, first):
                v.wait_ge(turned, p + 1)
                if not first:
                    v.wait_ge(tmm, p - 1)
                v.tensor_copy(zs[:, n], zt[:, n]).then_inc(zsd, 1)

            pairs(v, evac)


def hyena_spectrum(nc, d, z, zb, gate, g1, o, tag):
    NS = N2 + 1
    NBUF = 4
    with ExitStack() as ctx:
        sb, ps, sem = pools(nc, ctx)
        (m2, m2l), m2h = split_pair(nc, ctx, f"m2_{tag}", [P, 15, P]), sb(f"m2h_{tag}", [P, 15, P], F32R)
        (io, iol), ioh = split_pair(nc, ctx, f"io_{tag}", [P, NBUF, 2, DH]), sb(f"ioh_{tag}", [P, NBUF, 2, DH], F32R)
        hb = sb(f"hb_{tag}", [P, CT])
        ks = sb(f"ks_{tag}", [P, 2, 2, DH])
        m = sb(f"prod_{tag}", [P, 2, 2, DH])
        pr = sb(f"spec_{tag}", [P, 2, DH])
        prh, prl = [sb(f"spec_{n}_{tag}", [P, 2, DH], F32R) for n in ("hi", "lo")]
        vb = sb(f"v_sb_{tag}", [P, 2, DH])
        za = ps(f"za_ps_{tag}", [P, 2, 2, DH])
        ka = ps(f"ka_ps_{tag}", [P, 2, DH])
        vp = ps(f"v_ps_{tag}", [P, 2, DH])
        m2_in = sem(f"sp_m2_{tag}")
        in_ = [sem(f"sp_in{n}_{tag}") for n in range(NBUF)]
        late_in, hb_in, zbd = sem(f"sp_late_{tag}"), sem(f"sp_hb_{tag}"), sem(f"sp_zb_{tag}")
        st_out = [sem(f"sp_st0_{tag}"), sem(f"sp_st1_{tag}")]
        m2hd, m2ld, iohd, zld, kld, fwd, kmm, ksd, mul, prd, prhd, prld, inv, vev = [
            sem(f"sp_{n}_{tag}") for n in ("m2h", "m2l", "ioh", "zl", "kl", "fwd", "kmm", "ks", "mul", "pr", "prh", "prl",
                                           "inv", "vev")]
        zt = d.Tz.rearrange("(b j) n c -> b (j n) c", j=4)
        kt = d.Tk[o].rearrange("(b j) n c -> b (j n) c", j=4)
        vt = d.V.rearrange("(b j) n c -> b (j n) c", j=4)
        block = ctx.enter_context(nc.Block())
        VAR = {0: (1, 0, P // 2), 1: (2, P // 2, P)}
        LEAD = NBUF + 1

        def steps(eng, body):
            for q in range(LEAD):
                body(q, q % NBUF, q // NBUF)
            with eng.Fori(1, NS // NBUF - 1) as i:
                for k in range(1, NBUF + 1):
                    body(i * NBUF + k, k % NBUF, i + k // NBUF)
            for q in range(NS - NBUF, NS):
                body(q, q % NBUF, q // NBUF)

        def known(q):
            return isinstance(q, int)

        def at(b, r, by):
            return (b + by) % NBUF, r + (b + by) // NBUF

        @block.sync
        def _(sp):
            sp.dma_start(m2[:], d.m2).then_inc(m2_in, 16)

            def load(q, b, r):
                if not known(q) or q >= NBUF:
                    sp.wait_ge(kmm, q + (1 - NBUF))
                row = max(q - 1, 0) if known(q) else q - 1
                for k, src in enumerate((zt, kt)):
                    sp.dma_start(io[:, b, k], src[bass.ds(row, 1)].rearrange("a p c -> (a p) c")).then_inc(in_[b], 16)
                if known(q) and q in (1, 3, NS - 4, NS - 2):
                    c = (1, 3, NS - 4, NS - 2).index(q)
                    sp.dma_start(gate[:, c], d.uT[CT * (o + 1) + c]).then_inc(late_in, 16)

            steps(sp, load)
            if o == 0:
                sp.dma_start(g1[:], d.g1).then_inc(late_in, 16)
            sp.wait_ge(late_in, 16 * (CT + (o == 0)))

        @block.gpsimd
        def _(g):
            with nc.allow_non_contiguous_dma(reason="bias as columns"):
                g.dma_start(hb[:], d.hy_bias[o].rearrange("(j p) -> p j", p=P)).then_inc(hb_in, 16)

            def trail(q, b):
                g.wait_ge(iohd, q + 1)
                g.tensor_tensor(iol[:, b, 1], io[:, b, 1], ioh[:, b, 1].bitcast(F32), ALU.subtract).then_inc(kld, 1)

            def store(q, b, r):
                g.wait_ge(vev, q + 1)
                lo, hi = VAR[q][1:] if known(q) and q in VAR else (0, P)
                row = max(q - 1, 0) if known(q) else q - 1
                g.dma_start(vt[bass.ds(row, 1), lo:hi].rearrange("a p c -> (a p) c"), vb[lo:hi, b % 2])\
                    .then_inc(st_out[b % 2], 16)

            def step(q, b, r):
                if not known(q) or q < NS - 2:
                    trail(q + 2, at(b, r, 2)[0])
                if not known(q) or q >= 2:
                    store(q - 2, *at(b, r, -2))

            for q in range(2):
                trail(q, q)
            steps(g, step)
            for q in range(NS - 2, NS):
                store(q, q % NBUF, q // NBUF)
            g.wait_ge(st_out[0], 16 * (NS // 2 + 1))
            g.wait_ge(st_out[1], 16 * (NS // 2))

        @block.tensor
        def _(pe):
            pe.wait_ge(m2ld, 1)

            def product(out, k, hi, lo):
                pe.matmul(out, m2h[:, k], hi, start=True, stop=False)
                pe.matmul(out, m2h[:, k], lo, start=False, stop=False)
                return pe.matmul(out, m2l[:, k], hi, start=False, stop=True)

            def forward(q, b, r):
                v = VAR[q][0] if known(q) and q in VAR else 0
                pe.wait_ge(zld, q + 1)
                if not known(q) or q >= 2:
                    pe.wait_ge(mul, q - 1)
                for k in range(2):
                    last = product(za[:, b % 2, k], v * 5 + k, ioh[:, b, 0], iol[:, b, 0])
                last.then_inc(fwd, 1)
                pe.wait_ge(kld, q + 1)
                if not known(q) or q >= 1:
                    pe.wait_ge(ksd, q)
                for k in range(2):
                    last = product(ka[:, k], v * 5 + 2 + k, ioh[:, b, 1], iol[:, b, 1])
                last.then_inc(kmm, 1)

            def inverse(q, b, r):
                v = VAR[q][0] if known(q) and q in VAR else 0
                pe.wait_ge(prld, q + 1)
                if not known(q) or q >= 2:
                    pe.wait_ge(vev, q - 1)
                product(vp[:, b % 2], v * 5 + 4, prh[:, b % 2], prl[:, b % 2]).then_inc(inv, 1)

            def both(q, b, r):
                forward(q, b, r)
                if not known(q) or q >= 2:
                    inverse(q - 2, *at(b, r, -2))

            steps(pe, both)
            for q in range(NS - 2, NS):
                inverse(q, q % NBUF, q // NBUF)

        @block.scalar
        def _(s):
            s.wait_ge(m2_in, 16)
            s.activation(m2h[:], m2[:], ACT.Copy).then_inc(m2hd, 1)

            def lead(q, b, r):
                s.wait_ge(in_[b], r * 32 + 32)
                s.activation(ioh[:, b], io[:, b], ACT.Copy).then_inc(iohd, 1)

            def evac(q, b, r):
                s.wait_ge(inv, q + 1)
                if not known(q) or q >= 2:
                    s.wait_ge(st_out[b % 2], r * 32 + b // 2 * 16)
                s.activation(vb[:, b % 2], vp[:, b % 2], ACT.Copy).then_inc(vev, 1)

            def step(q, b, r):
                s.wait_ge(kmm, q + 1)
                if not known(q) or q >= 2:
                    s.wait_ge(mul, q - 1)
                s.activation(ks[:, b % 2], ka[:], ACT.Copy).then_inc(ksd, 1)
                if not known(q) or q < NS - 2:
                    lead(q + 2, *at(b, r, 2))
                if not known(q) or q >= 2:
                    evac(q - 2, *at(b, r, -2))
                s.wait_ge(prd, q + 1)
                if not known(q) or q >= 2:
                    s.wait_ge(inv, q - 1)
                s.activation(prh[:, b % 2], pr[:, b % 2], ACT.Copy).then_inc(prhd, 1)
                if known(q) and q == LEAD - 1:
                    s.wait_ge(hb_in, 16)
                    for c in range(CT):
                        s.activation(zb[:, c], z[:, c], ACT.Copy, scale=hb[:, c:c + 1]).then_inc(zbd, 1)

            for q in range(2):
                lead(q, q, 0)
            steps(s, step)
            for q in range(NS - 2, NS):
                evac(q, q % NBUF, q // NBUF)
            s.wait_ge(zbd, CT)

        @block.vector
        def _(v):
            v.wait_ge(m2hd, 1)
            v.tensor_tensor(m2l[:], m2[:], m2h[:].bitcast(F32), ALU.subtract).then_inc(m2ld, 1)

            def trail(q, b):
                v.wait_ge(iohd, q + 1)
                v.tensor_tensor(iol[:, b, 0], io[:, b, 0], ioh[:, b, 0].bitcast(F32), ALU.subtract).then_inc(zld, 1)

            def step(q, b, r):
                n = b % 2
                v.wait_ge(fwd, q + 1)
                v.wait_ge(ksd, q + 1)
                v.tensor_tensor(m[:, n], za[:, n], ks[:, n], ALU.mult).then_inc(mul, 1)
                v.wait_ge(mul, q + 1)
                if not known(q) or q >= 2:
                    v.wait_ge(prld, q - 1)
                v.tensor_tensor(pr[:, n], m[:, n, 0], m[:, n, 1], ALU.add).then_inc(prd, 1)
                if not known(q) or q < NS - 2:
                    trail(q + 2, at(b, r, 2)[0])
                v.wait_ge(prhd, q + 1)
                if not known(q) or q >= 2:
                    v.wait_ge(inv, q - 1)
                v.tensor_tensor(prl[:, n], pr[:, n], prh[:, n].bitcast(F32), ALU.subtract).then_inc(prld, 1)

            for q in range(2):
                trail(q, q)
            steps(v, step)


def hyena_inverse(nc, d, z, zb, gate, g1, tag):
    with ExitStack() as ctx:
        sb, ps, sem = pools(nc, ctx)
        vi = sb(f"vi_{tag}", [P, 4, 2, DH])
        tmp = sb(f"y_tmp_{tag}", [P, 2, 2, CT, NB1])
        yp = ps(f"y_ps_{tag}", [P, 2, 2, CT, NB1])
        v_in = [sem(f"hi_v{n}_{tag}") for n in range(4)]
        mm, added, gated = [sem(f"hi_{n}_{tag}") for n in ("mm", "add", "gate_done")]
        ND = N2 // 2
        block = ctx.enter_context(nc.Block())

        @block.sync
        def _(sp):
            for k in range(4):
                sp.dma_start(vi[:, k], d.V[:, 2 * k:2 * k + 2, :]).then_inc(v_in[k], 16)
            with sp.Fori(1, ND // 4) as i:
                for k in range(4):
                    sp.wait_ge(mm, i * 4 + (k - 3))
                    sp.dma_start(vi[:, k], d.V[:, bass.ds(i * 8 + 2 * k, 2), :]).then_inc(v_in[k], 16)

        @block.tensor
        def _(pe):
            def pair(i, k, first):
                n = k % 2
                pe.wait_ge(v_in[k], i * 16 + 16)
                if not first or k >= 2:
                    pe.wait_ge(added, i * 4 + (k - 1))
                for a in range(2):
                    for c in range(CT):
                        last = pe.matmul(yp[:, n, a, c, :], vi[:, k, a, c * P:(c + 1) * P],
                                         g1[:, bass.ds(i * 8 + (2 * k + a), 1), :], start=True, stop=True)
                last.then_inc(mm, 1)

            for k in range(4):
                pair(0, k, True)
            with pe.Fori(1, ND // 4) as i:
                for k in range(4):
                    pair(i, k, False)

        @block.vector
        def _(v):
            zv, bv, gv = [t[:].rearrange("p c (a b) -> p c a b", b=N2) for t in (z, zb, gate)]
            with v.Fori(0, ND // 2) as i:
                for n in range(2):
                    v.wait_ge(mm, i * 2 + (n + 1))
                    for k in range(2):
                        last = v.tensor_tensor(tmp[:, n, k], yp[:, n, k], bv[:, :, :, bass.ds(i * 4 + (2 * n + k), 1)],
                                               ALU.add)
                    last.then_inc(added, 1)
                    v.wait_ge(added, i * 2 + (n + 1))
                    for k in range(2):
                        at = bass.ds(i * 4 + (2 * n + k), 1)
                        last = v.tensor_tensor(zv[:, :, :, at], tmp[:, n, k], gv[:, :, :, at], ALU.mult)
                    last.then_inc(gated, 1)
            v.wait_ge(gated, ND)


def hyena(nc, d, z):
    hyena_filters(nc, d, z)
    with ExitStack() as ctx:
        zb, gate = [ctx.enter_context(nc.sbuf_tensor(f"{n}_hy", [P, CT, L], F32)) for n in ("zb", "gate")]
        g1 = ctx.enter_context(nc.sbuf_tensor("g1_hy", [P, N2, NB1], F32))
        for o in range(ORDER):
            hyena_forward(nc, d, z, f"a{o}")
            hyena_spectrum(nc, d, z, zb, gate, g1, o, f"b{o}")
            hyena_inverse(nc, d, z, zb, gate, g1, f"c{o}")


def ssd_weights(nc, d, dta, cum, wend, dec):
    NB = 2 * HEADS
    with ExitStack() as ctx:
        sb, ps, sem = pools(nc, ctx)
        tri = sb("tri", [P, 5, P])
        ident = sb("ident_w", [P, P])
        cT = sb("cum_T", [P, 3, P])
        cp = ps("cum_ps", [P, BANK])
        ep = ps("end_ps", [P, BANK])
        tp = ps("tot_ps", [P, BANK])
        ct = ps("cumT_ps", [P, 3, P])
        ins, mm, cumd, turned, wstep, out_done, evd = (sem("sw_in"), sem("sw_mm"), sem("sw_cum"), sem("sw_turn"),
                                                       sem("sw_step"), sem("sw_out"), sem("sw_ev"))
        block = ctx.enter_context(nc.Block())
        W = NT * NB

        @block.sync
        def _(sp):
            sp.dma_start(tri[:], d.tri).then_inc(ins, 16)
            sp.dma_start(ident[:], d.ident).then_inc(ins, 16)
            sp.dma_start(dta[:], d.dt_a).then_inc(ins, 16)
            sp.wait_ge(evd, 1)
            for k in range(3):
                rows = min(P, W - k * P)
                sp.dma_start(d.cumT[k * P:k * P + rows, :], cT[0:rows, k, :]).then_inc(out_done, 16)
            sp.wait_ge(out_done, 48)

        @block.tensor
        def _(pe):
            pe.wait_ge(ins, 48)
            av = dta[:, 1]
            for k, (acc, lo) in enumerate(((cp, 0), (cp, HEADS), (ep, 0), (ep, HEADS))):
                v = acc[:, 0:W].rearrange("p (t h) -> p t h", h=NB)[:, :, lo:lo + HEADS]
                pe.matmul(v, tri[:, k, :], av[:, :, lo:lo + HEADS], start=True, stop=True)
            pe.matmul(tp[:, 0:W], tri[:, 4, :], av.rearrange("p t h -> p (t h)"), start=True, stop=True).then_inc(mm, 1)
            pe.wait_ge(cumd, 1)
            for k in range(3):
                rows = min(P, W - k * P)
                last = pe.transpose(ct[0:rows, k, :], cum[:].rearrange("p t h -> p (t h)")[:, k * P:k * P + rows],
                                    ident[:])
            last.then_inc(turned, 1)

        @block.vector
        def _(v):
            v.wait_ge(mm, 1)
            v.tensor_copy(cum[:].rearrange("p t h -> p (t h)"), cp[:, 0:W]).then_inc(cumd, 1)
            v.wait_ge(wstep, 1)
            v.tensor_tensor(wend[:], wend[:], dta[:, 0], ALU.mult).then_inc(wstep, 1)
            v.wait_ge(turned, 1)
            v.tensor_copy(cT[:, 0:2], ct[:, 0:2])
            v.tensor_copy(cT[0:W - 2 * P, 2], ct[0:W - 2 * P, 2]).then_inc(evd, 1)

        @block.scalar
        def _(s):
            s.wait_ge(mm, 1)
            s.activation(dec[:].rearrange("p t h -> p (t h)"), tp[:, 0:W], ACT.Exp)
            s.activation(wend[:].rearrange("p t h -> p (t h)"), ep[:, 0:W], ACT.Exp).then_inc(wstep, 1)


def ssd_states(nc, d, H, dirn, wend, dec, lead, many, tag):
    N = len(lead) + (NTX if many else 0)
    W = D_SSD
    with ExitStack() as ctx:
        sb, ps, sem = pools(nc, ctx)
        ident = sb(f"ident_{tag}", [P, P])
        ch = sb(f"ch_{tag}", [P, 2, 6, P])
        bn = sb(f"bn_{tag}", [P, 2, 2 * P])
        xw = sb(f"xw_{tag}", [P, 2, W])
        th = sb(f"th_{tag}", [P, W])
        xp = ps(f"xp_{tag}", [P, 2, W])
        bp = ps(f"bp_{tag}", [P, 2, W])
        sp_ = ps(f"s_{tag}", [P, 2, W])
        small_in = sem(f"st_small_{tag}")
        in_ = [sem(f"st_in0_{tag}"), sem(f"st_in1_{tag}")]
        tp, bnd, xwd, smm, thd, hd = [sem(f"st_{n}_{tag}") for n in ("tp", "bn", "xw", "smm", "th", "h")]
        h_out = [sem(f"st_h0_{tag}"), sem(f"st_h1_{tag}")]
        block = ctx.enter_context(nc.Block())
        h0 = dirn * HEADS

        def run(eng, body):
            for k, c in enumerate(lead):
                body(k, k % 2, 0, c, False)
            if many:
                with eng.Fori(1, N // 2) as i:
                    for n in range(2):
                        body(i * 2 + n, n, i, eng.snap(i * -2 + (NT + 1 - n)), True)

        @block.sync
        def _(sp):
            sp.dma_start(ident[:], d.ident).then_inc(small_in, 16)
            src = d.sT.rearrange("j p t -> p j t")

            def step(k, n, h, c, many_):
                if many_:
                    sp.wait_ge(tp, k - 1)
                at = bass.ds(c * P, P)
                sp.dma_start(ch[:, n], src[:, 0:6, at]).then_inc(in_[n], 16)

            run(sp, step)

        if many:
            @block.gpsimd
            def _(g):
                def step(k, n, h, c, many_):
                    g.wait_ge(hd, k + 1)
                    g.dma_start(d.Hb[bass.ds(c, 1)].rearrange("a p w -> (a p) w"), H[:, n]).then_inc(h_out[n], 16)

                run(g, step)
                for n in range(2):
                    g.wait_ge(h_out[n], 16 * (NT // 2))

        @block.tensor
        def _(pe):
            def turn(k, n, h, some):
                pe.wait_ge(in_[n], h * 16 + 16)
                if some:
                    pe.wait_ge(xwd, k - 1)
                    pe.wait_ge(bnd, k - 1)
                pe.wait_ge(small_in, 16)
                for j in range(4):
                    pe.transpose(xp[:, n, j * P:(j + 1) * P], ch[:, n, j, :], ident[:])
                for j in range(2):
                    last = pe.transpose(bp[:, n, j * P:(j + 1) * P], ch[:, n, 4 + j, :], ident[:])
                last.then_inc(tp, 1)

            def states(k, n, some):
                pe.wait_ge(xwd, k + 1)
                pe.wait_ge(bnd, k + 1)
                if some:
                    pe.wait_ge(hd, k)
                for g in range(2):
                    last = pe.matmul(sp_[:, n, g * (W // 2):(g + 1) * (W // 2)], bn[:, n, g * P:(g + 1) * P],
                                     xw[:, n, g * (W // 2):(g + 1) * (W // 2)], start=True, stop=True)
                last.then_inc(smm, 1)

            turn(0, 0, 0, False)
            turn(1, 1, 0, False)
            states(0, 0, False)
            if many:
                with pe.Fori(1, N // 2) as i:
                    for n in range(2):
                        turn(i * 2 + n, n, i, True)
                        states(i * 2 + (n - 1), 1 - n, True)
            states(N - 1, 1, many)

        @block.scalar
        def _(s):
            def step(k, n, h, c, many_):
                s.wait_ge(tp, k + 1)
                if many_:
                    s.wait_ge(smm, k - 1)
                s.activation(bn[:, n], bp[:, n, 0:2 * P], ACT.Copy).then_inc(bnd, 1)

            run(s, step)

        @block.vector
        def _(v):
            v.memset(H[:, 0], 0.0).then_inc(hd, 1)

            def step(k, n, h, c, many_):
                v.wait_ge(tp, k + 1)
                if many_:
                    v.wait_ge(smm, k - 1)
                hs = [t[:, bass.ds(c, 1), h0:h0 + HEADS].rearrange("p a h -> p (a h)").unsqueeze(2)
                      .broadcast_to([P, HEADS, HD]) for t in (wend, dec)]
                v.tensor_tensor(xw[:, n].rearrange("p (h q) -> p h q", q=HD),
                                xp[:, n].rearrange("p (h q) -> p h q", q=HD), hs[0], ALU.mult).then_inc(xwd, 1)
                v.wait_ge(hd, k + 1)
                v.tensor_tensor(th[:].rearrange("p (h q) -> p h q", q=HD),
                                H[:, n].rearrange("p (h q) -> p h q", q=HD), hs[1], ALU.mult).then_inc(thd, 1)
                v.wait_ge(thd, k + 1)
                v.wait_ge(smm, k + 1)
                if many and (many_ or k > 0):
                    v.wait_ge(h_out[1 - n], (h + n) * 16)
                v.tensor_tensor(H[:, 1 - n], th[:], sp_[:, n], ALU.add).then_inc(hd, 1)

            run(v, step)


def ssd_main(nc, d, H, y, cum, wend, dec):
    W = D_SSD
    NB = 2 * HEADS
    NBUF = 4
    with ExitStack() as ctx:
        sb, ps, sem = pools(nc, ctx)
        ident = sb("ident_m", [P, P])
        mask = sb("mask_m", [P, 2, P])
        dta = sb("dta_m", [P, NT, NB])
        dsk = sb("dskip_m", [P, CT])
        ch = sb("ch_m", [P, NBUF, 8, P])
        zc = sb("z_m", [P, NBUF, CT, P])
        bc = sb("bc_m", [P, NBUF, NB, P])
        hb = sb("hb_m", [P, NBUF, W])
        xn, bn = sb("xn_m", [P, 2, W]), sb("bn_m", [P, 2, 2 * P])
        E = sb("E_m", [P, NB, P])
        Wt = sb("W_m", [P, 2, HEADS, P])
        eb = sb("eb_m", [P, 2, NB, P])
        cs = sb("cs_m", [P, 2, NB, P])
        xw, th = sb("xw_m", [P, 2, W]), sb("th_m", [P, W])
        yt = sb("yt_m", [P, CT, P])
        xp = ps("xp_m", [P, 2, W])
        bp = ps("bp_m", [P, W])
        cbp = ps("cb_m", [P, 2, W])
        s_ps = ps("s_m", [P, W])
        yp = ps("yp_m", [P, 2, CT, P])
        small_in, dsk_in = sem("sm_small"), sem("sm_dsk")
        in_ = [sem(f"sm_in{n}") for n in range(NBUF)]
        tp, xnd, bnd, segd, expd, ebd, csd, xwd, smm, hd, wd, ymm, ytd, yd, vstep, thd = [
            sem(f"sm_{n}") for n in ("tp", "xn", "bn", "seg", "exp", "eb", "cs", "xw", "smm", "h", "w", "ymm", "yt", "y",
                                     "step", "th")]
        block = ctx.enter_context(nc.Block())

        def chunks(eng, body):
            for k in range(NBUF):
                body(k, k % 2, (0, k), k < 2)
            with eng.Fori(1, NTX // NBUF) as i:
                for k in range(NBUF):
                    body(i * NBUF + k, k % 2, (i, k), False)

        def spread(t, k, lo, inner):
            return t[:, bass.ds(k + NTC, 1), lo:lo + HEADS].rearrange("p a h -> p (a h)").unsqueeze(2)\
                .broadcast_to([P, HEADS, inner])

        @block.sync
        def _(sp):
            sp.dma_start(ident[:], d.ident).then_inc(small_in, 16)
            sp.dma_start(mask[:], d.mask).then_inc(small_in, 16)
            sp.dma_start(dta[:], d.dt_a[:, 0]).then_inc(small_in, 16)

            def step(k, n, h, first):
                h, b = h
                if not isinstance(k, int) or k >= NBUF:
                    sp.wait_ge(yd, k + (1 - NBUF))
                    sp.wait_ge(csd, k + (1 - NBUF))
                    sp.wait_ge(segd, k * 2 + (2 - 2 * NBUF))
                sp.dma_start(ch[:, b], d.sT.rearrange("j p t -> p j t")[:, :, bass.ds(LC + k * P, P)])\
                    .then_inc(in_[b], 16)
                sp.dma_start(zc[:, b], d.zT.rearrange("j p t -> p j t")[:, :, bass.ds(k * P, P)]).then_inc(in_[b], 16)
                sp.dma_start(bc[:, b].rearrange("p a b -> p (a b)"),
                             d.cumT[bass.ds((k + NTC) * NB, NB), :].rearrange("(o a) b -> o (a b)", o=1)
                             .broadcast_to([P, NB * P])).then_inc(in_[b], 16)
                sp.dma_start(hb[:, b], d.Hb[bass.ds(k + NTC, 1)].rearrange("a p w -> (a p) w")).then_inc(in_[b], 16)

            chunks(sp, step)

        @block.gpsimd
        def _(g):
            for c in range(CT):
                for a in range(2):
                    g.dma_start(dsk[a * HD:(a + 1) * HD, c:c + 1],
                                d.ssd_d[2 * c + a:2 * c + a + 1].rearrange("(o a) -> o a", o=1).broadcast_to([HD, 1]))\
                        .then_inc(dsk_in, 16)

            def step(k, n, h, first):
                g.wait_ge(ebd, k + 1)
                if not first:
                    g.wait_ge(ymm, k - 1)
                cv = cs[:, n].rearrange("p (v h) t -> p v h t", v=2)
                ev = eb[:, n].rearrange("p (v h) t -> p v h t", v=2)
                for q in range(2):
                    hs = slice(q * HPG, (q + 1) * HPG)
                    c_ = ch[:, h[1], 6 + q, :].unsqueeze(1).unsqueeze(1).broadcast_to([P, 2, HPG, P])
                    last = g.tensor_tensor(cv[:, :, hs, :], ev[:, :, hs, :], c_, ALU.mult)
                last.then_inc(csd, 1)
                g.wait_ge(hd, k + 1)
                g.tensor_tensor(th[:].rearrange("p (h q) -> p h q", q=HD),
                                H[:, n].rearrange("p (h q) -> p h q", q=HD), spread(dec, k, 0, HD), ALU.mult)\
                    .then_inc(thd, 1)
                g.wait_ge(xnd, k + 1)
                if not first:
                    g.wait_ge(smm, k - 1)
                g.tensor_tensor(xw[:, n].rearrange("p (h q) -> p h q", q=HD),
                                xn[:, n].rearrange("p (h q) -> p h q", q=HD), spread(wend, k, 0, HD), ALU.mult)\
                    .then_inc(xwd, 1)

            chunks(g, step)

        @block.tensor
        def _(pe):
            pe.wait_ge(small_in, 16 * 3)

            def turn(k, n, h, first):
                pe.wait_ge(in_[h[1]], h[0] * 64 + 64)
                if not first:
                    pe.wait_ge(xnd, k - 1)
                    pe.wait_ge(wd, k - 1)
                if not first or k > 0:
                    pe.wait_ge(bnd, k)
                pe.wait_ge(small_in, 16 * 3)
                for j in range(4):
                    pe.transpose(xp[:, n, j * P:(j + 1) * P], ch[:, h[1], j, :], ident[:])
                for j in range(2):
                    pe.transpose(bp[:, j * P:(j + 1) * P], ch[:, h[1], 4 + j, :], ident[:])
                for j in range(2):
                    last = pe.matmul(cbp[:, n, j * P:(j + 1) * P], ch[:, h[1], 4 + j, :], ch[:, h[1], 6 + j, :],
                                     start=True, stop=True)
                last.then_inc(tp, 1)

            def out(k, n, b, first):
                pe.wait_ge(wd, k + 1)
                pe.wait_ge(csd, k + 1)
                pe.wait_ge(xnd, k + 1)
                pe.wait_ge(hd, k + 1)
                if not first:
                    pe.wait_ge(ytd, k)
                for a in range(HEADS):
                    dst = yp[(a % 2) * HD:(a % 2 + 1) * HD, n, a // 2, :]
                    hs = slice(a * HD, (a + 1) * HD)
                    pe.matmul(dst, xn[:, n, hs], Wt[:, n, a, :], start=True, stop=False, skip_group_check=True)
                    pe.matmul(dst, H[:, n, hs], cs[:, n, a, :], start=False, stop=False, skip_group_check=True)
                    last = pe.matmul(dst, hb[:, b, hs], cs[:, n, HEADS + a, :], start=False, stop=True,
                                     skip_group_check=True)
                last.then_inc(ymm, 1)

            def states(k, n):
                pe.wait_ge(xwd, k + 1)
                pe.wait_ge(bnd, k + 1)
                pe.wait_ge(hd, k + 1)
                for g in range(2):
                    hs = slice(g * (W // 2), (g + 1) * (W // 2))
                    last = pe.matmul(s_ps[:, hs], bn[:, n, g * P:(g + 1) * P], xw[:, n, hs], start=True, stop=True)
                last.then_inc(smm, 1)

            def step(k, n, h, first):
                turn(k, n, h, first)
                if not isinstance(k, int) or k:
                    out(k - 1, 1 - n, (h[1] - 1) % NBUF, isinstance(k, int) and k == 1)
                states(k, n)

            chunks(pe, step)
            out(NTX - 1, 1, NBUF - 1, False)

        @block.scalar
        def _(s):
            def decays(k, b, r):
                s.wait_ge(in_[b], r * 64 + 64)
                if not isinstance(k, int) or k >= 2:
                    s.wait_ge(csd, k - 1)
                s.activation(eb[:, b % 2], bc[:, b], ACT.Exp).then_inc(ebd, 1)

            def step(k, n, h, first):
                s.wait_ge(tp, k + 1)
                if not first:
                    s.wait_ge(ymm, k - 1)
                s.activation(xn[:, n], xp[:, n], ACT.Copy).then_inc(xnd, 1)
                if not first:
                    s.wait_ge(smm, k - 1)
                s.activation(bn[:, n], bp[:, 0:2 * P], ACT.Copy).then_inc(bnd, 1)
                if isinstance(k, int) or h[1] < NBUF - 1:
                    decays(k + 1, (h[1] + 1) % NBUF, h[0] + (h[1] + 1) // NBUF)
                else:
                    with s.If(h[0] < NTX // NBUF - 1):
                        decays(k + 1, 0, h[0] + 1)
                for v_ in range(2):
                    hs = slice(v_ * HEADS, (v_ + 1) * HEADS)
                    s.wait_ge(segd, k * 2 + (v_ + 1))
                    s.activation(E[:, hs], E[:, hs], ACT.Exp).then_inc(expd, 1)

            decays(0, 0, 0)
            chunks(s, step)

        @block.vector
        def _(v):
            v.wait_ge(small_in, 16 * 3)
            v.wait_ge(dsk_in, 16 * 2 * CT)

            def post(k, n, b, first):
                v.wait_ge(ymm, k + 1)
                if not first:
                    v.wait_ge(yd, k)
                for c in range(CT):
                    last = v.scalar_tensor_tensor(out=yt[:, c, :], in0=ch[:, b, c, :], scalar=dsk[:, c:c + 1],
                                                  in1=yp[:, n, c, :], op0=ALU.mult, op1=ALU.add)
                last.then_inc(ytd, 1)
                v.wait_ge(ytd, k + 1)
                v.tensor_tensor(y[:, :, bass.ds(k * P, P)], yt[:], zc[:, b], ALU.mult).then_inc(yd, 1)

            def step(k, n, h, first):
                v.wait_ge(in_[h[1]], h[0] * 64 + 64)
                if first is False or k:
                    v.wait_ge(wd, k)
                for a in range(NB):
                    last = v.scalar_tensor_tensor(out=E[:, a, :], in0=bc[:, h[1], a, :],
                                                  scalar=cum[:, bass.ds(k + NTC, 1), a], in1=mask[:, a // HEADS, :],
                                                  op0=ALU.subtract, op1=ALU.min)
                    if a % HEADS == HEADS - 1:
                        last.then_inc(segd, 1)
                for q in range(2):
                    v.wait_ge(expd, k * 2 + (q + 1))
                    last = v.tensor_tensor(E[:, q * HEADS:(q + 1) * HEADS, :], E[:, q * HEADS:(q + 1) * HEADS, :],
                                           spread(dta, k, q * HEADS, P), ALU.mult)
                last.then_inc(vstep, 1)
                if not isinstance(k, int) or k:
                    post(k - 1, 1 - n, (h[1] - 1) % NBUF, isinstance(k, int) and k == 1)
                v.wait_ge(vstep, k * 2 + 1)
                v.tensor_tensor(E[:, 0:HEADS, :], E[:, 0:HEADS, :], E[:, HEADS:NB, :], ALU.add).then_inc(vstep, 1)
                v.wait_ge(vstep, k * 2 + 2)
                if not first:
                    v.wait_ge(ymm, k - 1)
                for g in range(2):
                    hs = slice(g * HPG, (g + 1) * HPG)
                    cb = cbp[:, n, g * P:(g + 1) * P].unsqueeze(1).broadcast_to([P, HPG, P])
                    last = v.tensor_tensor(Wt[:, n, hs, :], E[:, hs, :], cb, ALU.mult)
                last.then_inc(wd, 1)

            def update(k, n):
                v.wait_ge(smm, k + 1)
                v.wait_ge(thd, k + 1)
                v.tensor_tensor(H[:, 1 - n], th[:], s_ps[:], ALU.add).then_inc(hd, 1)

            def both(k, n, h, first):
                step(k, n, h, first)
                update(k, n)

            v.sem_inc(hd, 1)
            chunks(v, both)
            post(NTX - 1, 1, NBUF - 1, False)
            v.wait_ge(yd, NTX)


def ssd_norm(nc, d, y, wo, wol, woh):
    with ExitStack() as ctx:
        sb, ps, sem = pools(nc, ctx)
        ones = sb("ones_n", [P, P])
        gn = sb("gn_n", [P, CT])
        sq = sb("sq_n", [P, 2, CT, BANK])
        ms = sb("ms_n", [P, 2, 2, BANK])
        ln, rs = sb("ln_n", [P, L // BANK, 2, BANK]), sb("rs_n", [P, L // BANK, 2, BANK])
        acc = ps("acc_n", [P, 2, 2, BANK])
        small_in, sqd, mm, msd, rtd, rcd, yd, whd, wld = [
            sem(f"sn_{n}") for n in ("in", "sq", "mm", "ms", "rt", "rc", "y", "wh", "wl")]
        w_in = [sem(f"sn_w{n}") for n in range(2)]
        NC4 = L // BANK
        block = ctx.enter_context(nc.Block())

        @block.sync
        def _(sp):
            sp.dma_start(ones[:], d.tri[:, 4, :]).then_inc(small_in, 16)
            with nc.allow_non_contiguous_dma(reason="norm weight as columns"):
                sp.dma_start(gn[:], d.ssd_norm_g.rearrange("(j p) -> p j", p=P)).then_inc(small_in, 16)
            for n in range(2):
                half = slice(n * DT // 2, (n + 1) * DT // 2)
                sp.dma_start(wo[:, half], d.w_out.rearrange("(j p) n -> p j n", p=P)[:, half]).then_inc(w_in[n], 16)

        @block.gpsimd
        def _(g):
            for n in range(2):
                half = slice(n * DT // 2, (n + 1) * DT // 2)
                g.wait_ge(whd, n + 1)
                g.tensor_tensor(wol[:, half], wo[:, half], woh[:, half].bitcast(F32), ALU.subtract).then_inc(wld, 1)

        @block.scalar
        def _(s):
            for c in range(NC4):
                if c >= 2:
                    s.wait_ge(mm, c - 1)
                s.activation(sq[:, c % 2], y[:, :, c * BANK:(c + 1) * BANK], ACT.Square).then_inc(sqd, 1)
            for n in range(2):
                half = slice(n * DT // 2, (n + 1) * DT // 2)
                s.wait_ge(w_in[n], 16)
                s.activation(woh[:, half], wo[:, half], ACT.Copy).then_inc(whd, 1)
            for c in range(NC4):
                s.wait_ge(msd, c + 1)
                s.activation(ln[:, c], ms[:, c % 2], ACT.Ln).then_inc(rtd, 1)
            for c in range(NC4):
                s.wait_ge(rtd, c + 1)
                s.activation(rs[:, c], ln[:, c], ACT.Exp, scale=-0.5).then_inc(rcd, 1)

        @block.tensor
        def _(pe):
            pe.wait_ge(small_in, 32)
            for c in range(NC4):
                pe.wait_ge(sqd, c + 1)
                if c >= 2:
                    pe.wait_ge(msd, c - 1)
                for g in range(2):
                    for j in range(2):
                        last = pe.matmul(acc[:, c % 2, g], ones[:], sq[:, c % 2, 2 * g + j], start=(j == 0), stop=(j == 1))
                last.then_inc(mm, 1)

        @block.vector
        def _(v):
            v.wait_ge(small_in, 32)
            for c in range(NC4):
                n = c % 2
                v.wait_ge(mm, c + 1)
                if c >= 2:
                    v.wait_ge(rtd, c - 1)
                v.tensor_scalar(ms[:, n], acc[:, n], 2.0 / D_SSD, EPS, ALU.mult, ALU.add).then_inc(msd, 1)
            for c in range(NC4):
                v.wait_ge(rcd, c + 1)
                for j in range(CT):
                    yv = y[:, j, c * BANK:(c + 1) * BANK]
                    last = v.scalar_tensor_tensor(out=yv, in0=yv, scalar=gn[:, j:j + 1], in1=rs[:, c, j // 2],
                                                  op0=ALU.mult, op1=ALU.mult)
                last.then_inc(yd, 1)
            v.wait_ge(yd, NC4)


def ssd(nc, d, y):
    NB = 2 * HEADS
    with ExitStack() as ctx:
        sb, _, _ = pools(nc, ctx)
        cum, wend, dec = sb("cum", [P, NT, NB]), sb("wend", [P, NT, NB]), sb("dec", [P, NT, NB])
        H = sb("H_state", [P, 2, D_SSD])
        with ExitStack() as inner:
            dta = inner.enter_context(nc.sbuf_tensor("dta_w", [P, 2, NT, NB], F32))
            ssd_weights(nc, d, dta, cum, wend, dec)
        ssd_states(nc, d, H, 1, wend, dec, [1, 0], True, "bwd")
        ssd_states(nc, d, H, 0, wend, dec, [0, 1], False, "fwd")
        ssd_main(nc, d, H, y, cum, wend, dec)


def out_proj(nc, d, z, y, wol, woh, logits):
    NR = MG + NE
    with ExitStack() as ctx:
        sb, ps, sem = pools(nc, ctx)
        wr = sb("w_router", [P, DT, NR])
        br = sb("b_router", [P, NR])
        ga, gs, sh = sb("gate1_row", [P, D]), sb("gs2_row", [P, D]), sb("sh2_row", [P, D])
        g2 = sb("g2_row", [P, D])
        ident = sb("ident_o", [P, P])
        yh, yl = [sb(f"y_{n}", [P, 2, DT, P], F32R) for n in ("hi", "lo")]
        x = sb("x_o", [P, 2, D])
        t1, x1, h, sq = sb("t_o", [P, D]), sb("x1_o", [P, 2, D]), sb("h2_o", [P, 2, D]), sb("sq_o", [P, D])
        ms, rt, rs = sb("ms_o", [P, 2]), sb("rt_o", [P, 2]), sb("rs_o", [P, 2])
        hT = sb("hT_o", [P, 2, DT, P])
        op = ps("o_ps", [P, 2, 2, BANK])
        tp = ps("h_tp", [P, 2, BANK])
        rp = ps("r_ps", [P, BANK])
        row_in, row_done, yhd, yld = sem("op_row"), sem("op_rowd"), sem("op_yh"), sem("op_yl")
        in_ = [sem("op_in0"), sem("op_in1")]
        x1_out = [sem("op_x10"), sem("op_x11")]
        h_out = [sem("op_h0"), sem("op_h1")]
        mm, gated, x1d, ssd_, msd, rtd, rsd, nd, h2d, tpd, hTd, rmm, lgd = [
            sem(f"op_{n}") for n in ("mm", "gated", "x1", "ss", "ms", "rt", "rs", "n", "h", "tp", "hT", "rmm",
                                     "lg")]
        block = ctx.enter_context(nc.Block())

        def tiles(eng, body, peel=False):
            for n in range(2):
                body(n, n, 0, True)
            with eng.Fori(1, NTX // 2 - peel) as i:
                for n in range(2):
                    body(i * 2 + n, n, i, False)
            if peel:
                for n in range(2):
                    body(NTX - 2 + n, n, NTX // 2 - 1, False, True)

        @block.gpsimd
        def _(g):
            row = lambda a: a.rearrange("(o n) -> o n", o=1)
            for dst, src in ((ga, d.mod[0, 2 * D:3 * D]), (sh, d.mod[0, 3 * D:4 * D]), (gs, d.mod[0, 4 * D:5 * D]),
                             (g2, d.g_norm2)):
                g.dma_start(dst[:], row(src).broadcast_to([P, D])).then_inc(row_in, 16)
            g.dma_start(br[:, 0:MG], row(d.b_group).broadcast_to([P, MG])).then_inc(row_in, 16)
            g.dma_start(br[:, MG:NR], row(d.b_expert).broadcast_to([P, NE])).then_inc(row_in, 16)
            g.dma_start(ident[:], d.ident).then_inc(row_in, 16)
            g.dma_start(wr[:, :, 0:MG], d.w_group.rearrange("(j p) n -> p j n", p=P)).then_inc(row_in, 16)
            g.dma_start(wr[:, :, MG:NR], d.w_expert.rearrange("(j p) n -> p j n", p=P)).then_inc(row_in, 16)

        @block.sync
        def _(sp):
            def load(t, n, h_, first):
                if not first:
                    sp.wait_ge(x1d, t - 1)
                at = bass.ds(t * P, P)
                sp.dma_start(x[:, n], d.x[at, :]).then_inc(in_[n], 16)

            def store(t, n):
                at = bass.ds(t * P, P)
                sp.wait_ge(x1d, t + 1)
                sp.dma_start(d.x1[at, :], x1[:, n]).then_inc(x1_out[n], 16)
                sp.wait_ge(h2d, t + 1)
                sp.dma_start(d.h2[at, :], h[:, n]).then_inc(h_out[n], 16)

            load(0, 0, 0, True)
            load(1, 1, 0, True)
            with sp.Fori(1, NTX // 2) as i:
                for n in range(2):
                    load(i * 2 + n, n, i, False)
                    store(i * 2 + (n - 2), n)
            for n in range(2):
                store(NTX - 2 + n, n)
            for n in range(2):
                sp.wait_ge(x1_out[n], 16 * (NTX // 2))
                sp.wait_ge(h_out[n], 16 * (NTX // 2))

        @block.tensor
        def _(pe):
            pe.wait_ge(row_in, 16 * 9)

            def project(t, n, h_, first):
                pe.wait_ge(yld, t * 2 + 2)
                if not first:
                    pe.wait_ge(gated, t - 1)
                for c in range(2):
                    at = slice(c * BANK, (c + 1) * BANK)
                    for j in range(DT):
                        pe.matmul(op[:, n, c], yh[:, n, j], woh[:, j, at], start=(j == 0), stop=False)
                        pe.matmul(op[:, n, c], yh[:, n, j], wol[:, j, at], start=False, stop=False)
                        last = pe.matmul(op[:, n, c], yl[:, n, j], woh[:, j, at], start=False, stop=(j == DT - 1))
                last.then_inc(mm, 1)

            def route(t, n, first):
                pe.wait_ge(h2d, t + 1)
                if not first:
                    pe.wait_ge(hTd, t)
                pe.wait_ge(row_in, 16 * 9)
                for j in range(DT):
                    last = pe.transpose(tp[:, j // 4, (j % 4) * P:(j % 4 + 1) * P], h[:, n, j * P:(j + 1) * P], ident[:])
                last.then_inc(tpd, 1)
                pe.wait_ge(hTd, t + 1)
                if not first:
                    pe.wait_ge(lgd, t)
                for j in range(DT):
                    last = pe.matmul(rp[:, 0:NR], hT[:, n, j], wr[:, j], start=(j == 0), stop=(j == DT - 1))
                last.then_inc(rmm, 1)

            project(0, 0, 0, True)
            project(1, 1, 0, True)
            route(0, 0, True)
            with pe.Fori(1, NTX // 2) as i:
                for n in range(2):
                    project(i * 2 + n, n, i, False)
                    route(i * 2 + (n - 1), 1 - n, False)
            route(NTX - 1, 1, False)

        @block.scalar
        def _(s):
            def lead(t, n):
                for k, a in enumerate((z, y)):
                    s.activation(yh[:, n, k * CT:(k + 1) * CT], a[:, :, bass.ds(t * P, P)], ACT.Copy).then_inc(yhd, 1)

            def step(t, n, h_, first, last=False):
                if not last:
                    s.wait_ge(mm, t + 1)
                    lead(t + 2, n)
                s.wait_ge(x1d, t + 1)
                if not first or n:
                    s.wait_ge(ssd_, t)
                s.activation(sq[:], x1[:, n], ACT.Square, accum_out=ms[:, n:n + 1]).then_inc(ssd_, 1)
                s.wait_ge(msd, t + 1)
                s.activation(rt[:, n:n + 1], ms[:, n:n + 1], ACT.Sqrt).then_inc(rtd, 1)
                s.wait_ge(tpd, t + 1)
                s.activation(hT[:, n].rearrange("p j t -> p (j t)"), tp[:].rearrange("p a b -> p (a b)"), ACT.Copy)\
                    .then_inc(hTd, 1)

            lead(0, 0)
            lead(1, 1)
            tiles(s, step, True)

        @block.vector
        def _(v):
            v.wait_ge(row_in, 16 * 9)
            v.scalar_tensor_tensor(out=gs[:], in0=gs[:], scalar=1.0, in1=g2[:], op0=ALU.add, op1=ALU.mult)\
                .then_inc(row_done, 1)

            def trail(t, n):
                for k, a in enumerate((z, y)):
                    v.wait_ge(yhd, t * 2 + (k + 1))
                    at = slice(k * CT, (k + 1) * CT)
                    v.tensor_tensor(yl[:, n, at], a[:, :, bass.ds(t * P, P)], yh[:, n, at].bitcast(F32), ALU.subtract)\
                        .then_inc(yld, 1)

            def step(t, n, h_, first, last=False):
                v.wait_ge(mm, t + 1)
                if not first or n:
                    v.wait_ge(x1d, t)
                v.tensor_tensor(t1[:], op[:, n].rearrange("p a b -> p (a b)"), ga[:], ALU.mult).then_inc(gated, 1)
                v.wait_ge(gated, t + 1)
                v.wait_ge(in_[n], h_ * 16 + 16)
                if not first:
                    v.wait_ge(x1_out[n], h_ * 16)
                    v.wait_ge(nd, t - 1)
                    v.wait_ge(ssd_, t - 1)
                v.tensor_tensor(x1[:, n], t1[:], x[:, n], ALU.add).then_inc(x1d, 1)
                if not last:
                    trail(t + 2, n)
                v.wait_ge(ssd_, t + 1)
                v.tensor_scalar(ms[:, n:n + 1], ms[:, n:n + 1], 1.0 / D, EPS, ALU.mult, ALU.add).then_inc(msd, 1)
                v.wait_ge(rtd, t + 1)
                v.reciprocal(rs[:, n:n + 1], rt[:, n:n + 1]).then_inc(rsd, 1)
                v.wait_ge(rsd, t + 1)
                v.wait_ge(row_done, 1)
                if not first:
                    v.wait_ge(h_out[n], h_ * 16)
                    v.wait_ge(tpd, t - 1)
                v.scalar_tensor_tensor(out=h[:, n], in0=x1[:, n], scalar=rs[:, n:n + 1], in1=gs[:], op0=ALU.mult,
                                       op1=ALU.mult).then_inc(nd, 1)
                v.wait_ge(nd, t + 1)
                v.tensor_tensor(h[:, n], h[:, n], sh[:], ALU.add).then_inc(h2d, 1)
                v.wait_ge(rmm, t + 1)
                v.tensor_tensor(logits[:, bass.ds(t, 1), :].rearrange("p a e -> p (a e)"), rp[:, 0:NR], br[:], ALU.add)\
                    .then_inc(lgd, 1)

            trail(0, 0)
            trail(1, 1)
            tiles(v, step, True)
            v.wait_ge(lgd, NTX)


def dispatch(nc, d, logits, gates, slots, blocks):
    T = NTX
    with ExitStack() as ctx:
        sb, ps, sem = pools(nc, ctx)
        tri = sb("tri_d", [P, 5, P])
        iot, ident = sb("iota_d", [P, NE]), sb("ident_d", [P, P])
        jcol = sb("j_d", [P, 1])
        mul = sb("mult_d", [P, MAXB])
        desc = sb("desc_d", [P, EPG])
        tok = sb("tok_d", [P, T], I32)
        zero = sb("zero_d", [P, NBLK], I32)
        s1 = [sb(f"s1_{n}", [P, T, 1]) for n in range(8)]
        m1, den, pg, mv, a1, a2, w1, w2 = s1
        gd, oh, ing, o1, o2, u8 = [sb(f"s8_{n}", [P, T, EPG]) for n in range(6)]
        big = sb("big_d", [P, T, MG, EPG])
        E1, E2, Es = [sb(f"E_{n}", [P, T, NE]) for n in range(3)]
        run = sb("run_d", [P, T + 1, NE])
        cnt, nov, incl, excl, one, cmp = [sb(f"c_{n}", [P, NE]) for n in range(6)]
        cb = sb("cmp_d", [P, NE, MAXB])
        r_, o_, q_, f_ = [sb(f"k_{n}", [P, 2, T]) for n in range(4)]
        cq = sb("cmpq_d", [P, T, MAXB])
        idx = sb("idx_d", [P, 2, T], I32)
        ec = sb("ec_d", [P, 1])
        rank = ps("rank_ps", [P, T, NE])
        cps = ps("cnt_ps", [P, BANK])
        bps = ps("blk_ps", [1, P])
        small_in, z_out, sc_out, tbl_in, tokd = sem("di_in"), sem("di_z"), sem("di_sc"), sem("di_tbl"), sem("di_tok")
        step, gexp, dexp, eready, rmm, idxd, zd, b_in = [sem(f"di_{n}") for n in
                                                         ("step", "gexp", "dexp", "E", "rmm", "idx", "zero", "bin")]
        subd, ecd, bmm = sem("di_sub"), sem("di_ec"), sem("di_bmm")
        block = ctx.enter_context(nc.Block())

        @block.sync
        def _(sp):
            sp.dma_start(tri[:], d.tri).then_inc(small_in, 16)
            for dst, src in ((iot, d.iota), (mul, d.mult), (desc, d.desc)):
                sp.dma_start(dst[:], src.rearrange("(o n) -> o n", o=1).broadcast_to([P, src.shape[0]]))\
                    .then_inc(small_in, 16)
            sp.dma_start(ident[:], d.ident).then_inc(b_in, 16)

        @block.gpsimd
        def _(g):
            g.memset(zero[:], 0).then_inc(zd, 1)
            g.iota(tok[:], pattern=[[P, T]], base=0, channel_multiplier=1).then_inc(tokd, 1)
            g.wait_ge(zd, 1)
            g.dma_start(d.i_slot.rearrange("(p b) o -> p (b o)", p=P), zero[:]).then_inc(z_out, 16)
            g.wait_ge(z_out, 16)
            g.wait_ge(tokd, 1)
            for k in range(2):
                g.wait_ge(idxd, k + 1)
                for t in range(T):
                    g.indirect_dma_start(out=d.i_slot, out_offset=bass.IndirectOffsetOnAxis(ap=idx[:, k, t:t + 1], axis=0),
                                         in_=tok[:, t:t + 1], in_offset=None).then_inc(sc_out, 16)
            g.wait_ge(sc_out, 16 * 2 * T)
            g.dma_start(slots[:, 2, 0:NBLK], d.i_slot.rearrange("(p b) o -> p (b o)", p=P)).then_inc(tbl_in, 16)
            g.wait_ge(tbl_in, 16)

        @block.scalar
        def _(s):
            s.wait_ge(subd, 1)
            s.activation(gd[:], gd[:], ACT.Exp).then_inc(gexp, 1)
            s.wait_ge(subd, 2)
            s.activation(a2[:], a1[:], ACT.Exp).then_inc(dexp, 1)

        @block.tensor
        def _(pe):
            pe.wait_ge(eready, 1)
            pe.wait_ge(small_in, 64)
            HT = T // 2
            for q in range(2):
                at = slice(q * HT, (q + 1) * HT)
                pe.matmul(rank[:, at], tri[:, 3], Es[:, at], start=True, stop=False)
                pe.matmul(rank[:, at], tri[:, 4], run[:, at], start=False, stop=True)
            pe.matmul(cps[:, 0:NE], tri[:, 4], run[:, T], start=True, stop=True).then_inc(rmm, 1)
            pe.wait_ge(b_in, 16)
            pe.wait_ge(ecd, 1)
            pe.matmul(bps[:], ec[:], ident[:], start=True, stop=True).then_inc(bmm, 1)

        @block.vector
        def _(v):
            st = Steps(v, step)
            link = st.link
            v.wait_ge(small_in, 64)
            gl = logits[:, :, 0:MG]
            el = logits[:, :, MG:MG + NE].rearrange("p t (g e) -> p t g e", g=MG)
            wide = lambda a, n: a[:].broadcast_to([P, T, n])
            dsc = desc[:].unsqueeze(1).broadcast_to([P, T, EPG])

            def first_of(out, val, m):
                link(v.tensor_tensor(out[:], val, wide(m, EPG), ALU.is_equal))
                link(v.tensor_tensor(out[:], out[:], dsc, ALU.mult))
                link(v.tensor_reduce(mv[:], out[:], AX.X, ALU.max))
                link(v.tensor_tensor(out[:], out[:], wide(mv, EPG), ALU.is_equal))

            link(v.tensor_reduce(m1[:], gl, AX.X, ALU.max))
            v.tensor_tensor(gd[:], gl, wide(m1, MG), ALU.subtract).then_inc(subd, 1)
            first_of(oh, gl, m1)
            link(v.tensor_tensor(big[:], el, oh[:].unsqueeze(3).broadcast_to([P, T, MG, EPG]), ALU.mult))
            link(v.tensor_reduce(ing[:], big[:].rearrange("p t g e -> p t e g"), AX.X, ALU.add))
            link(v.tensor_reduce(m1[:], ing[:], AX.X, ALU.max))
            first_of(o1, ing[:], m1)
            link(v.scalar_tensor_tensor(out=u8[:], in0=o1[:], scalar=-1e30, in1=ing[:], op0=ALU.mult, op1=ALU.add))
            link(v.tensor_reduce(a1[:], u8[:], AX.X, ALU.max))
            first_of(o2, u8[:], a1)
            link(v.tensor_tensor(a1[:], a1[:], m1[:], ALU.subtract))
            v.tensor_scalar(a1[:], a1[:], 0.0, None, ALU.add).then_inc(subd, 1)
            v.wait_ge(gexp, 1)
            link(v.tensor_reduce(den[:], gd[:], AX.X, ALU.add))
            link(v.reciprocal(pg[:], den[:]))
            v.wait_ge(dexp, 1)
            link(v.tensor_scalar(w1[:], a2[:], 1.0, None, ALU.add))
            link(v.reciprocal(w1[:], w1[:]))
            link(v.tensor_tensor(w2[:], w1[:], a2[:], ALU.mult))
            for k, w in enumerate((w1, w2)):
                link(v.tensor_tensor(gates[:, k], w[:].rearrange("p t o -> p (t o)"), pg[:].rearrange("p t o -> p (t o)"),
                                     ALU.mult))
            for E, o in ((E1, o1), (E2, o2)):
                link(v.tensor_tensor(E[:].rearrange("p t (g e) -> p t g e", g=MG),
                                     oh[:].unsqueeze(3).broadcast_to([P, T, MG, EPG]),
                                     o[:].unsqueeze(2).broadcast_to([P, T, MG, EPG]), ALU.mult))
            link(v.tensor_tensor(Es[:], E1[:], E2[:], ALU.add))
            link(v.memset(run[:, 0], 0.0))
            for t in range(T):
                link(v.tensor_tensor(run[:, t + 1], run[:, t], Es[:, t], ALU.add))
            v.memset(one[:], 1.0).then_inc(eready, 1)
            v.wait_ge(eready, 1)
            v.wait_ge(rmm, 1)
            link(v.tensor_copy(cnt[:], cps[:, 0:NE]))
            link(v.tensor_tensor(cb[:], cnt[:].unsqueeze(2).broadcast_to([P, NE, MAXB]),
                                 mul[:].unsqueeze(1).broadcast_to([P, NE, MAXB]), ALU.is_gt))
            link(v.tensor_reduce(nov[:], cb[:], AX.X, ALU.add))
            link(v.tensor_tensor_scan(incl[:], one[:], nov[:], 0.0, ALU.mult, ALU.add))
            link(v.tensor_tensor(excl[:], incl[:], nov[:], ALU.subtract))
            link(v.tensor_tensor(excl[:], excl[:], iot[:], ALU.add))
            link(v.scalar_tensor_tensor(out=incl[:], in0=incl[:], scalar=1.0, in1=iot[:], op0=ALU.add, op1=ALU.add))
            v.wait_ge(tokd, 1)
            link(v.tensor_copy(jcol[:], tok[:, 0:1]))
            link(v.tensor_tensor(cmp[:], incl[:], jcol[:].broadcast_to([P, NE]), ALU.is_le))
            link(v.tensor_reduce(ec[:], cmp[:], AX.X, ALU.add))
            v.tensor_scalar(ec[:], ec[:], float(NE - 1), None, ALU.min).then_inc(ecd, 1)
            row = lambda a: a[:].unsqueeze(1).broadcast_to([P, T, NE])
            bigf = big[:].rearrange("p t g e -> p t (g e)")
            for k, E in enumerate((E1, E2)):
                for dst, src in ((r_, rank[:]), (o_, row(excl))):
                    link(v.tensor_tensor(bigf, E[:], src, ALU.mult))
                    link(v.tensor_reduce(dst[:, k], bigf, AX.X, ALU.add))
                link(v.tensor_tensor(cq[:], r_[:, k].unsqueeze(2).broadcast_to([P, T, MAXB]),
                                     mul[:].unsqueeze(1).broadcast_to([P, T, MAXB]), ALU.is_ge))
                link(v.tensor_reduce(q_[:, k], cq[:], AX.X, ALU.add))
                link(v.tensor_tensor(o_[:, k], o_[:, k], q_[:, k], ALU.add))
                link(v.scalar_tensor_tensor(out=r_[:, k], in0=q_[:, k], scalar=-float(P), in1=r_[:, k], op0=ALU.mult,
                                            op1=ALU.add))
                link(v.scalar_tensor_tensor(out=f_[:, k], in0=r_[:, k], scalar=float(NBLK), in1=o_[:, k], op0=ALU.mult,
                                            op1=ALU.add))
                v.tensor_copy(idx[:, k], f_[:, k]).then_inc(idxd, 1)
            link(v.scalar_tensor_tensor(out=q_[:], in0=o_[:], scalar=float(P), in1=r_[:], op0=ALU.mult, op1=ALU.add))
            v.tensor_copy(slots[:, 0:2, 0:T], q_[:]).then_inc(idxd, 1)
            v.wait_ge(bmm, 1)
            link(v.tensor_copy(blocks[0:1, 0:NBLK + 1], bps[:, 0:NBLK + 1]))
            link(v.tensor_copy(blocks[0:1, NBLK + 1:NBLK + 2], incl[0:1, NE - 1:NE]))


def experts(nc, d, slots, blocks):
    FT = DE // P
    UNITS = 6
    PLACES = 3
    UW = DT * DE // 2
    with ExitStack() as ctx:
        sb, ps, sem = pools(nc, ctx)
        ident, ga = sb("ident_e", [P, P]), sb("gate2_row", [P, D])
        (w, wl), wh = split_pair(nc, ctx, "w_e", [P, PLACES, 3, UW]), sb("w_hi", [P, PLACES, 3, UW], F32R)
        idx = sb("idx_e", [P, 2], I32)
        xb = sb("xb", [P, 2, D])
        xh, xl = [sb(f"xT_{n}", [P, 2, DT, P], F32R) for n in ("hi", "lo")]
        s1, g = sb("s1_e", [P, 2, DE]), sb("g_e", [P, 2, DE])
        gh, gl = [sb(f"gT_{n}", [P, 2, FT, P], F32R) for n in ("hi", "lo")]
        yo = sb("y_e", [P, 2, D])
        tp = ps("tp_e", [P, 2, BANK])
        h1, h3 = ps("h1_e", [P, DE]), ps("h3_e", [P, DE])
        yp = ps("yp_e", [P, 2, BANK])
        gp = [ps(f"gp{k}_e", [P, 2, P]) for k in range(2)]
        ident_in, named, stored, arrived = sem("ex_id"), sem("ex_named"), sem("ex_stored"), sem("ex_arrived")
        w_in = [sem(f"ex_w{u}") for u in range(UNITS)]
        x_in, y_out = [[sem(f"ex_{n}{k}") for k in range(2)] for n in ("x", "yo")]
        idxd, tpd, xhd, xld, m1, m3, sd, gd, gtp, ghd, gld, ym, yd, whd, wld, w5d = [
            sem(f"ex_{n}") for n in ("idx", "tp", "xh", "xl", "m1", "m3", "s", "g", "gtp", "gh", "gl", "ym", "yd",
                                     "wh", "wl", "last")]
        block = ctx.enter_context(nc.Block())

        def used(eng):
            return eng.value_load(blocks[0:1, NBLK + 1:NBLK + 2], min_val=NE, max_val=NBLK)

        def run(eng, body):
            total = used(eng)
            for n in range(2):
                body(n, n, 0, True, total)
            with eng.Fori(1, NBLK // 2) as i:
                for n in range(2):
                    q = i * 2 + n
                    with eng.If(q < total):
                        body(q, n, i, False, total)

        def expert(eng, q, behind=0):
            return eng.value_load(blocks[0:1, bass.ds(q, 1)], min_val=0, max_val=NE - 1 - behind)

        def place(eng, e, u):
            group = e * 2 + u // 3
            if isinstance(e, int):
                return group % PLACES
            return eng.snap(group % PLACES)

        def unit(t, at, u):
            return t[:, bass.ds(at, 1), u % 3].rearrange("p a f -> p (a f)")

        def ahead(eng, q, first, total, body):
            if first:
                body()
            else:
                with eng.If(q + 1 < total):
                    body()

        @block.gpsimd
        def _(g_):
            def gather(q, n):
                g_.tensor_copy(idx[:, n:n + 1], slots[:, 2, bass.ds(q, 1)]).then_inc(idxd, 1)
                g_.wait_ge(idxd, q + 1)
                g_.sem_inc(named, 1)
                g_.indirect_dma_start(out=xb[:, n], out_offset=None, in_=d.h2,
                                      in_offset=bass.IndirectOffsetOnAxis(ap=idx[:, n:n + 1], axis=0))\
                    .then_inc(x_in[n], 16)

            def split(e):
                at = place(g_, e, 5)
                g_.wait_ge(whd, e * UNITS + 6)
                g_.sem_inc(named, 1)
                g_.tensor_tensor(unit(wl, at, 5), unit(w, at, 5), unit(wh, at, 5).bitcast(F32), ALU.subtract)\
                    .then_inc(w5d, 1)

            def step(q, n, h, first, total):
                e, behind = expert(g_, q), expert(g_, q + 1)
                g_.wait_ge(x_in[n], h * 16 + 16)
                g_.wait_ge(tpd, q + 1)
                if first:
                    gather(q + 2, n)
                else:
                    with g_.If(q + 2 < total):
                        gather(q + 2, n)
                with g_.If(behind > e):
                    split(behind)

            for k in range(2):
                gather(k, k)
            split(0)
            run(g_, step)

        @block.sync
        def _(sp):
            sp.dma_start(ident[:], d.ident).then_inc(ident_in, 16)
            sp.dma_start(ga[:], d.mod[0, 5 * D:6 * D].rearrange("(o n) -> o n", o=1).broadcast_to([P, D]))\
                .then_inc(ident_in, 16)

            def load(e, by, u):
                v = (d.w1, d.w3, d.w2)[u // 2][by:NE][bass.ds(e, 1)].rearrange("a (p j) f -> (a p) (j f)", p=P)
                sp.dma_start(unit(w, place(sp, e + by, u), u), v[:, u % 2 * UW:(u % 2 + 1) * UW]).then_inc(w_in[u], 16)

            def reload(q, e, u):
                new, by = ((u + 3, 1), (u - 3, 2))[u // 3]
                sp.wait_ge((m1, m3, ym)[u // 2], q * 2 + (u % 2 + 1))
                sp.wait_ge(w_in[new], (e + by) * 16)
                load(e, by, new)

            def step(q, n, h, first, total):
                e, behind = expert(sp, q), expert(sp, q + 1)
                with sp.If(behind > e):
                    one = expert(sp, q, 1)
                    for u in range(3):
                        reload(q, one, u)
                    with sp.If(e < NE - 2):
                        two = expert(sp, q, 2)
                        for u in range(3, UNITS):
                            reload(q, two, u)

            for u in range(UNITS):
                load(0, 0, u)
            for u in range(3):
                sp.wait_ge(w_in[u], 16)
                load(0, 1, u)
            run(sp, step)

        @block.tensor
        def _(pe):
            pe.wait_ge(ident_in, 32)

            def products(acc, hi, lo, g_, u, j, width, at, start, stop):
                a, b = [unit(t, g_, u).rearrange("p (j f) -> p j f", f=width)[:, j, at:at + BANK] for t in (wh, wl)]
                pe.matmul(acc, hi, a, start=start, stop=False)
                pe.matmul(acc, hi, b, start=False, stop=False)
                return pe.matmul(acc, lo, a, start=False, stop=stop)

            def turn(q, n, h, some):
                pe.wait_ge(x_in[n], h * 16 + 16)
                if some:
                    pe.wait_ge(xld, q)
                pe.wait_ge(ident_in, 32)
                xv = xb[:, n].rearrange("p (a j) -> p j a", j=DT)
                for j in range(DT):
                    last = pe.transpose(tp[:, j // 4, (j % 4) * P:(j % 4 + 1) * P], xv[:, j], ident[:])
                last.then_inc(tpd, 1)

            def body(q, n, h, first, total):
                e = expert(pe, q)
                at = [place(pe, e, 3 * k) for k in range(2)]
                pe.wait_ge(xld, q + 1)
                for acc, u0, free, done in ((h1, 0, sd, m1), (h3, 2, gd, m3)):
                    if not first or n:
                        pe.wait_ge(free, q)
                    for j in range(DT):
                        if j % 4 == 0:
                            pe.wait_ge(wld, e * (UNITS - 1) + (u0 + j // 4 + 1))
                        u = u0 + j // 4
                        last = products(acc[:], xh[:, n, j], xl[:, n, j], at[u // 3], u, j % 4, DE, 0, j == 0,
                                        j == DT - 1)
                        if j % 4 == 3:
                            last.then_inc(done, 1)
                ahead(pe, q, first, total, lambda: turn(q + 1, 1 - n, h + n, True))
                pe.wait_ge(gd, q + 1)
                if not first or n:
                    pe.wait_ge(gld, q * 2)
                pe.wait_ge(ident_in, 32)
                gv = g[:, n].rearrange("p (a j) -> p j a", j=FT)
                for j in range(FT):
                    last = pe.transpose(gp[j // 2][:, j % 2], gv[:, j], ident[:])
                    if j % 2:
                        last.then_inc(gtp, 1)
                if not first or n:
                    pe.wait_ge(yd, q)
                for j in range(FT):
                    if j % 2 == 0:
                        pe.wait_ge(gld, q * 2 + (j // 2 + 1))
                        if j:
                            pe.wait_ge(w5d, e + 1)
                        else:
                            pe.wait_ge(wld, e * (UNITS - 1) + 5)
                    for c in range(2):
                        last = products(yp[:, c], gh[:, n, j], gl[:, n, j], at[1], 4 + j // 2, j % 2, D, c * BANK, j == 0,
                                        j == FT - 1)
                    if j % 2:
                        last.then_inc(ym, 1)

            turn(0, 0, 0, False)
            run(pe, body)

        @block.scalar
        def _(s):
            def split(e, units):
                for u in units:
                    at = place(s, e, u)
                    s.wait_ge(w_in[u], e * 16 + 16)
                    s.sem_inc(arrived, 1)
                    s.activation(unit(wh, at, u), unit(w, at, u), ACT.Copy).then_inc(whd, 1)

            def turned(q, n, some):
                if some:
                    s.wait_ge(m3, q * 2 - 2)
                s.wait_ge(tpd, q + 1)
                s.activation(xh[:, n].rearrange("p j t -> p (j t)"), tp[:].rearrange("p a b -> p (a b)"), ACT.Copy)\
                    .then_inc(xhd, 1)

            def step(q, n, h, first, total):
                e, behind = expert(s, q), expert(s, q + 1)
                with s.If(behind > e):
                    split(behind, (0,))
                s.wait_ge(m1, q * 2 + 2)
                if not first:
                    s.wait_ge(gd, q - 1)
                s.activation(s1[:, n], h1[:], ACT.Silu).then_inc(sd, 1)
                with s.If(behind > e):
                    split(behind, (1,))
                for k in range(2):
                    s.wait_ge(gtp, q * 2 + (k + 1))
                    if not first:
                        s.wait_ge(ym, q * 2 - 2)
                    s.activation(gh[:, n, 2 * k:2 * k + 2], gp[k][:], ACT.Copy).then_inc(ghd, 1)
                ahead(s, q, first, total, lambda: turned(q + 1, 1 - n, not first or n == 1))
                with s.If(behind > e):
                    split(behind, (2, 3, 4, 5))
                s.wait_ge(yd, q + 1)
                s.dma_start(d.yb[bass.ds(q * P, P), :], yo[:, n]).then_inc(y_out[n], 16)

            split(0, (0,))
            turned(0, 0, False)
            split(0, (1, 2, 3, 4, 5))
            run(s, step)
            total = used(s)
            for n in range(2):
                s.wait_ge(y_out[n], ((total + (1 - n)) >> 1) * 16)
                s.sem_inc(stored, 1)

        @block.vector
        def _(v):
            def split(e, units):
                for u in units:
                    at = place(v, e, u)
                    v.wait_ge(whd, e * UNITS + (u + 1))
                    v.tensor_tensor(unit(wl, at, u), unit(w, at, u), unit(wh, at, u).bitcast(F32), ALU.subtract)\
                        .then_inc(wld, 1)

            def turned(q, n, some):
                if some:
                    v.wait_ge(m3, q * 2 - 2)
                v.wait_ge(xhd, q + 1)
                v.tensor_tensor(xl[:, n].rearrange("p j t -> p (j t)"), tp[:].rearrange("p a b -> p (a b)"),
                                xh[:, n].rearrange("p j t -> p (j t)").bitcast(F32), ALU.subtract).then_inc(xld, 1)

            def step(q, n, h, first, total):
                e, behind = expert(v, q), expert(v, q + 1)
                with v.If(behind > e):
                    split(behind, (0,))
                v.wait_ge(m3, q * 2 + 2)
                v.wait_ge(sd, q + 1)
                if not first:
                    v.wait_ge(gtp, q * 2 - 2)
                v.tensor_tensor(g[:, n], s1[:, n], h3[:], ALU.mult).then_inc(gd, 1)
                for k in range(2):
                    v.wait_ge(ghd, q * 2 + (k + 1))
                    if not first:
                        v.wait_ge(ym, q * 2 - 2)
                    at = slice(2 * k, 2 * k + 2)
                    v.tensor_tensor(gl[:, n, at], gp[k][:], gh[:, n, at].bitcast(F32), ALU.subtract).then_inc(gld, 1)
                ahead(v, q, first, total, lambda: turned(q + 1, 1 - n, not first or n == 1))
                with v.If(behind > e):
                    split(behind, (1, 2, 3, 4))
                v.wait_ge(ym, q * 2 + 2)
                if not first:
                    v.wait_ge(y_out[n], h * 16)
                v.tensor_tensor(yo[:, n], yp[:].rearrange("p a b -> p (a b)"), ga[:], ALU.mult).then_inc(yd, 1)

            v.wait_ge(ident_in, 32)
            split(0, (0,))
            turned(0, 0, False)
            split(0, (1, 2, 3, 4))
            run(v, step)


def combine(nc, d, gates, slots):
    NBUF = 4
    with ExitStack() as ctx:
        sb, _, sem = pools(nc, ctx)
        idx = sb("idx_c", [P, NBUF, 2], I32)
        yr = sb("yr_c", [P, NBUF, 2, D])
        x1, o = sb("x1_c", [P, NBUF, D]), sb("out_c", [P, 2, D])
        gf = sb("gf_row", [P, D])
        t = sb("t_c", [P, 2, D])
        sq = sb("sq_c", [P, D])
        ms, rt, rs = sb("ms_c", [P, 2]), sb("rt_c", [P, 2]), sb("rs_c", [P, 2])
        row_in, named = sem("cb_row"), sem("cb_named")
        x_in, y_in = [[sem(f"cb_{n}{k}") for k in range(NBUF)] for n in ("x", "y")]
        out_done = [sem(f"cb_o{k}") for k in range(2)]
        idxd, a, xd, ssd_, msd, rtd, rsd, od = [sem(f"cb_{n}") for n in
                                                ("idx", "a", "xd", "ss", "ms", "rt", "rs", "od")]
        block = ctx.enter_context(nc.Block())

        def tiles(eng, body):
            for k in range(NBUF):
                body(k, k, 0)
            with eng.Fori(1, NTX // NBUF) as i:
                for b in range(NBUF):
                    body(i * NBUF + b, b, i)

        def known(k):
            return isinstance(k, int)

        @block.gpsimd
        def _(g):
            def step(k, b, r):
                if not known(k):
                    g.wait_ge(y_in[b], r * 32)
                    g.wait_ge(xd, k + (1 - NBUF))
                g.tensor_copy(idx[:, b], slots[:, 0:2, bass.ds(k, 1)].rearrange("p a o -> p (a o)")).then_inc(idxd, 1)
                g.wait_ge(idxd, k + 1)
                g.sem_inc(named, 1)
                for c in range(2):
                    g.indirect_dma_start(out=yr[:, b, c], out_offset=None, in_=d.yb,
                                         in_offset=bass.IndirectOffsetOnAxis(ap=idx[:, b, c:c + 1], axis=0))\
                        .then_inc(y_in[b], 16)

            tiles(g, step)

        @block.sync
        def _(sp):
            sp.dma_start(gf[:], d.g_final.rearrange("(o n) -> o n", o=1).broadcast_to([P, D])).then_inc(row_in, 16)

            def load(k, b, r):
                if not known(k):
                    sp.wait_ge(od, k + (1 - NBUF))
                sp.dma_start(x1[:, b], d.x1[bass.ds(k * P, P), :]).then_inc(x_in[b], 16)

            tiles(sp, load)

        @block.scalar
        def _(s):
            def step(k, b, r):
                s.wait_ge(xd, k + 1)
                if not known(k) or k:
                    s.wait_ge(ssd_, k)
                if not known(k) or k >= 2:
                    s.wait_ge(msd, k - 1)
                    s.wait_ge(rtd, k - 1)
                s.activation(sq[:], x1[:, b], ACT.Square, accum_out=ms[:, b % 2:b % 2 + 1]).then_inc(ssd_, 1)
                s.wait_ge(msd, k + 1)
                if not known(k) or k >= 2:
                    s.wait_ge(rsd, k - 1)
                s.activation(rt[:, b % 2:b % 2 + 1], ms[:, b % 2:b % 2 + 1], ACT.Sqrt).then_inc(rtd, 1)
                s.wait_ge(od, k + 1)
                s.dma_start(d.out[bass.ds(k * P, P), :], o[:, b % 2]).then_inc(out_done[b % 2], 16)

            tiles(s, step)
            for n in range(2):
                s.wait_ge(out_done[n], 16 * (NTX // 2))

        @block.vector
        def _(v):
            v.wait_ge(row_in, 16)

            def sums(k, b, r):
                n = b % 2
                v.wait_ge(y_in[b], r * 32 + 32)
                v.wait_ge(x_in[b], r * 16 + 16)
                if not known(k) or k >= 2:
                    v.wait_ge(xd, k - 1)
                v.scalar_tensor_tensor(out=t[:, n], in0=yr[:, b, 0], scalar=gates[:, 0, bass.ds(k, 1)], in1=x1[:, b],
                                       op0=ALU.mult, op1=ALU.add).then_inc(a, 1)
                v.wait_ge(a, k + 1)
                v.scalar_tensor_tensor(out=x1[:, b], in0=yr[:, b, 1], scalar=gates[:, 1, bass.ds(k, 1)], in1=t[:, n],
                                       op0=ALU.mult, op1=ALU.add).then_inc(xd, 1)

            def normed(k, b, r):
                n = b % 2
                v.wait_ge(ssd_, k + 1)
                v.tensor_scalar(ms[:, n:n + 1], ms[:, n:n + 1], 1.0 / D, EPS, ALU.mult, ALU.add).then_inc(msd, 1)
                v.wait_ge(rtd, k + 1)
                v.reciprocal(rs[:, n:n + 1], rt[:, n:n + 1]).then_inc(rsd, 1)
                v.wait_ge(rsd, k + 1)
                if not known(k) or k >= 2:
                    v.wait_ge(out_done[n], r * 32 + b // 2 * 16)
                v.scalar_tensor_tensor(out=o[:, n], in0=x1[:, b], scalar=rs[:, n:n + 1], in1=gf[:], op0=ALU.mult,
                                       op1=ALU.mult).then_inc(od, 1)

            def step(k, b, r):
                sums(k, b, r)
                if not known(k) or k:
                    normed(k - 1, (b - 1) % NBUF, r + (b - 1) // NBUF)

            tiles(v, step)
            normed(NTX - 1, NBUF - 1, NTX // NBUF - 1)


def moe(nc, d, logits):
    with ExitStack() as ctx:
        sb, _, _ = pools(nc, ctx)
        gates = sb("gates", [P, 2, NTX])
        slots = sb("slots", [P, 3, NBLK + 2], I32)
        blocks = sb("blocks", [1, NBLK + 2], I32)
        dispatch(nc, d, logits, gates, slots, blocks)
        experts(nc, d, slots, blocks)
        combine(nc, d, gates, slots)


def constants():
    c = {}
    c["ident"] = np.eye(P, dtype=np.float32)
    fwd = np.arange(L)
    bwd = np.where(fwd == 0, 0, L - fwd)
    bands = np.linspace(1e-4, BANDS - 1, BANDS, dtype=np.float32)
    feats = []
    for pos in (fwd, bwd):
        ang = (np.float32(2 * math.pi / L) * pos[:, None].astype(np.float32)) * bands[None, :]
        t = (pos.astype(np.float32) / np.float32(L - 1))[:, None]
        feats.append(np.concatenate([t, np.cos(ang), -np.sin(ang)], axis=1).T)
    c["feats"] = np.concatenate(feats).astype(np.float32)
    pos = np.concatenate([fwd, bwd]).astype(np.float32) / np.float32(L - 1)
    c["t_col"] = np.ascontiguousarray(-pos.reshape(P, N2)).astype(np.float32)
    c["delta"] = np.abs(np.linspace(math.log(TARGET) / SLOW, math.log(TARGET) / FAST, DH, dtype=np.float32))
    N = 2 * L
    n1, n2 = np.arange(P), np.arange(N2)
    k1 = np.arange(1, NB1)
    ph = 2 * np.pi * ((N2 * n1[None, :, None] + n2[:, None, None]) * k1 % N) / N
    f1 = np.zeros((N2, P, P))
    f1[:, :, 0] = 1
    f1[:, :, 1] = (-1.0) ** n1
    f1[:, :, 2::2] = np.cos(ph)
    f1[:, :, 3::2] = -np.sin(ph)
    c["f1"] = f1.astype(np.float32)
    g1 = np.zeros((P, N2, NB1))
    half = ph[:, :NB1]
    g1[0] = 1
    g1[1] = (-1.0) ** n1[:NB1]
    g1[2::2] = 2 * np.cos(half).transpose(2, 0, 1)
    g1[3::2] = -2 * np.sin(half).transpose(2, 0, 1)
    c["g1"] = (g1 / N).astype(np.float32)
    th = 2 * np.pi * np.outer(n2, n2) / N2
    co, si = np.cos(th), np.sin(th)
    tw = 2 * np.pi * n2 / 64
    rr, ir, ri, ii = co, si, -si, co
    one = {"A": [[rr, ri], [ir, ii]], "B": [[ri, rr], [ii, ir]],
           "kA": [[rr, rr], [ir, ir]], "kB": [[-ri, ri], [-ii, ii]]}
    c64, s64 = np.cos(th + tw[:, None]), np.sin(th + tw[:, None])
    m2 = np.zeros((15, P, P))
    H = P // 2
    for n, name in enumerate(("A", "B", "kA", "kB")):
        b = np.block(one[name])
        m2[n, :H, :H] = m2[n, H:, H:] = b
        for row, (cc, ss) in enumerate(((co, si), (c64, s64))):
            real, imag = cc, -ss
            parts = {"A": (real, imag), "B": (imag, real), "kA": (real, real), "kB": (-imag, imag)}[name]
            m2[5 + n, row * N2:(row + 1) * N2, row * H:(row + 1) * H] = np.concatenate(parts, axis=1)
        m2[10 + n, H:, :H] = b
    inv = np.block([[co, si], [-si, co]])
    m2[4, :H, :H] = m2[4, H:, H:] = inv
    m2[9, 0:N2, 0:N2], m2[9, N2:H, 0:N2] = co, -si
    ci, s_i = np.cos(th + tw[None, :]), np.sin(th + tw[None, :])
    m2[9, H:H + N2, N2:H], m2[9, H + N2:, N2:H] = ci, -s_i
    m2[14, :H, H:] = inv
    j, l = np.arange(P)[:, None], np.arange(P)[None, :]
    c["tri"] = np.stack([j <= l, j >= l, j > l, j < l, j + l >= 0], axis=1).astype(np.float32)
    c["mask"] = np.where(np.stack([l >= j, l <= j], axis=1), 0.0, -1e30).astype(np.float32)
    c["iota"] = np.arange(NE, dtype=np.float32)
    c["mult"] = (P * np.arange(1, MAXB + 1)).astype(np.float32)
    c["desc"] = np.arange(EPG, 0, -1).astype(np.float32)
    c["m2"] = np.ascontiguousarray(m2.transpose(1, 0, 2)).astype(np.float32)
    return c


SCRATCH = {
    "mod": [2, 6 * D],
    "uT": [HYT, P, L],
    "zT": [ZT, P, L],
    "sT": [XBCT, P, TOK],
    "Tk": [ORDER, P, N2, DH],
    "Tz": [P, N2, DH],
    "V": [P, N2, DH],
    "cumT": [NT * 2 * HEADS, P],
    "Hb": [NT, P, D_SSD],
    "x1": [L, D],
    "h2": [L, D],
    "i_slot": [P * NBLK, 1],
    "yb": [NBLK * P, D],
    "dt_a": [P, 2, NT, 2 * HEADS],
}


def program(nc, d):
    with ExitStack() as ctx:
        logits = ctx.enter_context(nc.sbuf_tensor("logits", [P, NTX, MG + NE], F32))
        with ExitStack() as hctx:
            tokens = ExitStack()
            x = tokens.enter_context(nc.sbuf_tensor("x_tok", [P, NT, D], F32, side="right"))
            ms = tokens.enter_context(nc.sbuf_tensor("x_ms", [P, NT], F32, side="right"))
            adaln(nc, d, x, ms)
            hT, hl = split_pair(nc, hctx, "hT", [P, DT, TOK])
            norm_in(nc, d, x, ms, hT)
            tokens.close()
            with ExitStack() as split:
                hh = split.enter_context(nc.sbuf_tensor("hT_hi", [P, DT, TOK], F32R))
                in_proj(nc, d, hT, hl, hh)
                step_sizes(nc, d, hl, hh)
        with ExitStack() as mix:
            z = mix.enter_context(nc.sbuf_tensor("z_hyena", [P, CT, L], F32))
            hyena(nc, d, z)
            y = mix.enter_context(nc.sbuf_tensor("y_ssd", [P, CT, L], F32))
            ssd(nc, d, y)
            (wo, wol), woh = split_pair(nc, mix, "w_out_sb", [P, DT, D]), mix.enter_context(
                nc.sbuf_tensor("w_out_hi", [P, DT, D], F32R))
            ssd_norm(nc, d, y, wo, wol, woh)
            out_proj(nc, d, z, y, wol, woh, logits)
        moe(nc, d, logits)


NAMES = ["x", "c", "ctx", "c_ctx", "w_ada", "b_ada", "g_norm1", "g_norm2", "w_in", "hy_conv_w", "hy_conv_b",
         "hy_f_w1", "hy_f_b1", "hy_f_freq", "hy_f_w2", "hy_f_b2", "hy_f_w3", "hy_bias", "ssd_conv_w", "ssd_conv_b",
         "ssd_a_log", "ssd_dt_bias", "ssd_d", "ssd_norm_g", "w_out", "w_group", "b_group", "w_expert", "b_expert",
         "w1", "w3", "w2", "g_final"]


def layout(name, a):
    return a if name in ("c_ctx", "g_final") else a[0]


def kernel(**inputs):
    import concourse.bacc as _bacc
    from concourse.bass_utils import run_bass_kernel_spmd as _run

    nc = _bacc.Bacc("TRN2", target_bir_lowering=False, num_devices=1)
    arrays, put = {}, {}
    host = {n: np.ascontiguousarray(layout(n, inputs[n])) for n in NAMES}
    host.update(constants())
    for name, a in host.items():
        arrays[f"in_{name}"] = a
        put[name] = nc.dram_tensor(f"in_{name}", a.shape, mybir.dt.from_np(a.dtype), kind="ExternalInput").ap()
    put["out"] = nc.dram_tensor("out_0", (L, D), F32, kind="ExternalOutput").ap()
    for name, shape in SCRATCH.items():
        put[name] = nc.dram_tensor(f"s_{name}", shape, I32 if name.startswith("i_") else F32, kind="Internal").ap()
    program(nc, namedtuple("Arrays", sorted(put))(**put))
    r = _run(nc, [arrays], core_ids=[0])
    return r.results[0]["out_0"].reshape(1, L, D)
```
